# Optimizing a Trainium2 kernel written in Bass

```python
import math
import jax, jax.numpy as jnp
from jax import lax
import numpy as np

D_MODEL = 1024
BATCH = 1
SEQ = 512
DEPTH = 1

GRID_W = 64
CTX_LEN = 256
NORM_EPS = 1e-6
N_MOD = 6

MLA_HEADS = 8
MLA_NOPE = 64
MLA_ROPE = 32
MLA_V = 64
MLA_Q_LORA = 256
MLA_KV_LORA = 128
ROPE_BASE = 10000.0
Q_BLOCK = 128

S5_WIDTH = 512
S5_GROUP = 16
S5_GROUPS = S5_WIDTH // S5_GROUP
S5_STATE = 64
S5_DT_MIN = 0.001
S5_DT_MAX = 0.1

HY_WIDTH = 512
HY_ORDER = 2
HY_BANDS = 16
HY_POS_DIM = 1 + 2 * HY_BANDS
HY_FILTER_HIDDEN = 64
HY_FILTER_OUT = HY_ORDER * 2 * HY_WIDTH
HY_DECAY_TARGET = 1e-2
HY_DECAY_SHORT = 0.3
HY_DECAY_LONG = 1.5
HY_DECAY_SHIFT = 0.05

N_BRANCH = 3
D_FF = -(-8 * D_MODEL // (3 * 256)) * 256

OFF_CQ = 0
OFF_CKV = OFF_CQ + MLA_Q_LORA
OFF_KR = OFF_CKV + MLA_KV_LORA
OFF_S5 = OFF_KR + MLA_ROPE
OFF_HY = OFF_S5 + S5_WIDTH
OFF_GATE = OFF_HY + 3 * HY_WIDTH
IN_WIDTH = OFF_GATE + N_BRANCH * D_MODEL

kernel_name = "hybrid_mla_s5_hyena_prefix_dit"

def rmsnorm(x, g):
    xf = x.astype(jnp.float32)
    y = xf * lax.rsqrt(jnp.mean(xf * xf, axis=-1, keepdims=True) + NORM_EPS)
    return (y * g.astype(jnp.float32)).astype(x.dtype)

def modulate(xn, shift, scale):
    return xn * (1.0 + scale) + shift

def axial_rope(n_tok):
    rows = n_tok // GRID_W
    row = jnp.broadcast_to(jnp.arange(rows, dtype=jnp.float32)[:, None], (rows, GRID_W)).reshape(-1)
    col = jnp.broadcast_to(jnp.arange(GRID_W, dtype=jnp.float32)[None, :], (rows, GRID_W)).reshape(-1)
    n_freq = MLA_ROPE // 4
    inv = ROPE_BASE ** (-jnp.arange(n_freq, dtype=jnp.float32) / n_freq)
    ang = jnp.concatenate([row[:, None] * inv, col[:, None] * inv], axis=-1)
    return jnp.cos(ang), jnp.sin(ang)

def apply_rope(x, cos, sin):
    shp = (cos.shape[0],) + (1,) * (x.ndim - 3) + (cos.shape[1],)
    cos = cos.reshape(shp)
    sin = sin.reshape(shp)
    xf = x.astype(jnp.float32)
    x1 = xf[..., 0::2]
    x2 = xf[..., 1::2]
    out = jnp.stack([x1 * cos - x2 * sin, x1 * sin + x2 * cos], axis=-1).reshape(x.shape)
    return out.astype(x.dtype)

def mla_queries(z, q_norm, w_uq, rope):
    b, n, _ = z.shape
    q = (rmsnorm(z[..., OFF_CQ:OFF_CKV], q_norm) @ w_uq).reshape(b, n, MLA_HEADS, MLA_NOPE + MLA_ROPE)
    if rope is not None:
        q = jnp.concatenate([q[..., :MLA_NOPE], apply_rope(q[..., MLA_NOPE:], *rope)], axis=-1)
    return q

def mla_keys_values(z, kv_norm, w_ukv, rope):
    b, n, _ = z.shape
    kv = (rmsnorm(z[..., OFF_CKV:OFF_KR], kv_norm) @ w_ukv).reshape(b, n, MLA_HEADS, MLA_NOPE + MLA_V)
    k_rope = z[..., OFF_KR:OFF_S5]
    if rope is not None:
        k_rope = apply_rope(k_rope, *rope)
    k = jnp.concatenate(
        [kv[..., :MLA_NOPE], jnp.broadcast_to(k_rope[:, :, None, :], (b, n, MLA_HEADS, MLA_ROPE))], axis=-1)
    return k, kv[..., MLA_NOPE:]

def attend(q, k, v):
    s = jnp.einsum('bqhd,bkhd->bhqk', q, k).astype(jnp.float32) * ((MLA_NOPE + MLA_ROPE) ** -0.5)
    p = jax.nn.softmax(s, axis=-1).astype(v.dtype)
    return jnp.einsum('bhqk,bkhd->bqhd', p, v)

def blocked_attend(q, k, v):
    b, n, h, dq = q.shape
    nb = n // Q_BLOCK
    qb = jnp.moveaxis(q.reshape(b, nb, Q_BLOCK, h, dq), 1, 0)
    out = lax.map(lambda qq: attend(qq, k, v), qb)
    return jnp.moveaxis(out, 0, 1).reshape(b, n, h * v.shape[-1])

def s5_discretize(lam_re, lam_im, log_dt, b_re, b_im):
    lam = lax.complex(lam_re.astype(jnp.float32), lam_im.astype(jnp.float32))
    dt = jnp.exp(log_dt.astype(jnp.float32))[:, None]
    lam_bar = jnp.exp(lam * dt)
    b_mat = lax.complex(b_re.astype(jnp.float32), b_im.astype(jnp.float32))
    b_bar = ((lam_bar - 1.0) / lam)[:, :, None] * b_mat
    return lam_bar, b_bar

def _linear_combine(left, right):
    a_l, b_l = left
    a_r, b_r = right
    return a_r * a_l, a_r * b_l + b_r

def s5_states(u, lam_bar, b_bar, h0):
    bu = jnp.einsum('gpn,blgn->blgp', b_bar, u.astype(jnp.complex64))
    bu = bu.at[:, 0].add(lam_bar * h0)
    a = jnp.broadcast_to(lam_bar, bu.shape)
    _, h = lax.associative_scan(_linear_combine, (a, bu), axis=1)
    return h

def s5_readout(h, c_re, c_im):
    c_mat = lax.complex(c_re.astype(jnp.float32), c_im.astype(jnp.float32))
    return jnp.einsum('gnp,blgp->blgn', c_mat, h).real

def s5_mixer(u, disc, c_re, c_im, d, h0, want_output):
    b, n, _ = u.shape
    uf = u.astype(jnp.float32)
    ug = uf.reshape(b, n, S5_GROUPS, S5_GROUP)
    h_f = s5_states(ug, disc[0][0], disc[0][1], h0[0])
    h_b = s5_states(ug[:, ::-1], disc[1][0], disc[1][1], h0[1])
    finals = (h_f[:, -1], h_b[:, -1])
    if not want_output:
        return None, finals
    y = s5_readout(h_f, c_re[0], c_im[0]) + s5_readout(h_b, c_re[1], c_im[1])[:, ::-1]
    y = y.reshape(b, n, S5_WIDTH) + d.astype(jnp.float32) * uf
    return y, finals

def s5_glu(y, w_glu):
    y = jax.nn.gelu(y)
    return y * jax.nn.sigmoid(y @ w_glu.astype(jnp.float32))

def hyena_filters(n_tok, w1, b1, w2, b2, w3, freq):
    f32 = jnp.float32
    t = jnp.linspace(0.0, 1.0, n_tok, dtype=f32)[:, None]
    w = 2.0 * math.pi * jnp.arange(n_tok, dtype=f32)[:, None] / n_tok
    bands = jnp.linspace(1e-4, HY_BANDS - 1, HY_BANDS, dtype=f32)[None, :]
    z = jnp.concatenate([t, jnp.cos(bands * w), -jnp.sin(bands * w)], axis=-1)
    fq = freq.astype(f32)
    hid = jnp.sin(fq * (z @ w1.astype(f32) + b1.astype(f32)))
    hid = jnp.sin(fq * (hid @ w2.astype(f32) + b2.astype(f32)))
    filt = hid @ w3.astype(f32)
    deltas = jnp.abs(jnp.linspace(math.log(HY_DECAY_TARGET) / HY_DECAY_SHORT,
                                  math.log(HY_DECAY_TARGET) / HY_DECAY_LONG, HY_FILTER_OUT, dtype=f32))
    return filt * (jnp.exp(-t * deltas) + HY_DECAY_SHIFT)

def short_conv(z, w, b):
    zp = jnp.pad(z, ((0, 0), (1, 1), (0, 0)))
    return zp[:, :-2] * w[0] + zp[:, 1:-1] * w[1] + zp[:, 2:] * w[2] + b

def long_conv(u, h_fwd, h_bwd, bias):
    n = u.shape[1]
    n_fft = 2 * n
    spec_f = jnp.fft.rfft(h_fwd, n=n_fft, axis=0)
    spec_b = jnp.fft.rfft(h_bwd, n=n_fft, axis=0)
    y_f = jnp.fft.irfft(jnp.fft.rfft(u, n=n_fft, axis=1) * spec_f, n=n_fft, axis=1)[:, :n]
    y_b = jnp.fft.irfft(jnp.fft.rfft(u[:, ::-1], n=n_fft, axis=1) * spec_b, n=n_fft, axis=1)[:, :n][:, ::-1]
    return y_f + y_b + u * bias

def hyena_mixer(z, filt, conv_w, conv_b, bias):
    b, n, _ = z.shape
    u = short_conv(z, conv_w, conv_b).astype(jnp.float32)
    v, g1, g2 = jnp.split(u, 3, axis=-1)
    filt = filt.reshape(n, HY_ORDER, 2, HY_WIDTH)
    bias = bias.astype(jnp.float32)
    y = v
    for o, g in enumerate((g1, g2)):
        y = g * long_conv(y, filt[:, o, 0], filt[:, o, 1], bias[o])
    return y.astype(z.dtype)

def merge_branches(z, outs, w_branches, w_out):
    gates = jax.nn.sigmoid(z[..., OFF_GATE:].astype(jnp.float32))
    gates = gates.reshape(z.shape[:-1] + (N_BRANCH, D_MODEL))
    merged = gates[..., 0, :] * (outs[0] @ w_branches[0]).astype(jnp.float32)
    for j in range(1, N_BRANCH):
        merged = merged + gates[..., j, :] * (outs[j] @ w_branches[j]).astype(jnp.float32)
    return merged.astype(z.dtype) @ w_out

def swiglu(h, w_gu, w_down):
    gu = h @ w_gu
    return (jax.nn.silu(gu[..., :D_FF]) * gu[..., D_FF:]) @ w_down

def setup_inputs(seed: int = 0) -> dict:
    key = jax.random.key(seed)
    keys = iter(jax.random.split(key, 48))

    def nrm(shape, scale):
        return scale * jax.random.normal(next(keys), shape, jnp.float32)

    L = DEPTH
    D = D_MODEL
    x = nrm((BATCH, SEQ, D), 1.0)
    c = nrm((BATCH, D), 1.0)
    ctx = nrm((BATCH, CTX_LEN, D), 1.0)
    c_ctx = nrm((D,), 1.0)
    ada_w = nrm((L, D, N_MOD * D), 0.5 * D ** -0.5)
    ada_b = nrm((L, N_MOD * D), 0.01)
    norm_mix = 1.0 + nrm((L, D), 0.01)
    w_in = nrm((L, D, IN_WIDTH), D ** -0.5)
    mla_q_norm = 1.0 + nrm((L, MLA_Q_LORA), 0.01)
    mla_w_uq = nrm((L, MLA_Q_LORA, MLA_HEADS * (MLA_NOPE + MLA_ROPE)), MLA_Q_LORA ** -0.5)
    mla_kv_norm = 1.0 + nrm((L, MLA_KV_LORA), 0.01)
    mla_w_ukv = nrm((L, MLA_KV_LORA, MLA_HEADS * (MLA_NOPE + MLA_V)), MLA_KV_LORA ** -0.5)
    s5_lam_re = -0.5 + nrm((L, 2, S5_GROUPS, S5_STATE), 0.01)
    s5_lam_im = math.pi * jnp.arange(S5_STATE, dtype=jnp.float32) + nrm((L, 2, S5_GROUPS, S5_STATE), 0.01)
    s5_log_dt = jax.random.uniform(next(keys), (L, 2, S5_GROUPS), jnp.float32,
                                   math.log(S5_DT_MIN), math.log(S5_DT_MAX))
    s5_b_re = nrm((L, 2, S5_GROUPS, S5_STATE, S5_GROUP), (2 * S5_GROUP) ** -0.5)
    s5_b_im = nrm((L, 2, S5_GROUPS, S5_STATE, S5_GROUP), (2 * S5_GROUP) ** -0.5)
    s5_c_re = nrm((L, 2, S5_GROUPS, S5_GROUP, S5_STATE), S5_STATE ** -0.5)
    s5_c_im = nrm((L, 2, S5_GROUPS, S5_GROUP, S5_STATE), S5_STATE ** -0.5)
    s5_d = nrm((L, S5_WIDTH), 0.5)
    s5_w_glu = nrm((L, S5_WIDTH, S5_WIDTH), S5_WIDTH ** -0.5)
    hy_conv_w = nrm((L, 3, 3 * HY_WIDTH), 0.5)
    hy_conv_b = nrm((L, 3 * HY_WIDTH), 0.01)
    hy_f_w1 = nrm((L, HY_POS_DIM, HY_FILTER_HIDDEN), HY_POS_DIM ** -0.5)
    hy_f_b1 = nrm((L, HY_FILTER_HIDDEN), 0.1)
    hy_f_w2 = nrm((L, HY_FILTER_HIDDEN, HY_FILTER_HIDDEN), HY_FILTER_HIDDEN ** -0.5)
    hy_f_b2 = nrm((L, HY_FILTER_HIDDEN), 0.1)
    hy_f_w3 = nrm((L, HY_FILTER_HIDDEN, HY_FILTER_OUT), 0.03 * HY_FILTER_HIDDEN ** -0.5)
    hy_f_freq = 1.0 + nrm((L, HY_FILTER_HIDDEN), 0.01)
    hy_bias = nrm((L, HY_ORDER, HY_WIDTH), 0.5)
    w_branch_mla = nrm((L, MLA_HEADS * MLA_V, D), (MLA_HEADS * MLA_V) ** -0.5)
    w_branch_s5 = nrm((L, S5_WIDTH, D), S5_WIDTH ** -0.5)
    w_branch_hy = nrm((L, HY_WIDTH, D), HY_WIDTH ** -0.5)
    w_out = nrm((L, D, D), D ** -0.5)
    norm_ffn = 1.0 + nrm((L, D), 0.01)
    ffn_w_gu = nrm((L, D, 2 * D_FF), D ** -0.5)
    ffn_w_down = nrm((L, D_FF, D), D_FF ** -0.5)
    final_norm = 1.0 + nrm((D,), 0.01)
    return {
        "x": x, "c": c, "ctx": ctx, "c_ctx": c_ctx,
        "ada_w": ada_w, "ada_b": ada_b, "norm_mix": norm_mix, "w_in": w_in,
        "mla_q_norm": mla_q_norm, "mla_w_uq": mla_w_uq, "mla_kv_norm": mla_kv_norm, "mla_w_ukv": mla_w_ukv,
        "s5_lam_re": s5_lam_re, "s5_lam_im": s5_lam_im, "s5_log_dt": s5_log_dt,
        "s5_b_re": s5_b_re, "s5_b_im": s5_b_im, "s5_c_re": s5_c_re, "s5_c_im": s5_c_im,
        "s5_d": s5_d, "s5_w_glu": s5_w_glu,
        "hy_conv_w": hy_conv_w, "hy_conv_b": hy_conv_b,
        "hy_f_w1": hy_f_w1, "hy_f_b1": hy_f_b1, "hy_f_w2": hy_f_w2, "hy_f_b2": hy_f_b2,
        "hy_f_w3": hy_f_w3, "hy_f_freq": hy_f_freq, "hy_bias": hy_bias,
        "w_branch_mla": w_branch_mla, "w_branch_s5": w_branch_s5, "w_branch_hy": w_branch_hy,
        "w_out": w_out, "norm_ffn": norm_ffn, "ffn_w_gu": ffn_w_gu, "ffn_w_down": ffn_w_down,
        "final_norm": final_norm,
    }

def reference(x, c, ctx, c_ctx, ada_w, ada_b, norm_mix, w_in,
              mla_q_norm, mla_w_uq, mla_kv_norm, mla_w_ukv,
              s5_lam_re, s5_lam_im, s5_log_dt, s5_b_re, s5_b_im, s5_c_re, s5_c_im, s5_d, s5_w_glu,
              hy_conv_w, hy_conv_b, hy_f_w1, hy_f_b1, hy_f_w2, hy_f_b2, hy_f_w3, hy_f_freq, hy_bias,
              w_branch_mla, w_branch_s5, w_branch_hy, w_out,
              norm_ffn, ffn_w_gu, ffn_w_down, final_norm):
    bsz, n_tok, _ = x.shape
    n_ctx = ctx.shape[1]
    rope = axial_rope(n_tok)
    h0 = jnp.zeros((bsz, S5_GROUPS, S5_STATE), jnp.complex64)
    for i in range(DEPTH):
        last = i == DEPTH - 1
        mx = (jax.nn.silu(c) @ ada_w[i] + ada_b[i]).reshape(bsz, N_MOD, 1, D_MODEL)
        mc = (jax.nn.silu(c_ctx) @ ada_w[i] + ada_b[i]).reshape(N_MOD, D_MODEL)

        hx = modulate(rmsnorm(x, norm_mix[i]), mx[:, 0], mx[:, 1])
        hc = modulate(rmsnorm(ctx, norm_mix[i]), mc[0], mc[1])
        zx = hx @ w_in[i]
        zc = hc @ (w_in[i][:, :OFF_HY] if last else w_in[i])

        k_c, v_c = mla_keys_values(zc, mla_kv_norm[i], mla_w_ukv[i], None)
        k_x, v_x = mla_keys_values(zx, mla_kv_norm[i], mla_w_ukv[i], rope)
        q_x = mla_queries(zx, mla_q_norm[i], mla_w_uq[i], rope)
        a_x = blocked_attend(q_x, jnp.concatenate([k_c, k_x], axis=1), jnp.concatenate([v_c, v_x], axis=1))

        disc = tuple(s5_discretize(s5_lam_re[i, d], s5_lam_im[i, d], s5_log_dt[i, d],
                                   s5_b_re[i, d], s5_b_im[i, d]) for d in range(2))
        y_c, finals = s5_mixer(zc[..., OFF_S5:OFF_HY], disc, s5_c_re[i], s5_c_im[i], s5_d[i],
                               (h0, h0), not last)
        y_x, _ = s5_mixer(zx[..., OFF_S5:OFF_HY], disc, s5_c_re[i], s5_c_im[i], s5_d[i], finals, True)
        s_x = s5_glu(y_x, s5_w_glu[i]).astype(x.dtype)

        fparams = (hy_f_w1[i], hy_f_b1[i], hy_f_w2[i], hy_f_b2[i], hy_f_w3[i], hy_f_freq[i])
        e_x = hyena_mixer(zx[..., OFF_HY:OFF_GATE], hyena_filters(n_tok, *fparams),
                          hy_conv_w[i], hy_conv_b[i], hy_bias[i])

        branches = (w_branch_mla[i], w_branch_s5[i], w_branch_hy[i])
        x = x + mx[:, 2] * merge_branches(zx, (a_x, s_x, e_x), branches, w_out[i])
        x = x + mx[:, 5] * swiglu(modulate(rmsnorm(x, norm_ffn[i]), mx[:, 3], mx[:, 4]),
                                  ffn_w_gu[i], ffn_w_down[i])

        if not last:
            a_c = attend(mla_queries(zc, mla_q_norm[i], mla_w_uq[i], None), k_c, v_c).reshape(bsz, n_ctx, -1)
            s_c = s5_glu(y_c, s5_w_glu[i]).astype(ctx.dtype)
            e_c = hyena_mixer(zc[..., OFF_HY:OFF_GATE], hyena_filters(n_ctx, *fparams),
                              hy_conv_w[i], hy_conv_b[i], hy_bias[i])
            ctx = ctx + mc[2] * merge_branches(zc, (a_c, s_c, e_c), branches, w_out[i])
            ctx = ctx + mc[5] * swiglu(modulate(rmsnorm(ctx, norm_ffn[i]), mc[3], mc[4]),
                                       ffn_w_gu[i], ffn_w_down[i])
    return rmsnorm(x, final_norm)


_drawn_inputs = setup_inputs


def setup_inputs(seed=0):
    import zlib

    import numpy as np

    out = dict(_drawn_inputs(seed))
    spreads = {}
    factors = {'ctx': 8.0,
     'c_ctx': 4.158,
     'ada_b': 6.482,
     'norm_mix': 8.0,
     'mla_q_norm': 64.0,
     'mla_w_uq': 3.522,
     'mla_kv_norm': 64.0,
     's5_lam_re': 64.0,
     's5_lam_im': 55.008,
     's5_log_dt': 62.912,
     's5_b_re': 64.0,
     's5_b_im': 64.0,
     's5_c_re': 64.0,
     's5_c_im': 64.0,
     's5_w_glu': 60.73,
     'hy_conv_b': 8.0,
     'hy_f_b1': 8.0,
     'hy_f_w2': 2.714,
     'hy_f_b2': 8.0,
     'hy_f_w3': 3.064,
     'hy_f_freq': 8.0,
     'norm_ffn': 64.0,
     'final_norm': 29.886,
     's5_d': 5.77,
     'w_branch_s5': 5.191}
    for name, (base, spread) in spreads.items():
        noise = np.random.default_rng([zlib.crc32(name.encode()), seed]).standard_normal(out[name].shape)
        drawn = base * np.exp(spread * noise) if base else spread * noise
        out[name] = __import__('jax').numpy.asarray(drawn.astype(out[name].dtype))
    for name, factor in factors.items():
        out[name] = (out[name] * factor).astype(out[name].dtype)
    return out
```

```python
from contextlib import ExitStack

import concourse.bass as bass
from concourse import mybir

F32 = mybir.dt.float32
F32R = mybir.dt.float32r
ACT = mybir.ActivationFunctionType
ALU = mybir.AluOpType
AX = mybir.AxisListType

P = 128
D = 1024
KD = D // P
T = 512
TT = T // P
TC = 256
TTC = TC // P
EPS = 1e-6
HEADS, NOPE, ROPE, VD = 8, 64, 32, 64
QK = NOPE + ROPE
QL, KVL = 256, 128
KEYS = T + TC
KT = KEYS // P
SCALE = float(QK) ** -0.5
G, GC, ST = 32, 16, 64
PAIRS = G // 2
L = 8
NCX, NCC = T // L, TC // L
NCH = NCX + NCC
W5 = 512
HC = 256
FF = 2816
FT = FF // P
O_KV, O_KR, O_S5, O_HY, O_GATE = 256, 384, 416, 928, 2464
IN_W = 5536
TWO_PI_HI = 6.28125
TWO_PI_LO = 0.0019353071795864769
INV_2PI = 0.15915494309189535
ROUND = 12582912.0
PI = 3.1415925

C_ID, C_EYE16, C_GS, C_ALT, C_E9, C_K = 0, 128, 144, 148, 276, 285
C_N = C_K + NCH

VECS = [("c", 8), ("c_ctx", 8), ("norm_mix", 8), ("norm_ffn", 8), ("final_norm", 8), ("ada_b", 48),
        ("mla_q_norm", 2), ("mla_kv_norm", 1), ("s5_d", 4), ("hy_conv_b", 12)]
VOFF = {}
_at = 0
for _n, _r in VECS:
    VOFF[_n] = _at
    _at += _r
VROWS = _at


NSMALL = 1 + len(VECS) + 1 + 3
NS5 = 3 + 2 + 2 * 4 * 2 * 8
NHYP = 4


def build(nc, a, scratch, out):
    base = (nc.sbuf_base + 31) // 32 * 32
    ctx = ExitStack()
    with ctx:
        def sem(name):
            return ctx.enter_context(nc.semaphore(name))

        class Region:

            def __init__(self, start, end):
                self.at, self.end = start, end

            def __call__(self, name, shape, dt=F32):
                n = 4
                for s in shape[1:]:
                    n *= s
                n = (n + 31) // 32 * 32
                t = nc.alloc_sbuf_tensor_at(name, shape, dt, offset=base + self.at)
                self.at += n
                assert self.at <= self.end, (name, self.at, self.end)
                return t

        PS = ctx.enter_context(nc.psum_tensor("PS", [P, 8 * 512], F32))

        def bank(b, n=512, o=0):
            return PS[:, 512 * b + o:512 * b + o + n]

        K = 1024
        r = Region(0, 14 * K)
        cst = r("cst", [P, C_N])
        ident = cst[:, C_ID:C_ID + P]
        vc1 = r("vc1", [P, VROWS])
        vc2 = r("vc2", [P, 36])
        vc3 = r("vc3", [64, 3])
        modx = r("modx", [P, 48])
        modc = r("modc", [P, 16])
        amix = r("amix", [P, 2, KD])
        affn = r("affn", [P, KD])
        silc = r("silc", [P, 16])
        rs = r("rs", [P, 3, 6, 16])
        altr = r("altr", [P, P], F32R)
        alt_row = r("alt_row", [1, T], F32R)
        tmp = [r(f"tmp{i}", [P, T]) for i in range(3)]
        nyl = r("nyl", [1, HC], F32R)
        RING = 4
        r = Region(14 * K, 62 * K)
        raw = [r(f"raw{i}", [P, 1024]) for i in range(RING)]
        whi = [r(f"whi{i}", [P, 1024], F32R) for i in range(RING)]
        wlo = [r(f"wlo{i}", [P, 1024], F32R) for i in range(RING)]
        r = Region(62 * K, 94 * K)
        h_hi = r("h_hi", [P, KD, T], F32R)
        h_lo = r("h_lo", [P, KD, T], F32R)
        r = Region(62 * K, 94 * K)
        ytok = r("ytok", [P, TT, D])
        fnorm = r("fnorm", [P, D])
        fsq = r("fsq", [P, D])
        Z = 94 * K
        ZEND = 207 * K + 512
        r = Region(Z + 97 * K, ZEND)
        U = r("U", [P, G, P])
        r = Region(Z + 81 * K, Z + 97 * K)
        o_hi = r("o_hi", [P, TT, T], F32R)
        o_lo = r("o_lo", [P, TT, T], F32R)
        r = Region(Z, Z + 81 * K)
        hc_hi = r("hc_hi", [P, KD, TC], F32R)
        hc_lo = r("hc_lo", [P, KD, TC], F32R)
        a_at = r.at
        vr1 = r("vr1", [VROWS, P])
        vr2 = r("vr2", [36, P])
        vr3 = r("vr3", [3, 64])
        xt = r("xt", [P, TT + TTC, D])
        ada = [r(f"ada{i}", [P, KD, P]) for i in range(3)]
        sq0 = r("sq0", [P, D])
        r = Region(a_at, Z + 81 * K)
        us = r("us", [P, KT, W5])
        uch = r("uch", [NCH, L, W5])
        uch2 = r("uch2", [NCH, G, L, GC])
        c_at = r.at
        r = Region(a_at, Z + 81 * K)
        qtok = r("qtok", [P, TT, HEADS, QK])
        kvT_hi = r("kvT_hi", [P, KEYS], F32R)
        kvT_lo = r("kvT_lo", [P, KEYS], F32R)
        krtok = r("krtok", [P, KT, ROPE])
        b_at = r.at
        r = Region(c_at, Z + 97 * K)
        rope = r("rope", [P, TT, 2, 16])
        ztok = r("ztok", [P, KT, 416])
        qnT_hi = r("qnT_hi", [P, 2, T], F32R)
        qnT_lo = r("qnT_lo", [P, 2, T], F32R)
        rt = r("rt", [P, 4, HEADS, 16])
        sq1 = r("sq1", [P, 256])
        r = Region(b_at, Z + 81 * K)
        prob = r("prob", [P, TT, KEYS])
        kT_hi = r("kT_hi", [QK, KEYS], F32R)
        kT_lo = r("kT_lo", [QK, KEYS], F32R)
        qT_hi = r("qT_hi", [QK, T], F32R)
        qT_lo = r("qT_lo", [QK, T], F32R)
        v_hi = r("v_hi", [P, KT, P], F32R)
        v_lo = r("v_lo", [P, KT, P], F32R)
        mx = r("mx", [P, 2 * TT * HEADS])
        r = Region(Z, a_at)
        pTa_hi = r("pTa_hi", [P, 4, T], F32R)
        pTa_lo = r("pTa_lo", [P, 4, T], F32R)
        r = Region(b_at + 30 * K, Z + 81 * K)
        pTb_hi = r("pTb_hi", [P, 2, T], F32R)
        pTb_lo = r("pTb_lo", [P, 2, T], F32R)
        r = Region(Z, Z + 16 * K)
        merged = r("merged", [P, KD, T])
        r = Region(Z + 16 * K, Z + 81 * K)
        NPD = 2 * PAIRS
        lpr = r("lpr", [P, NPD, 9])
        lpi = r("lpi", [P, NPD, 9])
        th8 = r("th8", [P, NPD])
        rho8 = r("rho8", [P, NPD])
        base4 = r("base4", [P, 4, NPD])
        bbr = r("bbr", [P, NPD, GC])
        bbi = r("bbi", [P, NPD, GC])
        ctr = r("ctr", [P, NPD, GC])
        cti = r("cti", [P, NPD, GC])
        y5tok = r("y5tok", [P, TT, W5])
        s5_at = r.at
        row = r("row", [NPD, 12, P])
        dt2 = r("dt2", [NPD, 2])
        bld = r("bld", [P, 2, NPD, GC])
        cld = r("cld", [P, 2, 4, P])
        lt = r("lt", [P, 4, NPD * 9])
        r = Region(s5_at, Z + 97 * K)
        bdr = r("bdr", [P, 8, 32])
        bdi = r("bdi", [P, 8, 32])
        pmr = r("pmr", [P, 8, P])
        pmi = r("pmi", [P, 8, P])
        clr = r("clr", [P, 8, 9, GC])
        cli = r("cli", [P, 8, 9, GC])
        t5 = [r(f"t5_{i}", [P, 4 * 9 * GC]) for i in range(2)]
        WT = r("WT", [P, 2, 8, P])
        Mt = r("Mt", [P, 8, P])
        K2 = r("K2", [P, 15, GC])
        tsin = r("tsin", [P, 8, NCH])
        tcos = r("tcos", [P, 8, NCH])
        gr = r("gr", [P, 8, NCH])
        gi = r("gi", [P, 8, NCH])
        H = r("H", [P, 2, 8, NCX])
        Y2 = r("Y2", [NCX, L, P])
        sgr, sgi = (x[:, :, :].rearrange("p a b -> p (a b)")[:, 0:8 * NCH].rearrange("p (a c) -> p a c", c=NCH)
                    for x in (pmr, pmi))
        r = Region(s5_at, Z + 81 * K)
        yg = r("yg", [P, TT, T])
        yg_hi = r("yg_hi", [P, TT, T], F32R)
        yg_lo = r("yg_lo", [P, TT, T], F32R)
        r = Region(Z + 16 * K, ZEND)
        fc_hi = r("fc_hi", [P, 4, T], F32R)
        fc_lo = r("fc_lo", [P, 4, T], F32R)
        fs_hi = r("fs_hi", [P, 4, T], F32R)
        fs_lo = r("fs_lo", [P, 4, T], F32R)
        e_at = r.at
        e_hi = r("e_hi", [P, TT, T], F32R)
        e_lo = r("e_lo", [P, TT, T], F32R)
        u_hi = r("u_hi", [P, TT, HC], F32R)
        u_lo = r("u_lo", [P, TT, HC], F32R)
        y_hi = r("y_hi", [P, TT, 2 * HC], F32R)
        y_lo = r("y_lo", [P, TT, 2 * HC], F32R)
        g1t = r("g1t", [P, TT, HC])
        g2c = r("g2c", [P, 2, T])
        Gs = r("Gs", [P, 4, 2 * HC])
        hid2 = r("hid2", [64, T])
        w3 = r("w3", [64, 2, HC])
        win = r("win", [P, 2, HC])
        nyg = r("nyg", [1, HC])
        nyh = r("nyh", [1, HC], F32R)
        hyb = r("hyb", [1, HC])
        r = Region(e_at, e_at + 16 * K)
        hid1 = r("hid1", [64, T])
        harg = r("harg", [64, T])
        hrnd = r("hrnd", [64, T])
        zpos = r("zpos", [33, T])
        w12 = r("w12", [64, 2, 64])
        r = Region(Z + 16 * K, Z + 104 * K)
        act_hi = r("act_hi", [P, FT, T], F32R)
        act_lo = r("act_lo", [P, FT, T], F32R)
        r = Region(Z + 16 * K, Z + 104 * K)
        m_hi = r("m_hi", [P, KD, T], F32R)
        m_lo = r("m_lo", [P, KD, T], F32R)
        x2t = r("x2t", [P, TT, D])
        xT = merged
        r = Region(Z + 104 * K, ZEND)
        sqk = [r(f"sqk{i}", [P, T]) for i in range(2)]
        vrow = r("vrow", [P, T])
        srow = r("srow", [P, T])
        onesq = r("onesq", [P, P])

        bank_free = [sem(f"bank_free{b}") for b in range(8)]
        raw_in = [sem(f"raw_in{i}") for i in range(RING)]
        s_hi = sem("chunk_hi")
        s_lo = sem("chunk_lo")
        s_phase = sem("phase")
        s_act, s_dve, s_dvx = sem("act_chain"), sem("dve_chain"), sem("dve_for_others")
        ld = {n: sem("in_" + n) for n in ("small", "x", "ctx", "rope", "uch", "kfilt", "kread", "s5", "ytok",
                                          "hyp", "w3", "win", "hyb", "x2", "fnorm", "out")}
        mm = {n: sem("pe_" + n) for n in ("vec", "ada", "xT", "s5in", "uT", "proj", "nT", "q", "att", "merge",
                                          "s5", "glu", "hy", "out", "norm", "up", "down", "end")}
        s = {n: sem("s_" + n) for n in (
            "silu", "vc", "s5a", "sq", "var", "sqrt", "xh", "htmp", "hth", "htl", "mod", "us", "zn", "ntmp", "nth", "ntl",
            "qrope", "krope", "vones", "aqk", "exp", "max", "pTh", "oun", "oth", "otl", "sig", "s5row", "s5col",
            "s5c", "angle", "trig", "mag", "bb", "pm", "K2", "WTd", "rot", "Hs", "Yq", "gelu", "gtmp", "gth", "gtl",
            "hya", "hys", "hid", "zc", "zt", "cv", "hs", "hsh", "hsl", "yt", "yth", "ytl", "ut", "uth", "utl",
            "alt", "gsc", "nyq", "mh", "ml", "x1", "sq2", "vf", "sf", "h2t", "h2h", "h2l", "silf", "at", "ath",
            "atl", "x3", "yo", "fin")}

        chunks = []

        def add(src, kt, n, kind="split", dest=None):
            chunks.append((src, kt, n, kind, dest))

        def wcols(w, k0, kt, c0, n):
            return w[k0 * P:(k0 + kt) * P, c0:c0 + n].rearrange("(k p) n -> p k n", p=P)

        for m in range(16):
            add(wcols(a["ada_w"], 0, KD, m * P, P), KD, P, "plain")
        for i in range(4):
            add(wcols(a["w_in"], 2 * i, 2, O_S5, W5), 2, W5)
        for i in range(4):
            add(wcols(a["w_in"], 2 * i, 2, 0, 416), 2, 416)
        for k in range(2):
            add(wcols(a["mla_w_uq"], k, 1, 0, 768), 1, 768)
        add(wcols(a["mla_w_ukv"], 0, 1, 0, 1024), 1, 1024)
        branch_w = ["w_branch_mla", "w_branch_s5", "w_branch_hy"]

        def merge_chunks(j):
            for m in range(KD):
                add(wcols(a["w_in"], 0, KD, O_GATE + j * D + m * P, P), KD, P)
                add(wcols(a[branch_w[j]], 0, 4, m * P, P), 4, P)

        merge_chunks(0)
        for m in range(4):
            add(wcols(a["s5_w_glu"], 0, 4, m * P, P), 4, P)
        merge_chunks(1)
        for m in range(16, 48):
            add(wcols(a["ada_w"], 0, KD, m * P, P), KD, P, "plain")
        for src, hi_, lo_ in ((a["dft_cos"], fc_hi, fc_lo), (a["dft_sin"], fs_hi, fs_lo)):
            for i in range(2):
                add(wcols(src, 2 * i, 2, 0, T), 2, T, "const",
                    (hi_[:, 2 * i:2 * i + 2, :].rearrange("p a b -> p (a b)"),
                     lo_[:, 2 * i:2 * i + 2, :].rearrange("p a b -> p (a b)")))
        for half in range(2):
            for part in range(3):
                for i in range(2):
                    add(wcols(a["w_in"], 0, KD, O_HY + part * W5 + half * HC + i * P, P), KD, P)
        merge_chunks(2)
        for m in range(KD):
            add(wcols(a["w_out"], 0, KD, m * P, P), KD, P)
        for f in range(FT):
            add(wcols(a["ffn_w_gu"], 0, KD, f * P, P), KD, P)
            add(wcols(a["ffn_w_gu"], 0, KD, FF + f * P, P), KD, P)
        DOWN = (6, 6, 5, 5)
        for m in range(KD):
            k0 = 0
            for kt in DOWN:
                add(wcols(a["ffn_w_down"], k0, kt, m * P, P), kt, P)
                k0 += kt
        nth_split = []
        n = 0
        for ch in chunks:
            nth_split.append(n)
            n += ch[3] != "plain"

        uses = [0] * 8
        ends = {}
        taken = {}
        counts = {}

        def close(ins, which, name):
            counts[which] = counts.get(which, 0) + 1
            ins.then_inc(mm[which], 1)
            ends[name] = (mm[which], counts[which])

        def wait(eng, at):
            eng.wait_ge(at[0], at[1])

        block = ctx.enter_context(nc.Block())

        @block.tensor
        def _(pe):
            nxt = [0]

            def open_(b, name):
                if uses[b]:
                    pe.wait_ge(bank_free[b], uses[b])
                uses[b] += 1
                taken[name] = (bank_free[b], uses[b])

            def chunk():
                c = nxt[0]
                nxt[0] += 1
                _, kt, n, kind, dest = chunks[c]
                i = c % RING
                if kind == "plain":
                    pe.wait_ge(raw_in[i], 16 * (c // RING + 1))
                    return c, raw[i][:, 0:kt * n].rearrange("p (k n) -> p k n", k=kt)
                pe.wait_ge(s_lo, nth_split[c] + 1)
                if kind == "const":
                    return c, None
                return c, tuple(w[i][:, 0:kt * n].rearrange("p (k n) -> p k n", k=kt) for w in (whi, wlo))

            def mm3(o, w, x, first, last):
                pe.matmul(o, w[0], x[0], start=first, stop=False)
                pe.matmul(o, w[0], x[1], start=False, stop=False)
                return pe.matmul(o, w[1], x[0], start=False, stop=last)

            def to_tokens(m):
                wait(pe, taken[("down", m)])
                open_(4 + m % 4, ("yo", m))
                for t in range(TT):
                    ins = pe.transpose(bank(4 + m % 4, P, t * P), xT[:, m, t * P:(t + 1) * P], ident)
                close(ins, "end", ("yo", m))

            def phase_end(k):
                pe.drain().then_inc(s_phase, 1)
                pe.wait_ge(s_phase, 3 * k)

            pe.wait_ge(ld["small"], 16 * NSMALL)
            open_(0, "vec")
            pe.transpose(bank(0, VROWS), vr1[:, :], cst[0:VROWS, C_ID:C_ID + VROWS])
            pe.transpose(bank(0, 36, 128), vr2[:, :], cst[0:36, C_ID:C_ID + 36])
            close(pe.transpose(bank(0, 3, 256)[0:64], vr3[:, :], cst[0:3, C_ID:C_ID + 3]), "vec", "vec")

            def ada_part(ms, b, name):
                open_(b, name)
                for m in ms:
                    c, w = chunk()
                    o = bank(b, 2, 2 * m)
                    for k in range(KD):
                        ins = pe.matmul(o, w[:, k, :], silc[:, k:k + 9:8], start=(k == 0), stop=(k == KD - 1))
                    close(ins, "ada", ("chunk", c))
                ends[name] = ends[("chunk", c)]

            pe.wait_ge(s["silu"], 1)
            ada_part(range(16), 1, "ada0")

            pe.wait_ge(s["xh"], TT + TTC)
            for k in range(KD):
                open_(2 + k % 3, ("xT", k, 0))
                for t in range(TT):
                    ins = pe.transpose(bank(2 + k % 3, P, t * P), xt[:, t, k * P:(k + 1) * P], ident)
                close(ins, "xT", ("xT", k, 0))
                open_(5 + k % 3, ("xT", k, 1))
                for t in range(TTC):
                    ins = pe.transpose(bank(5 + k % 3, P, t * P), xt[:, TT + t, k * P:(k + 1) * P], ident)
                close(ins, "xT", ("xT", k, 1))

            def tokens(t, k):
                hi_, lo_, o = (h_hi, h_lo, t) if t < TT else (hc_hi, hc_lo, t - TT)
                return hi_[:, k, o * P:(o + 1) * P], lo_[:, k, o * P:(o + 1) * P]

            pe.wait_ge(s["htl"], 2 * KD)
            for i in range(4):
                c, w = chunk()
                for t in range(KT):
                    if i == 0:
                        open_(t, ("us", t))
                    for k in range(2):
                        ins = mm3(bank(t), tokens(t, 2 * i + k), (w[0][:, k, :], w[1][:, k, :]),
                                  i == 0 and k == 0, i == 3 and k == 1)
                    if i == 3:
                        close(ins, "s5in", ("us", t))
                if i < 3:
                    close(ins, "s5in", ("chunk", c))
            ends[("chunk", c)] = ends[("us", KT - 1)]

            for i in range(4):
                c, w = chunk()
                for t in range(KT):
                    o, n = (0, 416) if t < TT else (256, 160)
                    if i == 0:
                        open_(t, ("z", t))
                    for k in range(2):
                        ins = mm3(bank(t, n, o), tokens(t, 2 * i + k), (w[0][:, k, o:], w[1][:, k, o:]),
                                  i == 0 and k == 0, i == 3 and k == 1)
                    if i == 3:
                        close(ins, "proj", ("z", t))
                if i < 3:
                    close(ins, "proj", ("chunk", c))
            ends[("chunk", c)] = ends[("z", KT - 1)]

            pe.wait_ge(s["us"], 1)
            for i in range(8):
                b = 6 + i % 2
                open_(b, ("uT", i))
                for j in range(4):
                    g = 4 * i + j
                    ins = pe.transpose(bank(b, NCH, j * NCH), uch2[:, g].rearrange("c s m -> c (s m)"),
                                       cst[0:NCH, C_ID:C_ID + NCH])
                close(ins, "uT", ("uT", i))
            phase_end(1)

            pe.wait_ge(s["zn"], KT)
            for k in range(2):
                open_(k, ("nT", k))
                for t in range(TT):
                    ins = pe.transpose(bank(k, P, t * P), ztok[:, t, k * P:(k + 1) * P], ident)
                close(ins, "nT", ("nT", k))
            for k in range(2):
                open_(2 + k, ("nT", 2 + k))
                for t in range(*((0, TT) if k == 0 else (TT, KT))):
                    ins = pe.transpose(bank(2 + k, P, (t % TT) * P), ztok[:, t, QL:QL + KVL], ident)
                close(ins, "nT", ("nT", 2 + k))
            pe.wait_ge(s["ntl"], 4)
            c0, w0 = chunk()
            c1, w1 = chunk()
            for t in range(TT):
                for hf in range(2):
                    b = 4 + (2 * t + hf) % 4
                    open_(b, ("q", t, hf))
                    for k, w in enumerate((w0, w1)):
                        q = qnT_hi[:, k, t * P:(t + 1) * P], qnT_lo[:, k, t * P:(t + 1) * P]
                        ins = mm3(bank(b, 384), q, tuple(x[:, 0, hf * 384:(hf + 1) * 384] for x in w),
                                  k == 0, k == 1)
                    close(ins, "q", ("q", t, hf))
            ends[("chunk", c0)] = ends[("chunk", c1)] = ends[("q", TT - 1, 1)]
            phase_end(2)

            for part, (t0, t1) in enumerate(((0, TT), (TT, KT))):
                open_(part, ("kr", part))
                for t in range(t0, t1):
                    ins = pe.transpose(bank(part, P, (t - t0) * P)[0:ROPE], krtok[:, t, :], ident)
                close(ins, "att", ("kr", part))
            c, ukv = chunk()
            kv = kvT_hi, kvT_lo
            for h in range(HEADS):
                open_(0, ("qT", h))
                for t in range(TT):
                    ins = pe.transpose(bank(0, P, t * P)[0:QK], qtok[:, t, h, :], ident)
                close(ins, "att", ("qT", h))
                for part, (k0, n) in enumerate(((0, T), (T, TC))):
                    open_(1 + part, ("k", h, part))
                    close(mm3(bank(1 + part, n), tuple(x[:, 0, h * P:(h + 1) * P] for x in ukv),
                              tuple(x[:, k0:k0 + n] for x in kv), True, True), "att", ("k", h, part))
                open_(3, ("v", h))
                for t in range(KT):
                    ins = mm3(bank(3, VD, t * VD), tuple(x[:, t * P:(t + 1) * P] for x in kv),
                              tuple(x[:, 0, h * P + NOPE:(h + 1) * P] for x in ukv), True, True)
                close(ins, "att", ("v", h))
                wait(pe, taken[("qT", h)])
                wait(pe, taken[("k", h, 0)])
                wait(pe, taken[("k", h, 1)])
                wait(pe, taken[("kr", 1)])
                for t in range(TT):
                    b = 4 + 2 * (t % 2)
                    open_(b, ("s", h, t))
                    q = qT_hi[:, t * P:(t + 1) * P], qT_lo[:, t * P:(t + 1) * P]
                    mm3(bank(b), q, (kT_hi[:, 0:T], kT_lo[:, 0:T]), True, True)
                    close(mm3(bank(b + 1, TC), q, (kT_hi[:, T:KEYS], kT_lo[:, T:KEYS]), True, True),
                          "att", ("s", h, t))
                for t in range(TT):
                    wait(pe, taken[("s", h, t)])
                for kt in range(KT):
                    open_(kt % 3, ("pT", h, kt))
                    for t in range(TT):
                        ins = pe.transpose(bank(kt % 3, P, t * P), prob[:, t, kt * P:(kt + 1) * P], ident)
                    close(ins, "att", ("pT", h, kt))
                wait(pe, taken[("v", h)])
                pe.wait_ge(s["vones"], 2)
                open_(3, ("o", h))
                for kt in range(KT):
                    wait(pe, taken[("pT", h, kt)])
                    pt = (pTa_hi[:, kt, :], pTa_lo[:, kt, :]) if kt < 4 else (pTb_hi[:, kt - 4, :], pTb_lo[:, kt - 4, :])
                    ins = mm3(bank(3), (v_hi[:, kt, :], v_lo[:, kt, :]), pt, kt == 0, kt == KT - 1)
                close(ins, "att", ("o", h))
            ends[("chunk", c)] = ends[("v", HEADS - 1)]
            phase_end(3)

            def merge(j, x):
                for m in range(KD):
                    b = 2 * (m % 4)
                    c, w = chunk()
                    open_(b, ("gate", j, m))
                    for k in range(KD):
                        ins = mm3(bank(b), (w[0][:, k, :], w[1][:, k, :]), (h_hi[:, k, :], h_lo[:, k, :]),
                                  k == 0, k == KD - 1)
                    close(ins, "merge", ("gate", j, m))
                    ends[("chunk", c)] = ends[("gate", j, m)]
                    c, w = chunk()
                    open_(b + 1, ("branch", j, m))
                    for k in range(4):
                        ins = mm3(bank(b + 1), (w[0][:, k, :], w[1][:, k, :]), (x[0][:, k, :], x[1][:, k, :]),
                                  k == 0, k == 3)
                    close(ins, "merge", ("branch", j, m))
                    ends[("chunk", c)] = ends[("branch", j, m)]

            pe.wait_ge(s["otl"], HEADS)
            merge(0, (o_hi, o_lo))
            phase_end(4)

            pe.wait_ge(s["s5row"], 1)
            open_(0, "s5row")
            for i in range(4):
                ins = pe.transpose(bank(0, NPD, i * NPD), row[:, 8 + i, :], cst[0:NPD, C_ID:C_ID + NPD])
            close(ins, "s5", "s5row")
            pe.wait_ge(ld["s5"], 16 * NS5)
            for part in range(2):
                open_(1 + part, ("ct", part))
                for i in range(4):
                    ins = pe.transpose(bank(1 + part, P, i * P), cld[:, part, i, :], ident)
                close(ins, "s5", ("ct", part))
            for q in range(4):
                pe.wait_ge(s["pm"], 2 * q + 2)
                open_(3, ("K", q))
                for d in range(2):
                    l0 = 0 if d == 0 else 1
                    for j in range(4):
                        o = PS[32 * j:32 * j + 32, 512 * 3 + 128 * d:512 * 3 + 128 * d + 128]
                        pd = 4 * d + j
                        pe.matmul(o, bdr[:, pd, :], clr[:, pd, l0:l0 + 8, :], start=True, stop=False)
                        ins = pe.matmul(o, bdi[:, pd, :], cli[:, pd, l0:l0 + 8, :], start=False, stop=True)
                close(ins, "s5", ("K", q))
                for part, pm in enumerate((pmr, pmi)):
                    for d in range(2):
                        b = 4 + 2 * part + d
                        open_(b, ("WT", q, part, d))
                        for j in range(4):
                            ins = pe.transpose(bank(b, P, j * P), pm[:, 4 * d + j, :], ident)
                        close(ins, "s5", ("WT", q, part, d))
                for part in range(2):
                    for d in range(2):
                        wait(pe, taken[("WT", q, part, d)])
                        b = 4 + 2 * part + d
                        open_(b, ("S", q, part, d))
                        for j in range(4):
                            for g2 in range(2):
                                o = PS[64 * g2:64 * g2 + 64, 512 * b + NCH * j:512 * b + NCH * (j + 1)]
                                c0 = 0 if d == 0 else NCC
                                ins = pe.matmul(o, WT[:, part, 4 * d + j, 64 * g2:64 * g2 + 64],
                                                U[:, 8 * q + 2 * j + g2, c0:c0 + NCH], start=True, stop=True)
                        close(ins, "s5", ("S", q, part, d))
                pe.wait_ge(ld["kread"], 16 * L * (q + 1))
                pe.wait_ge(s["Hs"], 2 * (q + 1))
                for half in range(2):
                    b = 1 + half
                    open_(b, ("Y", q, half))
                    for jj in range(4):
                        gl, j, g2 = 2 * jj + half, jj, half
                        o = PS[0:NCX, 512 * b + P * jj:512 * b + P * (jj + 1)]
                        sl = slice(64 * g2, 64 * g2 + 64)
                        pe.matmul(o, U[:, 8 * q + gl, NCC:NCC + NCX], Mt[:, gl, :], start=True, stop=False)
                        for d in range(2):
                            l0 = 1 if d == 0 else 0
                            for part, cl in enumerate((clr, cli)):
                                ins = pe.matmul(o, H[sl, part, 4 * d + j, :], cl[sl, 4 * d + j, l0:l0 + 8, :],
                                                start=False, stop=(d == 1 and part == 1))
                    close(ins, "s5", ("Y", q, half))
            pe.wait_ge(ld["ytok"], 16 * TT * 4)
            for k in range(4):
                open_(3 + k, ("yT", k))
                for t in range(TT):
                    ins = pe.transpose(bank(3 + k, P, t * P), y5tok[:, t, k * P:(k + 1) * P], ident)
                close(ins, "glu", ("yT", k))
            pe.wait_ge(s["gtl"], 4)
            for m in range(4):
                c, w = chunk()
                b = 7 * (m % 2)
                open_(b, ("glu", m))
                for k in range(4):
                    ins = mm3(bank(b), (w[0][:, k, :], w[1][:, k, :]), (yg_hi[:, k, :], yg_lo[:, k, :]),
                              k == 0, k == 3)
                close(ins, "glu", ("glu", m))
                ends[("chunk", c)] = ends[("glu", m)]
            pe.wait_ge(s["otl"], HEADS + 4)
            merge(1, (o_hi, o_lo))
            ada_part(range(16, 48), 0, "ada1")
            phase_end(5)

            pe.wait_ge(ld["hyp"], 16 * NHYP)
            open_(0, ("hid", 0))
            close(pe.matmul(bank(0)[0:64], w12[0:33, 0, :], zpos[:, :], start=True, stop=True), "hy", ("hid", 0))
            pe.wait_ge(s["hid"], 1)
            open_(0, ("hid", 1))
            close(pe.matmul(bank(0)[0:64], w12[:, 1, :], hid1[:, :], start=True, stop=True), "hy", ("hid", 1))
            pe.wait_ge(s["hid"], 2)
            pe.wait_ge(s["alt"], 2)
            for _ in range(4):
                cc, _w = chunk()
                assert chunks[cc][3] == "const"
            nw = 0
            for half in range(2):
                for part in range(3):
                    for i in range(2):
                        c, w = chunk()
                        b = (2 * part + i) % 4
                        open_(b, ("hz", half, part, i))
                        for k in range(KD):
                            ins = mm3(bank(b), (w[0][:, k, :], w[1][:, k, :]), (h_hi[:, k, :], h_lo[:, k, :]),
                                      k == 0, k == KD - 1)
                        close(ins, "hy", ("hz", half, part, i))
                        ends[("chunk", c)] = ends[("hz", half, part, i)]
                        if part < 2:
                            n = 2 * part + i + 1
                            wait(pe, taken[("hz", half, part, i)])
                            b = 4 + (2 * part + i) % 2
                            open_(b, ("ht", half, part, i))
                            for t in range(TT):
                                ins = pe.transpose(bank(b, P, t * P), tmp[(n - 1) % 2][:, t * P:(t + 1) * P], ident)
                            close(ins, "hy", ("ht", half, part, i))
                for o in range(2):
                    it = 2 * half + o
                    pe.wait_ge(ld["w3"], 16 * (it + 1))
                    for t in range(TT):
                        b = 6 + t % 2
                        open_(b, ("f", half, o, t))
                        close(pe.matmul(bank(b), hid2[:, t * P:(t + 1) * P], w3[:, :, :], start=True, stop=True),
                              "hy", ("f", half, o, t))
                    pe.wait_ge(s["hsl"], TT * (it + 1))
                    for j in range(4):
                        b = j % 4
                        open_(b, ("G", half, o, j))
                        js = slice(j * P, (j + 1) * P)
                        for k in range(TT):
                            mm3(bank(b, HC), (fc_hi[:, k, js], fc_lo[:, k, js]),
                                (y_hi[:, k, 0:HC], y_lo[:, k, 0:HC]), k == 0, k == 3)
                        for k in range(TT):
                            ins = mm3(bank(b, HC, HC), (fs_hi[:, k, js], fs_lo[:, k, js]),
                                      (y_hi[:, k, HC:2 * HC], y_lo[:, k, HC:2 * HC]), k == 0, k == 3)
                        close(ins, "hy", ("G", half, o, j))
                    b = 4
                    open_(b, ("Gn", half, o))
                    for k in range(TT):
                        pe.matmul(bank(b, HC), altr[:, :], y_hi[:, k, 0:HC], start=(k == 0), stop=False)
                        ins = pe.matmul(bank(b, HC), altr[:, :], y_lo[:, k, 0:HC], start=False, stop=(k == 3))
                    close(ins, "hy", ("Gn", half, o))
                    if o == 0:
                        wait(pe, taken[("ht", half, 0, 0)])
                        wait(pe, taken[("ht", half, 0, 1)])
                    else:
                        pe.wait_ge(s["utl"], TT * (half + 1))
                    for j in range(4):
                        b = j % 4
                        open_(b, ("Us", half, o, j))
                        js = slice(j * P, (j + 1) * P)
                        for k in range(TT):
                            mm3(bank(b, HC), (fc_hi[:, k, js], fc_lo[:, k, js]), (u_hi[:, k, :], u_lo[:, k, :]),
                                k == 0, k == 3)
                        for k in range(TT):
                            ins = mm3(bank(b, HC, HC), (fs_hi[:, k, js], fs_lo[:, k, js]),
                                      (u_hi[:, k, :], u_lo[:, k, :]), k == 0, k == 3)
                        close(ins, "hy", ("Us", half, o, j))
                    open_(5, ("Un", half, o))
                    for k in range(TT):
                        pe.matmul(bank(5, HC), altr[:, :], u_hi[:, k, :], start=(k == 0), stop=False)
                        ins = pe.matmul(bank(5, HC), altr[:, :], u_lo[:, k, :], start=False, stop=(k == 3))
                    close(ins, "hy", ("Un", half, o))
                    pe.wait_ge(s["ytl"], 4 * (it + 1))
                    pe.wait_ge(s["nyq"], it + 1)
                    if o == 0:
                        for t in range(TT):
                            b = 6 + t % 2
                            open_(b, ("c1", half, t))
                            ts = slice(t * P, (t + 1) * P)
                            for j in range(4):
                                mm3(bank(b, HC), (fc_hi[:, j, ts], fc_lo[:, j, ts]),
                                    (y_hi[:, j, 0:HC], y_lo[:, j, 0:HC]), j == 0, False)
                                mm3(bank(b, HC), (fs_hi[:, j, ts], fs_lo[:, j, ts]),
                                    (y_hi[:, j, HC:2 * HC], y_lo[:, j, HC:2 * HC]), False, False)
                            pe.matmul(bank(b, HC), alt_row[:, 0:P], nyh[:, :], start=False, stop=False)
                            close(pe.matmul(bank(b, HC), alt_row[:, 0:P], nyl[:, :], start=False, stop=True),
                                  "hy", ("c1", half, t))
                    else:
                        for i in range(2):
                            b = 6 + i
                            open_(b, ("c2", half, i))
                            cs, cs2 = slice(i * P, (i + 1) * P), slice(HC + i * P, HC + (i + 1) * P)
                            for j in range(4):
                                mm3(bank(b), (y_hi[:, j, cs], y_lo[:, j, cs]), (fc_hi[:, j, :], fc_lo[:, j, :]),
                                    j == 0, False)
                                mm3(bank(b), (y_hi[:, j, cs2], y_lo[:, j, cs2]), (fs_hi[:, j, :], fs_lo[:, j, :]),
                                    False, False)
                            pe.matmul(bank(b), nyh[:, cs], alt_row[:, :], start=False, stop=False)
                            close(pe.matmul(bank(b), nyl[:, cs], alt_row[:, :], start=False, stop=True),
                                  "hy", ("c2", half, i))
            pe.wait_ge(s["otl"], HEADS + 8)
            merge(2, (e_hi, e_lo))
            phase_end(6)

            pe.wait_ge(ld["x2"], 16)
            pe.wait_ge(s["ml"], KD)
            for k in range(KD):
                b = 4 + k % 4
                open_(b, ("x2T", k))
                for t in range(TT):
                    ins = pe.transpose(bank(b, P, t * P), x2t[:, t, k * P:(k + 1) * P], ident)
                close(ins, "out", ("x2T", k))

            def square_sum(k):
                if k == 0:
                    open_(4, "ss")
                pe.wait_ge(s["sq2"], k + 1)
                ins = pe.matmul(bank(4), onesq[:, :], sqk[k % 2][:, :], start=(k == 0), stop=(k == KD - 1))
                close(ins, "norm", ("ssk", k))

            for m in range(KD):
                c, w = chunk()
                b = m % 4
                open_(b, ("wo", m))
                for k in range(KD):
                    ins = mm3(bank(b), (w[0][:, k, :], w[1][:, k, :]), (m_hi[:, k, :], m_lo[:, k, :]),
                              k == 0, k == KD - 1)
                close(ins, "out", ("wo", m))
                ends[("chunk", c)] = ends[("wo", m)]
                if m:
                    square_sum(m - 1)
            square_sum(KD - 1)
            ends["ss"] = ends[("ssk", KD - 1)]
            phase_end(7)

            pe.wait_ge(s["h2l"], KD)
            for f in range(FT):
                for u in range(2):
                    c, w = chunk()
                    b = (2 * f + u) % 8
                    open_(b, ("gu", f, u))
                    for k in range(KD):
                        ins = mm3(bank(b), (w[0][:, k, :], w[1][:, k, :]), (h_hi[:, k, :], h_lo[:, k, :]),
                                  k == 0, k == KD - 1)
                    close(ins, "up", ("gu", f, u))
                    ends[("chunk", c)] = ends[("gu", f, u)]
            pe.wait_ge(s["atl"], FT)
            for m in range(KD):
                b = m % 4
                open_(b, ("down", m))
                k0 = 0
                for i, kt in enumerate(DOWN):
                    c, w = chunk()
                    for k in range(kt):
                        ins = mm3(bank(b), (w[0][:, k, :], w[1][:, k, :]),
                                  (act_hi[:, k0 + k, :], act_lo[:, k0 + k, :]), k0 + k == 0, k0 + k == FT - 1)
                    k0 += kt
                    close(ins, "down", ("chunk", c))
                ends[("down", m)] = ends[("chunk", c)]
                if m:
                    to_tokens(m - 1)
            to_tokens(KD - 1)
            assert nxt[0] == len(chunks)

        @block.scalar
        def _(act):
            chain = [0]
            settled = [True]

            def after():
                if not settled[0]:
                    act.drain()
                settled[0] = False
                return act

            at = [0]

            def link(ins):
                chain[0] += 1
                ins.then_inc(s_act, 1)
                act.wait_ge(s_act, chain[0])
                settled[0] = True

            def split_to(c1):
                while at[0] <= min(c1, len(chunks) - 1):
                    c = at[0]
                    at[0] += 1
                    _, kt, n, kind, dest = chunks[c]
                    if kind == "plain":
                        continue
                    i = c % RING
                    act.wait_ge(raw_in[i], 16 * (c // RING + 1))
                    if kind == "const":
                        o = dest[0]
                    else:
                        o = whi[i][:, 0:kt * n]
                        if c >= RING and chunks[c - RING][3] != "const":
                            wait(act, ends[("chunk", c - RING)])
                    after().activation(o, raw[i][:, 0:kt * n], ACT.Copy).then_inc(s_hi, 1)

            def phase_end(k):
                act.drain().then_inc(s_phase, 1)
                act.wait_ge(s_phase, 3 * k)

            def copy(o, i):
                return after().activation(o, i, ACT.Copy)

            act.wait_ge(s["vc"], 1)
            after().activation(silc[:, :], vc1[:, 0:16], ACT.Silu).then_inc(s["silu"], 1)
            act.wait_ge(ld["x"], 16)
            act.wait_ge(ld["ctx"], 16)
            for t in range(KT):
                link(after().activation(sq0[:, :], xt[:, t, :], ACT.Square, accum_out=rs[:, 0, 0, t:t + 1]))
            act.drain().then_inc(s["sq"], 1)
            act.wait_ge(s["var"], 1)
            after().activation(rs[:, 0, 2, 0:KT], rs[:, 0, 1, 0:KT], ACT.Sqrt).then_inc(s["sqrt"], 1)
            split_to(19)
            for j in range(2 * KD):
                k, x = j // 2, j % 2
                act.wait_ge(s["htmp"], j + 1)
                o = hc_hi[:, k, :] if x else h_hi[:, k, :]
                copy(o, tmp[j % 2][:, 0:TC if x else T]).then_inc(s["hth"], 1)
            split_to(22)
            for t in range(KT):
                wait(act, ends[("us", t)])
                copy(us[:, t, :], bank(t)).then_inc(bank_free[t], 1)
            act.wait_ge(ld["uch"], 16 * KT)
            copy(uch2[:, :, :, :], uch[:, :, :].rearrange("c s (g m) -> c g s m", g=G)).then_inc(s["us"], 1)
            split_to(23)
            for t in range(KT):
                wait(act, ends[("z", t)])
                if t < TT:
                    link(after().activation(sq1[:, :], bank(t, QL), ACT.Square, accum_out=rs[:, 1, 0, t:t + 1]))
                link(after().activation(sq1[:, 0:KVL], bank(t, KVL, QL), ACT.Square,
                                    accum_out=rs[:, 1, 0, TT + t:TT + t + 1]))
                act.drain().then_inc(s["sq"], 1)
            act.wait_ge(s["var"], 2)
            after().activation(rs[:, 1, 2, 0:10], rs[:, 1, 1, 0:10], ACT.Sqrt).then_inc(s["sqrt"], 1)
            for i in range(8):
                b = 6 + i % 2
                wait(act, ends[("uT", i)])
                src = bank(b, 4 * NCH).rearrange("p (g c) -> p g c", g=4)
                gs = slice(4 * i, 4 * i + 4)
                copy(U[:, gs, NCC:NCC + NCX], src[:, :, 0:NCX])
                copy(U[:, gs, 0:NCC], src[:, :, NCX:NCH])
                copy(U[:, gs, NCC + NCX:P], src[:, :, NCX:NCH]).then_inc(bank_free[b], 1)
            phase_end(1)
            split_to(26)
            for i in range(4):
                act.wait_ge(s["ntmp"], i + 1)
                o = (qnT_hi[:, 0, :], qnT_hi[:, 1, :], kvT_hi[:, 0:T], kvT_hi[:, T:KEYS])[i]
                copy(o, tmp[i % 2][:, 0:TC if i == 3 else T]).then_inc(s["nth"], 1)
            phase_end(2)

            split_to(29)
            for part, (k0, n) in enumerate(((0, T), (T, TC))):
                wait(act, ends[("kr", part)])
                copy(kT_hi[NOPE:QK, k0:k0 + n], bank(part, n)[0:ROPE]).then_inc(s["aqk"], 1)
            for h in range(HEADS):
                wait(act, ends[("qT", h)])
                copy(qT_hi[:, :], bank(0)[0:QK]).then_inc(s["aqk"], 1)
                for part, (k0, n) in enumerate(((0, T), (T, TC))):
                    wait(act, ends[("k", h, part)])
                    copy(kT_hi[0:NOPE, k0:k0 + n], bank(1 + part, n)[0:NOPE]).then_inc(s["aqk"], 1)
                wait(act, ends[("v", h)])
                copy(v_hi[:, :, 0:VD], bank(3, KT * VD).rearrange("p (k v) -> p k v", k=KT)).then_inc(s["aqk"], 1)
                for t in range(TT):
                    i = TT * h + t
                    act.wait_ge(s["max"], i + 1)
                    after().activation(prob[:, t, :], bank(4 + 2 * (t % 2), KEYS), ACT.Exp, bias=mx[:, 2 * i + 1:2 * i + 2],
                                   scale=SCALE).then_inc(bank_free[4 + 2 * (t % 2)], 1)
                for kt in range(KT):
                    wait(act, ends[("pT", h, kt)])
                    o = pTa_hi[:, kt, :] if kt < 4 else pTb_hi[:, kt - 4, :]
                    copy(o, bank(kt % 3)).then_inc(s["pTh"], 1)
                rows = slice(64 * (h % 2), 64 * (h % 2) + 64)
                act.wait_ge(s["oun"], h + 1)
                copy(o_hi[rows, h // 2, :], tmp[2][rows, :]).then_inc(s["oth"], 1)
            phase_end(3)

            def merge(j, c0):
                for m in range(KD):
                    split_to(c0 + 2 * m + 3)
                    wait(act, ends[("gate", j, m)])
                    if m >= 2:
                        wait(act, taken[("branch", j, m - 2)])
                    after().activation(tmp[m % 2][:, :], bank(2 * (m % 4)), ACT.Sigmoid).then_inc(bank_free[2 * (m % 4)], 1)

            merge(0, 27)
            phase_end(4)

            act.wait_ge(ld["s5"], 16 * NS5)
            after().activation(dt2[:, :], dt2[:, :], ACT.Exp).then_inc(s["s5c"], 1)
            act.wait_ge(s["s5a"], 1)
            link(after().activation(row[:, 6, :], row[:, 8, :], ACT.Exp))
            link(after().activation(row[:, 7, :], row[:, 9, :], ACT.Sin))
            after().activation(row[:, 5, :], row[:, 5, :], ACT.Sin).then_inc(s["s5c"], 1)
            for part, dst in enumerate((ctr, cti)):
                wait(act, ends[("ct", part)])
                copy(dst[:, :, :].rearrange("p a n -> p (a n)"), bank(1 + part)).then_inc(bank_free[1 + part], 1)
            act.wait_ge(s["s5a"], 2)
            link(after().activation(lt[:, 2, :], lt[:, 2, :], ACT.Exp))
            link(after().activation(lt[:, 0, :], lt[:, 0, :], ACT.Sin))
            after().activation(lt[:, 1, :], lt[:, 1, :], ACT.Sin).then_inc(s["s5c"], 1)
            for q in range(4):
                for d in range(2):
                    act.wait_ge(s["angle"], 2 * q + d + 1)
                    ds = slice(4 * d, 4 * d + 4)
                    after().activation(tsin[:, ds, :], gr[:, ds, :], ACT.Sin)
                    after().activation(tcos[:, ds, :], gi[:, ds, :], ACT.Sin).then_inc(s["trig"], 1)
                for part in range(2):
                    for d in range(2):
                        b = 4 + 2 * part + d
                        wait(act, ends[("WT", q, part, d)])
                        copy(WT[:, part, 4 * d:4 * d + 4, :].rearrange("p a n -> p (a n)"), bank(b))\
                            .then_inc(bank_free[b], 1)
                for half in range(2):
                    wait(act, ends[("Y", q, half)])
                    if half == 0 and q:
                        act.wait_ge(ld["ytok"], 16 * TT * q)
                    src = bank(1 + half)[0:NCX].rearrange("c (g t n) -> c g t n", g=4, t=L)
                    o = Y2[:, :, :].rearrange("c t (g two n) -> c two g t n", g=4, two=2)[:, half]
                    for g in range(4):
                        ins = copy(o[:, g], src[:, g])
                    ins.then_inc(bank_free[1 + half], 1)
            for k in range(4):
                wait(act, ends[("yT", k)])
                after().activation(yg[:, k, :], bank(3 + k), ACT.Gelu_apprx_tanh).then_inc(bank_free[3 + k], 1)
                wait(act, taken[("yT", k)])
                copy(yg_hi[:, k, :], yg[:, k, :]).then_inc(s["gth"], 1)
            split_to(46)
            for m in range(4):
                wait(act, ends[("glu", m)])
                after().activation(tmp[m % 2][:, :], bank(7 * (m % 2)), ACT.Sigmoid).then_inc(bank_free[7 * (m % 2)], 1)
                act.wait_ge(s["oun"], HEADS + m + 1)
                copy(o_hi[:, m, :], yg[:, m, :]).then_inc(s["oth"], 1)
            merge(1, 47)
            split_to(62)
            phase_end(5)

            for i in range(2):
                act.wait_ge(s["hya"], i + 1)
                after().activation((hid1, hid2)[i][:, :], harg[:, :], ACT.Sin).then_inc(s["hid"], 1)
            split_to(98)
            c = 99
            for half in range(2):
                for part in range(3):
                    for i in range(2):
                        split_to(c + 2)
                        c += 1
                        ct = 4 * part + 2 * half + i
                        n = 2 * part + i
                        wait(act, ends[("hz", half, part, i)])
                        if part < 2 and n >= 2:
                            wait(act, ends[("ht", half, (n - 2) // 2, n % 2)])
                        o = tmp[n % 2][:, :] if part < 2 else g2c[:, i, :]
                        after().activation(o, bank(n % 4), ACT.Identity, scale=vc2[:, 12 + ct:13 + ct],
                                       bias=vc1[:, VOFF["hy_conv_b"] + ct:VOFF["hy_conv_b"] + ct + 1])\
                            .then_inc(s["zc"], 1)
                        if part < 2:
                            wait(act, ends[("ht", half, part, i)])
                            b = 4 + n % 2
                            src = bank(b).rearrange("p (t c) -> p t c", t=TT)
                            cs = slice(i * P, (i + 1) * P)
                            if part == 0:
                                copy(u_hi[:, :, cs], src).then_inc(s["zt"], 1)
                            else:
                                copy(g1t[:, :, cs], src).then_inc(bank_free[b], 1)
                for o in range(2):
                    it = 2 * half + o
                    for t in range(TT):
                        act.wait_ge(s["hs"], TT * it + t + 1)
                        copy(y_hi[:, t, :], tmp[2][:, :]).then_inc(s["hsh"], 1)
                    for j in range(4):
                        wait(act, ends[("G", half, o, j)])
                        after().activation(Gs[:, j, :], bank(j), ACT.Identity, scale=cst[:, C_GS + j:C_GS + j + 1])\
                            .then_inc(bank_free[j], 1)
                    for j in range(4):
                        act.wait_ge(s["yt"], 4 * it + j + 1)
                        copy(y_hi[:, j, :], tmp[2][:, :]).then_inc(s["yth"], 1)
                    if o == 0:
                        for t in range(TT):
                            act.wait_ge(s["ut"], TT * half + t + 1)
                            copy(u_hi[:, t, :], tmp[t % 2][:, 0:HC]).then_inc(s["uth"], 1)
                    else:
                        for i in range(2):
                            act.wait_ge(s["oun"], HEADS + 4 + 2 * half + i + 1)
                            copy(e_hi[:, 2 * half + i, :], tmp[i][:, :]).then_inc(s["oth"], 1)
            merge(2, 111)
            phase_end(6)

            for k in range(KD):
                copy(m_hi[:, k, :], merged[:, k, :]).then_inc(s["mh"], 1)
            for k in range(KD):
                wait(act, ends[("x2T", k)])
                copy(xT[:, k, :], bank(4 + k % 4)).then_inc(bank_free[4 + k % 4], 1)
            for m in range(KD):
                split_to(127 + m + 2)
                wait(act, taken[("wo", m)])
                if m >= 2:
                    wait(act, ends[("ssk", m - 2)])
                after().activation(sqk[m % 2][:, :], xT[:, m, :], ACT.Square).then_inc(s["sq2"], 1)
            act.wait_ge(s["vf"], 1)
            after().activation(srow[:, :], vrow[:, :], ACT.Sqrt).then_inc(s["sf"], 1)
            for k in range(KD):
                act.wait_ge(s["h2t"], k + 1)
                copy(h_hi[:, k, :], tmp[k % 2][:, :]).then_inc(s["h2h"], 1)
            phase_end(7)

            for f in range(FT):
                split_to(135 + 2 * f + 3)
                wait(act, ends[("gu", f, 0)])
                if f >= 3:
                    act.wait_ge(s["atl"], f - 2)
                after().activation(tmp[f % 3][:, :], bank((2 * f) % 8), ACT.Silu).then_inc(bank_free[(2 * f) % 8], 1)
                wait(act, taken[("gu", f, 1)])
                copy(act_hi[:, f, :], tmp[f % 3][:, :]).then_inc(s["ath"], 1)
            for m in range(KD):
                split_to(179 + 4 * m + 6)
                if m:
                    wait(act, ends[("yo", m - 1)])
                    copy(ytok[:, :, (m - 1) * P:m * P], bank(4 + (m - 1) % 4).rearrange("p (t c) -> p t c", t=TT))\
                        .then_inc(bank_free[4 + (m - 1) % 4], 1)
            wait(act, ends[("yo", KD - 1)])
            copy(ytok[:, :, D - P:D], bank(7).rearrange("p (t c) -> p t c", t=TT)).then_inc(bank_free[7], 1)
            wait(act, taken[("yo", KD - 1)])
            for t in range(TT):
                link(after().activation(fsq[:, :], ytok[:, t, :], ACT.Square, accum_out=rs[:, 2, 0, t:t + 1]))
            act.drain().then_inc(s["sq"], 1)
            act.wait_ge(s["var"], 3)
            after().activation(rs[:, 2, 2, 0:TT], rs[:, 2, 1, 0:TT], ACT.Sqrt).then_inc(s["sqrt"], 1)

        @block.vector
        def _(dve):
            chain = [0]
            settled = [True]

            def after():
                if not settled[0]:
                    dve.drain()
                settled[0] = False
                return dve

            at = [0]

            def link(ins):
                chain[0] += 1
                ins.then_inc(s_dve, 1)
                dve.wait_ge(s_dve, chain[0])
                settled[0] = True

            def tt(o, x, y, op):
                return after().tensor_tensor(o, x, y, op)

            def low(o, x, hi_):
                return after().tensor_tensor(o, x, hi_.bitcast(F32), ALU.subtract)

            def split_to(c1):
                while at[0] <= min(c1, len(chunks) - 1):
                    c = at[0]
                    at[0] += 1
                    _, kt, n, kind, dest = chunks[c]
                    if kind == "plain":
                        continue
                    i = c % RING
                    dve.wait_ge(s_hi, nth_split[c] + 1)
                    o, hi_ = (dest[1], dest[0]) if kind == "const" else (wlo[i][:, 0:kt * n], whi[i][:, 0:kt * n])
                    low(o, raw[i][:, 0:kt * n], hi_).then_inc(s_lo, 1)

            def phase_end(k):
                dve.drain().then_inc(s_phase, 1)
                dve.wait_ge(s_phase, 3 * k)

            def refine(v, sq, r_, t_, o):
                link(after().reciprocal(r_, sq))
                link(tt(t_, r_, r_, ALU.mult))
                link(tt(t_, t_, v, ALU.mult))
                link(after().tensor_scalar(t_, t_, -0.5, 1.5, ALU.mult, ALU.add))
                link(tt(o, r_, t_, ALU.mult))

            def reduce_angle(v, n):
                link(after().tensor_scalar(n, v, INV_2PI, ROUND, ALU.mult, ALU.add))
                link(after().tensor_scalar(n, n, ROUND, None, ALU.subtract))
                link(after().scalar_tensor_tensor(v, n, -TWO_PI_HI, v, ALU.mult, ALU.add))
                link(after().scalar_tensor_tensor(v, n, -TWO_PI_LO, v, ALU.mult, ALU.add))
                link(after().tensor_scalar(v, v, PI, -PI, ALU.min, ALU.max))

            wait(dve, ends["vec"])
            after().tensor_copy(vc1[:, :], bank(0, VROWS)).then_inc(s["vc"], 1)
            after().tensor_copy(vc2[:, :], bank(0, 36, 128))
            after().tensor_copy(vc3[:, :], bank(0, 3, 256)[0:64]).then_inc(bank_free[0], 1)
            dve.wait_ge(s["sq"], 1)
            link(after().tensor_scalar(rs[:, 0, 1, 0:KT], rs[:, 0, 0, 0:KT], 1.0 / D, EPS, ALU.mult, ALU.add))
            dve.drain().then_inc(s["var"], 1)
            dve.wait_ge(s["sqrt"], 1)
            refine(rs[:, 0, 1, 0:KT], rs[:, 0, 2, 0:KT], rs[:, 0, 3, 0:KT], rs[:, 0, 4, 0:KT], rs[:, 0, 5, 0:KT])
            for t in range(KT):
                after().tensor_scalar(xt[:, t, :], xt[:, t, :], rs[:, 0, 5, t:t + 1], None, ALU.mult).then_inc(s["xh"], 1)
            wait(dve, ends["ada0"])
            dve.wait_ge(s["vc"], 1)
            pv = bank(1, 32).rearrange("p (m x) -> p m x", x=2)
            ab = vc1[:, VOFF["ada_b"]:VOFF["ada_b"] + 48]
            nm = vc1[:, VOFF["norm_mix"]:VOFF["norm_mix"] + KD]
            link(tt(modx[:, 0:16], pv[:, :, 0], ab[:, 0:16], ALU.add))
            tt(modc[:, :], pv[:, :, 1], ab[:, 0:16], ALU.add).then_inc(bank_free[1], 1)
            wait(dve, taken["ada0"])
            after().scalar_tensor_tensor(amix[:, 0, :], modx[:, 8:16], 1.0, nm, ALU.add, ALU.mult)
            link(after().scalar_tensor_tensor(amix[:, 1, :], modc[:, 8:16], 1.0, nm, ALU.add, ALU.mult))
            split_to(18)

            def low_h(j):
                k, x = j // 2, j % 2
                dve.wait_ge(s["hth"], j + 1)
                n = TC if x else T
                low((hc_lo if x else h_lo)[:, k, :], tmp[j % 2][:, 0:n], (hc_hi if x else h_hi)[:, k, :])\
                    .then_inc(s["htl"], 1)

            for j in range(2 * KD):
                k, x = j // 2, j % 2
                n = TC if x else T
                b = (5 if x else 2) + k % 3
                wait(dve, ends[("xT", k, x)])
                after().tensor_scalar(tmp[j % 2][:, 0:n], bank(b, n), amix[:, x, k:k + 1],
                                  (modc if x else modx)[:, k:k + 1], ALU.mult, ALU.add).then_inc(bank_free[b], 1)
                wait(dve, taken[("xT", k, x)])
                dve.drain().then_inc(s["htmp"], 1)
                if j:
                    low_h(j - 1)
            low_h(2 * KD - 1)
            split_to(23)
            for t in range(KT):
                dve.wait_ge(s["sq"], t + 2)
                o = 0 if t < TT else 256
                after().tensor_copy(ztok[:, t, o:416], bank(t, 416 - o, o)).then_inc(bank_free[t], 1)
            link(after().tensor_scalar(rs[:, 1, 1, 0:TT], rs[:, 1, 0, 0:TT], 1.0 / QL, EPS, ALU.mult, ALU.add))
            link(after().tensor_scalar(rs[:, 1, 1, TT:10], rs[:, 1, 0, TT:10], 1.0 / KVL, EPS, ALU.mult, ALU.add))
            dve.drain().then_inc(s["var"], 1)
            dve.wait_ge(s["sqrt"], 2)
            refine(rs[:, 1, 1, 0:10], rs[:, 1, 2, 0:10], rs[:, 1, 3, 0:10], rs[:, 1, 4, 0:10], rs[:, 1, 5, 0:10])
            for t in range(KT):
                wait(dve, taken[("z", t)])
                if t < TT:
                    after().tensor_scalar(ztok[:, t, 0:QL], ztok[:, t, 0:QL], rs[:, 1, 5, t:t + 1], None, ALU.mult)
                after().tensor_scalar(ztok[:, t, QL:QL + KVL], ztok[:, t, QL:QL + KVL],
                                  rs[:, 1, 5, TT + t:TT + t + 1], None, ALU.mult).then_inc(s["zn"], 1)
            phase_end(1)
            split_to(26)

            def low_n(i):
                dve.wait_ge(s["nth"], i + 1)
                o, hi_ = ((qnT_lo[:, 0, :], qnT_hi[:, 0, :]), (qnT_lo[:, 1, :], qnT_hi[:, 1, :]),
                          (kvT_lo[:, 0:T], kvT_hi[:, 0:T]), (kvT_lo[:, T:KEYS], kvT_hi[:, T:KEYS]))[i]
                low(o, tmp[i % 2][:, 0:TC if i == 3 else T], hi_).then_inc(s["ntl"], 1)

            for i in range(4):
                n = TC if i == 3 else T
                col = VOFF["mla_q_norm"] + i if i < 2 else VOFF["mla_kv_norm"]
                wait(dve, ends[("nT", i)])
                after().tensor_scalar(tmp[i % 2][:, 0:n], bank(i, n), vc1[:, col:col + 1], None, ALU.mult)\
                    .then_inc(bank_free[i], 1)
                wait(dve, taken[("nT", i)])
                dve.drain().then_inc(s["ntmp"], 1)
                if i:
                    low_n(i - 1)
            low_n(3)

            def rotate(x1, x2, cos, sin, o1, o2, shape):
                r_ = [rt[:, i, 0:shape[1], :] for i in range(4)]
                tt(r_[0], x1, cos, ALU.mult)
                tt(r_[1], x2, sin, ALU.mult)
                tt(r_[2], x1, sin, ALU.mult)
                link(tt(r_[3], x2, cos, ALU.mult))
                tt(o1, r_[0], r_[1], ALU.subtract)
                return tt(o2, r_[2], r_[3], ALU.add)

            dve.wait_ge(ld["rope"], 16)
            for t in range(KT):
                kr = ztok[:, t, 384:416]
                if t < TT:
                    c_, s_ = rope[:, t, 0:1, :], rope[:, t, 1:2, :]
                    k1, k2 = kr[:, 0::2].unsqueeze(1), kr[:, 1::2].unsqueeze(1)
                    o = krtok[:, t, :]
                    link(rotate(k1, k2, c_, s_, o[:, 0::2].unsqueeze(1), o[:, 1::2].unsqueeze(1), (P, 1)))
                else:
                    after().tensor_copy(krtok[:, t, :], kr)
            for t in range(TT):
                for hf in range(2):
                    b = 4 + (2 * t + hf) % 4
                    wait(dve, ends[("q", t, hf)])
                    after().tensor_copy(qtok[:, t, 4 * hf:4 * hf + 4, :].rearrange("p h d -> p (h d)"), bank(b, 384))\
                        .then_inc(bank_free[b], 1)
                    wait(dve, taken[("q", t, hf)])
                q = qtok[:, t, :, NOPE:QK]
                c_ = rope[:, t, 0:1, :].to_broadcast([P, HEADS, 16])
                s_ = rope[:, t, 1:2, :].to_broadcast([P, HEADS, 16])
                link(rotate(q[:, :, 0::2], q[:, :, 1::2], c_, s_, q[:, :, 0::2], q[:, :, 1::2], (P, HEADS)))
            phase_end(2)

            split_to(29)
            after().memset(v_hi[:, :, VD:P].bitcast(F32), 1.0).then_inc(s["vones"], 1)
            after().memset(v_lo[:, :, VD:P].bitcast(F32), 0.0).then_inc(s["vones"], 1)
            for part, (k0, n) in enumerate(((0, T), (T, TC))):
                dve.wait_ge(s["aqk"], part + 1)
                low(kT_lo[NOPE:QK, k0:k0 + n], bank(part, n)[0:ROPE], kT_hi[NOPE:QK, k0:k0 + n])\
                    .then_inc(bank_free[part], 1)
            for h in range(HEADS):
                dve.wait_ge(s["aqk"], 3 + 4 * h)
                low(qT_lo[:, :], bank(0)[0:QK], qT_hi[:, :]).then_inc(bank_free[0], 1)
                for part, (k0, n) in enumerate(((0, T), (T, TC))):
                    dve.wait_ge(s["aqk"], 4 + 4 * h + part)
                    low(kT_lo[0:NOPE, k0:k0 + n], bank(1 + part, n)[0:NOPE], kT_hi[0:NOPE, k0:k0 + n])\
                        .then_inc(bank_free[1 + part], 1)
                dve.wait_ge(s["aqk"], 6 + 4 * h)
                low(v_lo[:, :, 0:VD], bank(3, KT * VD).rearrange("p (k v) -> p k v", k=KT), v_hi[:, :, 0:VD])\
                    .then_inc(bank_free[3], 1)
                for t in range(TT):
                    i = TT * h + t
                    wait(dve, ends[("s", h, t)])
                    link(after().tensor_reduce(mx[:, 2 * i:2 * i + 1], bank(4 + 2 * (t % 2), KEYS), AX.X, ALU.max))
                    after().tensor_scalar(mx[:, 2 * i + 1:2 * i + 2], mx[:, 2 * i:2 * i + 1], -SCALE, None, ALU.mult)\
                        .then_inc(s["max"], 1)
                for kt in range(KT):
                    dve.wait_ge(s["pTh"], KT * h + kt + 1)
                    hi_, lo_ = (pTa_hi, pTa_lo) if kt < 4 else (pTb_hi, pTb_lo)
                    low(lo_[:, kt % 4, :], bank(kt % 3), hi_[:, kt % 4, :]).then_inc(bank_free[kt % 3], 1)
                rows = slice(64 * (h % 2), 64 * (h % 2) + 64)
                wait(dve, ends[("o", h)])
                link(after().reciprocal(tmp[0][0:64, :], bank(3)[64:128]))
                tt(tmp[2][rows, :], bank(3)[0:64], tmp[0][0:64, :], ALU.mult).then_inc(bank_free[3], 1)
                wait(dve, taken[("o", h)])
                dve.drain().then_inc(s["oun"], 1)
                dve.wait_ge(s["oth"], h + 1)
                low(o_lo[rows, h // 2, :], tmp[2][rows, :], o_hi[rows, h // 2, :]).then_inc(s["otl"], 1)
            phase_end(3)

            def merge(j, c0):
                for m in range(KD):
                    split_to(c0 + 2 * m + 3)
                    b = 2 * (m % 4)
                    wait(dve, ends[("branch", j, m)])
                    wait(dve, taken[("gate", j, m)])
                    if j == 0:
                        tt(merged[:, m, :], bank(b + 1), tmp[m % 2][:, :], ALU.mult).then_inc(bank_free[b + 1], 1)
                    else:
                        tt(tmp[2][:, :], bank(b + 1), tmp[m % 2][:, :], ALU.mult).then_inc(bank_free[b + 1], 1)
                        wait(dve, taken[("branch", j, m)])
                        link(tt(merged[:, m, :], merged[:, m, :], tmp[2][:, :], ALU.add))

            merge(0, 27)
            phase_end(4)

            dve.wait_ge(ld["s5"], 16 * NS5)
            dve.wait_ge(s["s5c"], 1)

            def R(i):
                return row[:, i, :]

            dtb = dt2[:, :].unsqueeze(2).to_broadcast([NPD, 2, 64])
            link(tt(R(8).rearrange("r (g p) -> r g p", g=2), R(0).rearrange("r (g p) -> r g p", g=2), dtb, ALU.mult))
            link(tt(R(9).rearrange("r (g p) -> r g p", g=2), R(1).rearrange("r (g p) -> r g p", g=2), dtb, ALU.mult))
            reduce_angle(R(9), R(4))
            link(after().tensor_scalar(R(5), R(9), PI / 2, None, ALU.add))
            reduce_angle(R(5), R(4))
            dve.drain().then_inc(s["s5a"], 1)
            link(tt(R(2), R(0), R(0), ALU.mult))
            link(tt(R(3), R(1), R(1), ALU.mult))
            link(tt(R(2), R(2), R(3), ALU.add))
            link(after().reciprocal(R(3), R(2)))
            dve.wait_ge(s["s5c"], 2)
            link(tt(R(5), R(6), R(5), ALU.mult))
            link(after().tensor_scalar(R(5), R(5), 1.0, None, ALU.subtract))
            link(tt(R(6), R(6), R(7), ALU.mult))
            link(tt(R(2), R(5), R(0), ALU.mult))
            link(tt(R(4), R(6), R(1), ALU.mult))
            link(tt(R(2), R(2), R(4), ALU.add))
            link(tt(R(10), R(2), R(3), ALU.mult))
            link(tt(R(2), R(6), R(0), ALU.mult))
            link(tt(R(4), R(5), R(1), ALU.mult))
            link(tt(R(2), R(2), R(4), ALU.subtract))
            link(tt(R(11), R(2), R(3), ALU.mult))
            dve.drain().then_inc(s["s5row"], 1)
            wait(dve, ends["s5row"])
            after().tensor_copy(base4[:, :, :].rearrange("p a n -> p (a n)"), bank(0, 4 * NPD)).then_inc(bank_free[0], 1)
            wait(dve, taken["s5row"])
            e9 = cst[:, C_E9:C_E9 + 9].unsqueeze(1).to_broadcast([P, NPD, 9])

            def v9(i):
                return lt[:, i, :].rearrange("p (a e) -> p a e", e=9)

            def b9(x):
                return x.unsqueeze(2).to_broadcast([P, NPD, 9])

            link(tt(v9(2), b9(base4[:, 0, :]), e9, ALU.mult))
            link(tt(v9(0), b9(base4[:, 1, :]), e9, ALU.mult))
            reduce_angle(lt[:, 0, :], lt[:, 3, :])
            link(after().tensor_copy(th8[:, :], v9(0)[:, :, 8]))
            link(after().tensor_scalar(lt[:, 1, :], lt[:, 0, :], PI / 2, None, ALU.add))
            reduce_angle(lt[:, 1, :], lt[:, 3, :])
            dve.drain().then_inc(s["s5a"], 1)
            dve.wait_ge(s["s5c"], 3)
            tt(lpr[:, :, :], v9(2), v9(1), ALU.mult)
            tt(lpi[:, :, :], v9(2), v9(0), ALU.mult)
            link(after().tensor_copy(rho8[:, :], v9(2)[:, :, 8]))
            w1_, w2_ = (tmp[i][:, 0:NPD * GC].rearrange("p (a n) -> p a n", n=GC) for i in range(2))

            def b16(x):
                return x.unsqueeze(2).to_broadcast([P, NPD, GC])

            cr_, ci_ = b16(base4[:, 2, :]), b16(base4[:, 3, :])
            link(tt(w1_, cr_, bld[:, 0], ALU.mult))
            link(tt(w2_, ci_, bld[:, 1], ALU.mult))
            link(tt(bbr[:, :, :], w1_, w2_, ALU.subtract))
            link(tt(w1_, cr_, bld[:, 1], ALU.mult))
            link(tt(w2_, ci_, bld[:, 0], ALU.mult))
            link(tt(bbi[:, :, :], w1_, w2_, ALU.add))
            wait(dve, taken[("ct", 0)])
            wait(dve, taken[("ct", 1)])
            link(after().memset(bdr[:, :, :], 0.0))
            link(after().memset(bdi[:, :, :], 0.0))
            for q in range(4):
                if q:
                    wait(dve, ends[("Y", q - 1, 1)])
                for d in range(2):
                    gl = slice(16 * d + 4 * q, 16 * d + 4 * q + 4)
                    ds = slice(4 * d, 4 * d + 4)
                    kb = cst[:, C_K:C_K + NCH].unsqueeze(1).to_broadcast([P, 4, NCH])
                    tb = th8[:, gl].unsqueeze(2).to_broadcast([P, 4, NCH])
                    n = t5[0][:, 0:4 * NCH]
                    A, B = (x[:, ds, :].rearrange("p a c -> p (a c)") for x in (gr, gi))
                    link(tt(gr[:, ds, :], tb, kb, ALU.mult))
                    reduce_angle(A, n)
                    link(after().tensor_scalar(B, A, PI / 2, None, ALU.add))
                    reduce_angle(B, n)
                    dve.drain().then_inc(s["angle"], 1)
                    sl = slice(7, None, -1) if d == 0 else slice(0, 8)
                    sh = [P, 4, 8, GC]
                    pr = lpr[:, gl, sl].unsqueeze(3).to_broadcast(sh)
                    pi = lpi[:, gl, sl].unsqueeze(3).to_broadcast(sh)
                    br = bbr[:, gl, :].unsqueeze(2).to_broadcast(sh)
                    bi = bbi[:, gl, :].unsqueeze(2).to_broadcast(sh)
                    x0, x1 = (t[:, 0:512].rearrange("p (a e n) -> p a e n", a=4, e=8) for t in t5)
                    o_r, o_i = (x[:, ds, :].rearrange("p a (e n) -> p a e n", e=8) for x in (pmr, pmi))
                    link(tt(x0, pr, br, ALU.mult))
                    link(tt(x1, pi, bi, ALU.mult))
                    link(tt(pmr[:, ds, :].rearrange("p a m -> p (a m)"), t5[0][:, 0:512], t5[1][:, 0:512], ALU.subtract))
                    link(tt(x0, pr, bi, ALU.mult))
                    link(tt(x1, pi, br, ALU.mult))
                    link(tt(pmi[:, ds, :].rearrange("p a m -> p (a m)"), t5[0][:, 0:512], t5[1][:, 0:512], ALU.add))
                    sl = slice(0, 9) if d == 0 else slice(None, None, -1)
                    sh = [P, 4, 9, GC]
                    pr = lpr[:, gl, sl].unsqueeze(3).to_broadcast(sh)
                    pi = lpi[:, gl, sl].unsqueeze(3).to_broadcast(sh)
                    cr = ctr[:, gl, :].unsqueeze(2).to_broadcast(sh)
                    ci = cti[:, gl, :].unsqueeze(2).to_broadcast(sh)
                    x0, x1 = (t[:, :].rearrange("p (a e n) -> p a e n", a=4, e=9) for t in t5)
                    link(tt(x0, pr, cr, ALU.mult))
                    link(tt(x1, pi, ci, ALU.mult))
                    link(tt(clr[:, ds].rearrange("p a e n -> p (a e n)"), t5[0][:, :], t5[1][:, :], ALU.subtract))
                    link(tt(x0, pr, ci, ALU.mult))
                    link(tt(x1, pi, cr, ALU.mult))
                    link(after().scalar_tensor_tensor(cli[:, ds].rearrange("p a e n -> p (a e n)"), t5[0][:, :], -1.0,
                                                  t5[1][:, :], ALU.mult, ALU.subtract))
                    for dst, src in ((bdr, bbr), (bdi, bbi)):
                        after().tensor_copy(dst[0:64, ds, 0:GC], src[0:64, gl, :])
                        link(after().tensor_copy(dst[64:P, ds, GC:2 * GC], src[64:P, gl, :]))
                    dve.drain().then_inc(s["pm"], 1)
                wait(dve, ends[("K", q)])
                if q:
                    dve.wait_ge(ld["kfilt"], 16 * q)
                kf = bank(3, 128).rearrange("p (l n) -> p l n", n=GC)
                kb_ = bank(3, 128, 128).rearrange("p (l n) -> p l n", n=GC)
                dcol = VOFF["s5_d"] + q
                link(after().scalar_tensor_tensor(K2[:, 7, :], cst[:, C_EYE16:C_EYE16 + GC], vc1[:, dcol:dcol + 1],
                                              kf[:, 0, :], ALU.mult, ALU.add))
                link(tt(K2[:, 7, :], kb_[:, 7, :], K2[:, 7, :], ALU.add))
                after().tensor_copy(K2[:, 0:7, :], kb_[:, 0:7, :])
                after().tensor_copy(K2[:, 8:15, :], kf[:, 1:8, :]).then_inc(bank_free[3], 1)
                for d in range(2):
                    gl0 = 16 * d + 4 * q
                    ds = slice(4 * d, 4 * d + 4)
                    wait(dve, ends[("S", q, 1, d)])
                    dve.wait_ge(s["trig"], 2 * q + d + 1)
                    sr, si = (bank(4 + 2 * p_ + d, 4 * NCH).rearrange("p (a c) -> p a c", a=4) for p_ in range(2))
                    if d:
                        sr, si = sr[:, :, ::-1], si[:, :, ::-1]
                    x0, x1 = (t[:, 0:4 * NCH].rearrange("p (a c) -> p a c", a=4) for t in t5)
                    tc_, ts_ = tcos[:, ds, :], tsin[:, ds, :]
                    link(tt(x0, sr, tc_, ALU.mult))
                    link(tt(x1, si, ts_, ALU.mult))
                    link(tt(gr[:, ds, :], x0, x1, ALU.add))
                    tt(x0, si, tc_, ALU.mult).then_inc(bank_free[6 + d], 1)
                    tt(x1, sr, ts_, ALU.mult).then_inc(bank_free[4 + d], 1)
                    wait(dve, taken[("S", q, 0, d)])
                    wait(dve, taken[("S", q, 1, d)])
                    link(tt(gi[:, ds, :], x0, x1, ALU.subtract))
                wait(dve, ends[("S", q, 1, 1)])
                for d in range(2):
                    gl0 = 16 * d + 4 * q
                    ds = slice(4 * d, 4 * d + 4)
                    for j in range(4):
                        rb = rho8[:, gl0 + j:gl0 + j + 1].to_broadcast([P, NCH])
                        for dst, src in ((sgr, gr), (sgi, gi)):
                            ins = after().tensor_tensor_scan(dst[:, 4 * d + j, :], rb, src[:, 4 * d + j, :], 0.0,
                                                         ALU.mult, ALU.add)
                    link(ins)
                    w = slice(NCC - 1, NCH - 1)
                    x0, x1 = (t[:, 0:4 * NCX].rearrange("p (a c) -> p a c", a=4) for t in t5)
                    tc_, ts_ = tcos[:, ds, w], tsin[:, ds, w]
                    a_, b_ = sgr[:, ds, w], sgi[:, ds, w]
                    hr, hi_ = H[:, 0, ds, :], H[:, 1, ds, :]
                    if d:
                        hr, hi_ = hr[:, :, ::-1], hi_[:, :, ::-1]
                    link(tt(x0, a_, tc_, ALU.mult))
                    link(tt(x1, b_, ts_, ALU.mult))
                    link(tt(hr, x0, x1, ALU.subtract))
                    link(tt(x0, a_, ts_, ALU.mult))
                    link(tt(x1, b_, tc_, ALU.mult))
                    tt(hi_, x0, x1, ALU.add).then_inc(s["Hs"], 1)
            for k in range(4):
                dve.wait_ge(s["gth"], k + 1)
                low(yg_lo[:, k, :], yg[:, k, :], yg_hi[:, k, :]).then_inc(s["gtl"], 1)
            split_to(46)
            for m in range(4):
                wait(dve, taken[("glu", m)])
                tt(yg[:, m, :], yg[:, m, :], tmp[m % 2][:, :], ALU.mult).then_inc(s["oun"], 1)
                dve.wait_ge(s["oth"], HEADS + m + 1)
                low(o_lo[:, m, :], yg[:, m, :], o_hi[:, m, :]).then_inc(s["otl"], 1)
            merge(1, 47)
            wait(dve, ends["ada1"])
            pv = bank(0, 64, 32).rearrange("p (m x) -> p m x", x=2)
            tt(modx[:, 16:48], pv[:, :, 0], ab[:, 16:48], ALU.add).then_inc(bank_free[0], 1)
            wait(dve, taken["ada1"])
            nf = vc1[:, VOFF["norm_ffn"]:VOFF["norm_ffn"] + KD]
            link(after().scalar_tensor_tensor(affn[:, :], modx[:, 32:40], 1.0, nf, ALU.add, ALU.mult))
            phase_end(5)

            dve.wait_ge(ld["hyp"], 16 * NHYP)
            after().tensor_copy(altr[:, :], cst[:, C_ALT:C_ALT + P]).then_inc(s["alt"], 1)
            after().tensor_copy(alt_row[:, :], hrnd[0:1, :]).then_inc(s["alt"], 1)
            dve.wait_ge(s["alt"], 2)
            for i in range(2):
                wait(dve, ends[("hid", i)])
                after().tensor_scalar(harg[:, :], bank(0)[0:64], vc3[:, i:i + 1], vc3[:, 2:3], ALU.add, ALU.mult)\
                    .then_inc(bank_free[0], 1)
                wait(dve, taken[("hid", i)])
                reduce_angle(harg[:, :], hrnd[:, :])
                dve.drain().then_inc(s["hya"], 1)
            split_to(98)
            c = 99
            for half in range(2):
                for part in range(3):
                    for i in range(2):
                        split_to(c + 2)
                        c += 1
                        n = 2 * part + i
                        ct = 4 * part + 2 * half + i
                        o = tmp[n % 2] if part < 2 else g2c[:, i]
                        z = bank(n % 4)
                        dve.wait_ge(s["zc"], 6 * half + n + 1)
                        o = tmp[n % 2][:, :] if part < 2 else g2c[:, i, :]
                        link(after().scalar_tensor_tensor(o[:, 1:T], z[:, 0:T - 1], vc2[:, ct:ct + 1], o[:, 1:T],
                                                      ALU.mult, ALU.add))
                        after().scalar_tensor_tensor(o[:, 0:T - 1], z[:, 1:T], vc2[:, 24 + ct:25 + ct], o[:, 0:T - 1],
                                                 ALU.mult, ALU.add).then_inc(bank_free[n % 4], 1)
                        if part == 0:
                            cs = slice(i * P, (i + 1) * P)
                            dve.wait_ge(s["zt"], 2 * half + i + 1)
                            low(u_lo[:, :, cs], bank(4 + n % 2).rearrange("p (t c) -> p t c", t=TT), u_hi[:, :, cs])\
                                .then_inc(bank_free[4 + n % 2], 1)
                for o in range(2):
                    it = 2 * half + o
                    dve.wait_ge(ld["hyb"], 16 * (it + 1))
                    for t in range(TT):
                        n = TT * it + t
                        wait(dve, ends[("f", half, o, t)])
                        dve.wait_ge(ld["win"], 16 * (n + 1))
                        fb = tmp[t % 2]
                        tt(fb[:, :], bank(6 + t % 2), win[:, :, :].rearrange("p a c -> p (a c)"), ALU.mult)\
                            .then_inc(bank_free[6 + t % 2], 1)
                        wait(dve, taken[("f", half, o, t)])
                        tt(tmp[2][:, HC:T], fb[:, 0:HC], fb[:, HC:T], ALU.subtract)
                        ins = tt(tmp[2][:, 0:HC], fb[:, 0:HC], fb[:, HC:T], ALU.add)
                        if t == 0:
                            link(ins)
                            ins = tt(tmp[2][0:1, 0:HC], tmp[2][0:1, 0:HC], hyb[:, :], ALU.add)
                        ins.then_inc(s["hs"], 1)
                        dve.wait_ge(s["hsh"], n + 1)
                        low(y_lo[:, t, :], tmp[2][:, :], y_hi[:, t, :]).then_inc(s["hsl"], 1)
                    for j in range(4):
                        wait(dve, ends[("Us", half, o, j)])
                        wait(dve, taken[("G", half, o, j)])
                        g = Gs[:, j, :].rearrange("p (r c) -> p r c", r=2)
                        uu = bank(j).rearrange("p (r c) -> p r c", r=2)
                        link(tt(tmp[0][:, :], bank(j), Gs[:, j, :], ALU.mult))
                        tt(tmp[1][:, :].rearrange("p (r c) -> p r c", r=2), uu, g[:, ::-1, :], ALU.mult)\
                            .then_inc(bank_free[j], 1)
                        wait(dve, taken[("Us", half, o, j)])
                        tt(tmp[2][:, 0:HC], tmp[0][:, 0:HC], tmp[0][:, HC:T], ALU.subtract)
                        tt(tmp[2][:, HC:T], tmp[1][:, 0:HC], tmp[1][:, HC:T], ALU.add).then_inc(s["yt"], 1)
                        dve.wait_ge(s["yth"], 4 * it + j + 1)
                        low(y_lo[:, j, :], tmp[2][:, :], y_hi[:, j, :]).then_inc(s["ytl"], 1)
                    wait(dve, ends[("Un", half, o)])
                    after().tensor_scalar(nyg[:, :], bank(4, HC)[0:1], 1.0 / 1024, None, ALU.mult).then_inc(bank_free[4], 1)
                    wait(dve, taken[("Gn", half, o)])
                    tt(nyg[:, :], bank(5, HC)[0:1], nyg[:, :], ALU.mult).then_inc(bank_free[5], 1)
                    wait(dve, taken[("Un", half, o)])
                    link(after().tensor_copy(nyh[:, :], nyg[:, :]))
                    low(nyl[:, :], nyg[:, :], nyh[:, :]).then_inc(s["nyq"], 1)
                    if o == 0:
                        for t in range(TT):
                            wait(dve, ends[("c1", half, t)])
                            b = 6 + t % 2
                            tt(tmp[t % 2][:, 0:HC], bank(b, HC), g1t[:, t, :], ALU.mult).then_inc(bank_free[b], 1)
                            wait(dve, taken[("c1", half, t)])
                            dve.drain().then_inc(s["ut"], 1)
                            dve.wait_ge(s["uth"], TT * half + t + 1)
                            low(u_lo[:, t, :], tmp[t % 2][:, 0:HC], u_hi[:, t, :]).then_inc(s["utl"], 1)
                    else:
                        for i in range(2):
                            wait(dve, ends[("c2", half, i)])
                            tt(tmp[i][:, :], bank(6 + i), g2c[:, i, :], ALU.mult).then_inc(bank_free[6 + i], 1)
                            wait(dve, taken[("c2", half, i)])
                            dve.drain().then_inc(s["oun"], 1)
                            dve.wait_ge(s["oth"], HEADS + 4 + 2 * half + i + 1)
                            low(e_lo[:, 2 * half + i, :], tmp[i][:, :], e_hi[:, 2 * half + i, :])\
                                .then_inc(s["otl"], 1)
            merge(2, 111)
            phase_end(6)

            link(after().memset(onesq[:, :], 1.0))
            for k in range(KD):
                dve.wait_ge(s["mh"], k + 1)
                low(m_lo[:, k, :], merged[:, k, :], m_hi[:, k, :]).then_inc(s["ml"], 1)
            for m in range(KD):
                split_to(127 + m + 2)
                wait(dve, ends[("wo", m)])
                wait(dve, taken[("x2T", m)])
                after().scalar_tensor_tensor(xT[:, m, :], bank(m % 4), modx[:, 16 + m:17 + m], xT[:, m, :],
                                         ALU.mult, ALU.add).then_inc(bank_free[m % 4], 1)
            wait(dve, ends["ss"])
            after().tensor_scalar(vrow[:, :], bank(4), 1.0 / D, EPS, ALU.mult, ALU.add).then_inc(bank_free[4], 1)
            wait(dve, taken["ss"])
            dve.drain().then_inc(s["vf"], 1)
            dve.wait_ge(s["sf"], 1)
            refine(vrow[:, :], srow[:, :], sqk[0][:, :], sqk[1][:, :], srow[:, :])

            def low_h2(k):
                dve.wait_ge(s["h2h"], k + 1)
                low(h_lo[:, k, :], tmp[k % 2][:, :], h_hi[:, k, :]).then_inc(s["h2l"], 1)

            for k in range(KD):
                link(tt(tmp[k % 2][:, :], xT[:, k, :], srow[:, :], ALU.mult))
                after().tensor_scalar(tmp[k % 2][:, :], tmp[k % 2][:, :], affn[:, k:k + 1], modx[:, 24 + k:25 + k],
                                  ALU.mult, ALU.add).then_inc(s["h2t"], 1)
                if k:
                    low_h2(k - 1)
            low_h2(KD - 1)
            phase_end(7)

            for f in range(FT):
                split_to(135 + 2 * f + 3)
                wait(dve, ends[("gu", f, 1)])
                wait(dve, taken[("gu", f, 0)])
                b = (2 * f + 1) % 8
                tt(tmp[f % 3][:, :], bank(b), tmp[f % 3][:, :], ALU.mult).then_inc(bank_free[b], 1)
                dve.wait_ge(s["ath"], f + 1)
                low(act_lo[:, f, :], tmp[f % 3][:, :], act_hi[:, f, :]).then_inc(s["atl"], 1)
            for m in range(KD):
                split_to(179 + 4 * m + 6)
                wait(dve, ends[("down", m)])
                after().scalar_tensor_tensor(xT[:, m, :], bank(m % 4), modx[:, 40 + m:41 + m], xT[:, m, :],
                                         ALU.mult, ALU.add).then_inc(bank_free[m % 4], 1)
            dve.wait_ge(s["sq"], 8)
            link(after().tensor_scalar(rs[:, 2, 1, 0:TT], rs[:, 2, 0, 0:TT], 1.0 / D, EPS, ALU.mult, ALU.add))
            dve.drain().then_inc(s["var"], 1)
            dve.wait_ge(s["sqrt"], 3)
            refine(rs[:, 2, 1, 0:TT], rs[:, 2, 2, 0:TT], rs[:, 2, 3, 0:TT], rs[:, 2, 4, 0:TT], rs[:, 2, 5, 0:TT])
            dve.wait_ge(ld["fnorm"], 16)
            for t in range(TT):
                after().scalar_tensor_tensor(ytok[:, t, :], ytok[:, t, :], rs[:, 2, 5, t:t + 1], fnorm[:, :],
                                         ALU.mult, ALU.mult).then_inc(s["fin"], 1)

        @block.sync
        def _(sp):
            at = [0]

            def load(o, i, which, n=16):
                sp.dma_start(o, i).then_inc(ld[which], 16)

            def ring_to(c1):
                while at[0] <= min(c1, len(chunks) - 1):
                    c = at[0]
                    at[0] += 1
                    src, kt, n, kind, dest = chunks[c]
                    i = c % RING
                    if c >= RING:
                        p = c - RING
                        if chunks[p][3] == "plain":
                            wait(sp, ends[("chunk", p)])
                        else:
                            sp.wait_ge(s_lo, nth_split[p] + 1)
                    sp.dma_start(raw[i][:, 0:kt * n].rearrange("p (k n) -> p k n", k=kt), src).then_inc(raw_in[i], 16)

            load(cst[:, :], a["cst"], "small")
            for name, rows in VECS:
                o = VOFF[name]
                src = a[name]
                load(vr1[o:o + rows, :], src.rearrange("(r p) -> r p", p=P), "small")
            load(vr2[:, :], a["hy_conv_w"].rearrange("j (r p) -> (j r) p", p=P), "small")
            for i, name in enumerate(("hy_f_b1", "hy_f_b2", "hy_f_freq")):
                load(vr3[i:i + 1, :], a[name].rearrange("(r p) -> r p", p=64), "small")
            load(xt[:, 0:TT, :], a["x"].rearrange("(t p) d -> p t d", p=P), "x")
            load(xt[:, TT:KT, :], a["ctx"].rearrange("(t p) d -> p t d", p=P), "ctx")
            ring_to(23)
            for t in range(KT):
                wait(sp, taken[("us", t)])
                load(uch[16 * t:16 * t + 16, :, :], us[:, t, :], "uch")
            wait(sp, ends[("us", KT - 1)])
            sp.wait_ge(s["htl"], 2 * KD)
            load(rope[:, :, :, :], a["rope"].rearrange("(t p) x f -> p t x f", p=P), "rope")
            ring_to(29)
            sp.wait_ge(s_phase, 9)
            ring_to(46)
            sp.wait_ge(s_phase, 12)
            load(row[:, 0, :], a["s5_lam_re"], "s5")
            load(row[:, 1, :], a["s5_lam_im"], "s5")
            load(dt2[:, :], a["s5_log_dt"], "s5")
            for part, name in enumerate(("s5_b_re", "s5_b_im")):
                load(bld[:, part], a[name], "s5")
            for part, name in enumerate(("s5_c_re", "s5_c_im")):
                for i in range(4):
                    for g2 in range(2):
                        for dp in range(8):
                            load(cld[16 * dp:16 * dp + 16, part, i, 64 * g2:64 * g2 + 64],
                                 a[name][8 * i + dp, g2], "s5")
            for q in range(4):
                wait(sp, taken[("K", q)])
                load(scratch[q], K2[:, :, :].rearrange("p l n -> p (l n)"), "kfilt")
                sp.wait_ge(ld["kfilt"], 16 * (q + 1))
                if q:
                    wait(sp, ends[("Y", q - 1, 1)])
                for st in range(L):
                    load(Mt[GC * st:GC * (st + 1), :, :],
                         scratch[q].rearrange("(g m) c -> m g c", m=GC)[:, :, (7 - st) * GC:(15 - st) * GC], "kread")
                wait(sp, taken[("Y", q, 0)])
                wait(sp, taken[("Y", q, 1)])
                for t in range(TT):
                    load(y5tok[:, t, q * P:(q + 1) * P], Y2[16 * t:16 * t + 16, :, :], "ytok")
            ring_to(98)
            sp.wait_ge(s_phase, 15)
            load(w12[0:33, 0, :], a["hy_f_w1"], "hyp")
            load(w12[:, 1, :], a["hy_f_w2"], "hyp")
            load(zpos[:, :], a["zpos"], "hyp")
            load(hrnd[0:1, :], a["alt_row"], "hyp")
            c = 99
            for half in range(2):
                ring_to(c + 8)
                c += 6
                hs = slice(half * HC, (half + 1) * HC)
                for o in range(2):
                    it = 2 * half + o
                    if it:
                        wait(sp, ends[("f", (it - 1) // 2, (it - 1) % 2, TT - 1)])
                        sp.wait_ge(s["hs"], TT * (it - 1) + 1)
                    load(w3[:, :, :], a["hy_f_w3"].rearrange("h (o d c) -> h o d c", o=2, d=2)[:, o, :, hs], "w3")
                    load(hyb[:, :], a["hy_bias"][o:o + 1, hs], "hyb")
                    for t in range(TT):
                        n = TT * it + t
                        if n:
                            sp.wait_ge(s["hs"], n)
                        load(win[:, :, :], a["window"][t * P:(t + 1) * P].rearrange("p (o d c) -> p o d c", o=2, d=2)
                             [:, o, :, hs], "win")
            ring_to(128)
            sp.wait_ge(s_phase, 18)
            load(x2t[:, :, :], a["x"].rearrange("(t p) d -> p t d", p=P), "x2")
            ring_to(len(chunks) - 1)
            wait(sp, ends[("gu", FT - 1, 1)])
            load(fnorm[:, :], a["final_norm"].rearrange("(r n) -> r n", r=1).to_broadcast([P, D]), "fnorm")
            for t in range(TT):
                sp.wait_ge(s["fin"], t + 1)
                load(out[t * P:(t + 1) * P, :], ytok[:, t, :], "out")
            sp.wait_ge(ld["out"], 16 * TT)


def _constants():
    import math

    import numpy as np
    c = np.zeros((P, C_N), np.float64)
    c[:, C_ID:C_ID + P] = np.eye(P)
    c[:, C_EYE16:C_EYE16 + GC] = np.tile(np.eye(GC), (P // GC, 1))
    c[:, C_GS:C_GS + 4] = 2.0 / 1024
    c[0, C_GS] = 1.0 / 1024
    c[:, C_ALT:C_ALT + P] = np.where(np.arange(P) % 2, -1.0, 1.0)[:, None]
    c[:, C_E9:C_E9 + 9] = np.arange(9)
    c[:, C_K:C_K + NCH] = np.arange(1, NCH + 1)
    n = np.arange(T)
    ang = 2 * np.pi * (np.outer(n, n) % 1024) / 1024
    t = np.linspace(0.0, 1.0, T)[:, None]
    w = 2 * np.pi * n[:, None] / T
    bands = np.linspace(1e-4, 15, 16)[None, :]
    zpos = np.concatenate([t, np.cos(bands * w), -np.sin(bands * w)], axis=-1).T
    deltas = np.abs(np.linspace(math.log(1e-2) / 0.3, math.log(1e-2) / 1.5, 4 * W5))
    window = np.exp(-t * deltas) + 0.05
    inv = 10000.0 ** (-np.arange(8) / 8)
    ang2 = np.concatenate([(n // 64)[:, None] * inv, (n % 64)[:, None] * inv], axis=-1)
    rope = np.stack([np.cos(ang2), np.sin(ang2)], axis=1)
    alt = np.where(n % 2, -1.0, 1.0)[None, :]
    got = {"cst": c, "dft_cos": np.cos(ang), "dft_sin": -np.sin(ang), "zpos": zpos, "window": window,
           "rope": rope, "alt_row": alt}
    return {k: np.ascontiguousarray(v.astype(np.float32)) for k, v in got.items()}


def make(nc, arrays, dt_of):
    a = {}
    for name, v in arrays.items():
        ap = nc.dram_tensor("in_" + name, v.shape, dt_of(v.dtype), kind="ExternalInput").ap()
        a[name] = ap
    for name in list(a):
        if name in ("x", "ctx", "c"):
            a[name] = a[name][0]
        elif len(a[name].shape) > 1 and name not in ("cst", "dft_cos", "dft_sin", "zpos", "window", "rope", "alt_row"):
            a[name] = a[name][0]
    for name in ("s5_lam_re", "s5_lam_im"):
        a[name] = a[name].rearrange("d (a g) p -> (d a) (g p)", g=2)
    a["s5_log_dt"] = a["s5_log_dt"].rearrange("d (a g) -> (d a) g", g=2)
    for name in ("s5_b_re", "s5_b_im"):
        a[name] = a[name].rearrange("d (a g) p n -> (g p) (d a) n", g=2)
    for name in ("s5_c_re", "s5_c_im"):
        a[name] = a[name].rearrange("d (a g) n p -> (d a) g n p", g=2)
    scratch = nc.dram_tensor("lag_kernels", (4, P, 15 * GC), F32, kind="Internal").ap()
    out = nc.dram_tensor("out_x", (1, T, D), F32, kind="ExternalOutput").ap()
    build(nc, a, scratch, out[0])


def kernel(**inputs):
    import numpy as np
    from concourse import bacc
    from concourse.bass_utils import run_bass_kernel_spmd

    nc = bacc.Bacc("TRN2", target_bir_lowering=False, num_devices=1)
    arrays = {k: np.ascontiguousarray(v) for k, v in inputs.items()}
    arrays.update(_constants())
    make(nc, arrays, mybir.dt.from_np)
    r = run_bass_kernel_spmd(nc, [{"in_" + k: v for k, v in arrays.items()}], core_ids=[0])
    return r.results[0]["out_x"]
```

```python
from contextlib import ExitStack

import concourse.bass as bass
from concourse import mybir

F32 = mybir.dt.float32
F32R = mybir.dt.float32r
ACT = mybir.ActivationFunctionType
ALU = mybir.AluOpType
AX = mybir.AxisListType

P = 128
D = 1024
KD = D // P
T = 512
TT = T // P
TC = 256
TTC = TC // P
EPS = 1e-6
HEADS, NOPE, ROPE, VD = 8, 64, 32, 64
QK = NOPE + ROPE
QL, KVL = 256, 128
KEYS = T + TC
KT = KEYS // P
SCALE = float(QK) ** -0.5
G, GC, ST = 32, 16, 64
PAIRS = G // 2
L = 8
NCX, NCC = T // L, TC // L
NCH = NCX + NCC
W5 = 512
HC = 256
CONVS = [(0, 0), (1, 0), (0, 1), (1, 1)]
FF = 2816
FT = FF // P
O_KV, O_KR, O_S5, O_HY, O_GATE = 256, 384, 416, 928, 2464
IN_W = 5536
TWO_PI_HI = 6.28125
TWO_PI_LO = 0.0019353071795864769
INV_2PI = 0.15915494309189535
ROUND = 12582912.0
PI = 3.1415925

C_ID, C_EYE16, C_GS, C_ALT, C_E9, C_K = 0, 128, 144, 148, 276, 285
C_N = C_K + NCH

VECS = [("c", 8), ("c_ctx", 8), ("norm_mix", 8), ("norm_ffn", 8), ("final_norm", 8), ("ada_b", 48),
        ("mla_q_norm", 2), ("mla_kv_norm", 1), ("s5_d", 4), ("hy_conv_b", 12)]
VOFF = {}
_at = 0
for _n, _r in VECS:
    VOFF[_n] = _at
    _at += _r
VROWS = _at


NSMALL = 1 + len(VECS) + 1 + 3
NS5 = 3 + 2 + 2
NHYP = 4


def build(nc, a, scratch, out):
    base = (nc.sbuf_base + 31) // 32 * 32
    ctx = ExitStack()
    with ctx:
        def sem(name):
            return ctx.enter_context(nc.semaphore(name))

        class Region:

            def __init__(self, start, end):
                self.at, self.end = start, end

            def __call__(self, name, shape, dt=F32):
                n = 4
                for s in shape[1:]:
                    n *= s
                n = (n + 31) // 32 * 32
                t = nc.alloc_sbuf_tensor_at(name, shape, dt, offset=base + self.at)
                self.at += n
                assert self.at <= self.end, (name, self.at, self.end)
                return t

        PS = ctx.enter_context(nc.psum_tensor("PS", [P, 8 * 512], F32))

        def bank(b, n=512, o=0):
            return PS[:, 512 * b + o:512 * b + o + n]

        K = 1024
        r = Region(0, 14 * K)
        cst = r("cst", [P, C_N])
        ident = cst[:, C_ID:C_ID + P]
        vc1 = r("vc1", [P, VROWS])
        vc2 = r("vc2", [P, 36])
        vc3 = r("vc3", [64, 3])
        modx = r("modx", [P, 48])
        modc = r("modc", [P, 16])
        amix = r("amix", [P, 2, KD])
        affn = r("affn", [P, KD])
        silc = r("silc", [P, 16])
        rs = r("rs", [P, 3, 6, 16])
        altr = r("altr", [P, P], F32R)
        alt_row = r("alt_row", [1, T], F32R)
        tmp = [r(f"tmp{i}", [P, T]) for i in range(3)]
        nyl = r("nyl", [1, HC], F32R)
        RING = 4
        r = Region(14 * K, 62 * K)
        raw = [r(f"raw{i}", [P, 1024]) for i in range(RING)]
        whi = [r(f"whi{i}", [P, 1024], F32R) for i in range(RING)]
        wlo = [r(f"wlo{i}", [P, 1024], F32R) for i in range(RING)]
        r = Region(62 * K, 94 * K)
        h_hi = r("h_hi", [P, KD, T], F32R)
        h_lo = r("h_lo", [P, KD, T], F32R)
        r = Region(62 * K, 94 * K)
        ytok = r("ytok", [P, TT, D])
        fnorm = r("fnorm", [P, D])
        fsq = r("fsq", [P, D])
        Z = 94 * K
        ZEND = 207 * K + 512
        r = Region(Z + 97 * K, ZEND)
        U = r("U", [P, G, P])
        r = Region(Z + 81 * K, Z + 97 * K)
        o_hi = r("o_hi", [P, TT, T], F32R)
        o_lo = r("o_lo", [P, TT, T], F32R)
        r = Region(Z, Z + 81 * K)
        hc_hi = r("hc_hi", [P, KD, TC], F32R)
        hc_lo = r("hc_lo", [P, KD, TC], F32R)
        a_at = r.at
        vr1 = r("vr1", [VROWS, P])
        vr2 = r("vr2", [36, P])
        vr3 = r("vr3", [3, 64])
        xt = r("xt", [P, TT + TTC, D])
        ada = [r(f"ada{i}", [P, KD, P]) for i in range(3)]
        sq0 = r("sq0", [P, D])
        r = Region(a_at, Z + 81 * K)
        us = r("us", [P, KT, W5])
        uch = r("uch", [NCH, L, W5])
        uch2 = r("uch2", [NCH, G, L, GC])
        c_at = r.at
        r = Region(a_at, Z + 81 * K)
        qtok = r("qtok", [P, TT, HEADS, QK])
        kvT_hi = r("kvT_hi", [P, KEYS], F32R)
        kvT_lo = r("kvT_lo", [P, KEYS], F32R)
        krtok = r("krtok", [P, KT, ROPE])
        b_at = r.at
        r = Region(c_at, Z + 97 * K)
        rope = r("rope", [P, TT, 2, 16])
        ztok = r("ztok", [P, KT, 416])
        qnT_hi = r("qnT_hi", [P, 2, T], F32R)
        qnT_lo = r("qnT_lo", [P, 2, T], F32R)
        sq1 = r("sq1", [P, 256])
        r = Region(b_at, Z + 81 * K)
        prob = r("prob", [P, TT, KEYS])
        kT_hi = r("kT_hi", [QK, KEYS], F32R)
        kT_lo = r("kT_lo", [QK, KEYS], F32R)
        qT_hi = r("qT_hi", [QK, T], F32R)
        qT_lo = r("qT_lo", [QK, T], F32R)
        v_hi = r("v_hi", [P, KT, 2, VD], F32R)
        v_lo = r("v_lo", [P, KT, 2, VD], F32R)
        den = r("den", [P, 2, HEADS, TT])
        ones = r("ones", [P, P])
        mx = r("mx", [P, 2 * TT * HEADS])
        r = Region(Z, a_at)
        pTa_hi = r("pTa_hi", [P, 4, T], F32R)
        pTa_lo = r("pTa_lo", [P, 4, T], F32R)
        r = Region(b_at + 36 * K, Z + 81 * K)
        pTb_hi = r("pTb_hi", [P, 2, T], F32R)
        pTb_lo = r("pTb_lo", [P, 2, T], F32R)
        r = Region(Z, Z + 16 * K)
        merged = r("merged", [P, KD, T])
        r = Region(Z + 16 * K, Z + 81 * K)
        NPD = 2 * PAIRS
        lpr = r("lpr", [P, NPD, 9])
        lpi = r("lpi", [P, NPD, 9])
        th8 = r("th8", [P, NPD])
        rho8 = r("rho8", [P, NPD])
        base4 = r("base4", [P, 4, NPD])
        bbr = r("bbr", [P, NPD, GC])
        bbi = r("bbi", [P, NPD, GC])
        ctr = r("ctr", [P, NPD, GC])
        cti = r("cti", [P, NPD, GC])
        y5tok = r("y5tok", [P, TT, W5])
        s5_at = r.at
        row = r("row", [NPD, 12, P])
        dt2 = r("dt2", [NPD, 2])
        bld = r("bld", [P, 2, NPD, GC])
        cld = r("cld", [P, 2, 8, ST])
        lt = r("lt", [P, 4, NPD * 9])
        r = Region(s5_at, Z + 97 * K)
        bdr = r("bdr", [P, 8, 32])
        bdi = r("bdi", [P, 8, 32])
        pmr = r("pmr", [P, 8, P])
        pmi = r("pmi", [P, 8, P])
        t5w = r("t5", [P, 2 * 4 * 9 * GC])
        t5g = [r(f"t5g_{i}", [P, 4, 9, GC]) for i in range(2)]
        t5 = [t5w[:, i * 4 * 9 * GC:(i + 1) * 4 * 9 * GC] for i in range(2)]
        WT = r("WT", [P, 2, 8, P])
        Mt = r("Mt", [P, 8, P])
        K2 = r("K2", [P, 15, GC])
        ang_s, ang_c = (r(n, [P, 8, NCH]) for n in ("ang_s", "ang_c"))
        gr = r("gr", [P, 8, NCH])
        gi = r("gi", [P, 8, NCH])
        H = r("H", [P, 2, 8, NCX])
        Y2 = r("Y2", [NCX, L, P])
        sgr, sgi = (x[:, :, :].rearrange("p a b -> p (a b)")[:, 0:8 * NCH].rearrange("p (a c) -> p a c", c=NCH)
                    for x in (pmr, pmi))
        r = Region(30 * K, 62 * K)
        clr2, cli2 = ([r(f"{n}{i}", [P, 8, 9, GC]) for i in range(2)] for n in ("clr", "cli"))
        tsin2, tcos2 = ([r(f"{n}{i}", [P, 8, NCH]) for i in range(2)] for n in ("tsin", "tcos"))
        r = Region(s5_at, Z + 81 * K)
        yg = r("yg", [P, TT, T])
        yg_hi = r("yg_hi", [P, TT, T], F32R)
        yg_lo = r("yg_lo", [P, TT, T], F32R)
        r = Region(Z + 16 * K, ZEND)
        fc_hi = r("fc_hi", [P, 4, T], F32R)
        fc_lo = r("fc_lo", [P, 4, T], F32R)
        fs_hi = r("fs_hi", [P, 4, T], F32R)
        fs_lo = r("fs_lo", [P, 4, T], F32R)
        e_at = r.at
        e_hi = r("e_hi", [P, TT, T], F32R)
        e_lo = r("e_lo", [P, TT, T], F32R)
        u_hi, u_lo, g1t, g2c = [], [], [], []
        for half in range(2):
            u_hi.append(r(f"u_hi{half}", [P, TT, HC], F32R))
            u_lo.append(r(f"u_lo{half}", [P, TT, HC], F32R))
            g1t.append(r(f"g1t{half}", [P, TT, HC]))
            g2c.append(r(f"g2c{half}", [P, 2, T]))
        Gs = r("Gs", [P, 4, 2 * HC])
        hid2 = r("hid2", [64, T])
        w3 = r("w3", [64, 2, HC])
        win = r("win", [P, 2, HC])
        nyg = r("nyg", [1, HC])
        nyh = r("nyh", [1, HC], F32R)
        hyb = r("hyb", [1, HC])
        ybuf = []
        for i, at_ in enumerate((e_at, 30 * K, 46 * K)):
            r = Region(at_, at_ + 16 * K)
            ybuf.append((r(f"y_hi{i}", [P, TT, 2 * HC], F32R), r(f"y_lo{i}", [P, TT, 2 * HC], F32R)))
        ybuf.append(ybuf[1])
        r = Region(e_at, e_at + 16 * K)
        hid1 = r("hid1", [64, T])
        harg = r("harg", [64, T])
        hrnd = r("hrnd", [64, T])
        zpos = r("zpos", [33, T])
        w12 = r("w12", [64, 2, 64])
        r = Region(Z + 16 * K, Z + 104 * K)
        act_hi = r("act_hi", [P, FT, T], F32R)
        act_lo = r("act_lo", [P, FT, T], F32R)
        r = Region(Z + 16 * K, Z + 104 * K)
        m_hi = r("m_hi", [P, KD, T], F32R)
        m_lo = r("m_lo", [P, KD, T], F32R)
        r = Region(Z + 64 * K, Z + 104 * K)
        x2t = r("x2t", [P, TT, D])
        xT = merged
        r = Region(Z + 104 * K, ZEND)
        sqk = [r(f"sqk{i}", [P, T]) for i in range(2)]
        vrow = r("vrow", [P, T])
        srow = r("srow", [P, T])
        onesq = r("onesq", [P, P])

        bank_free = [sem(f"bank_free{b}") for b in range(8)]
        raw_in = [sem(f"raw_in{i}") for i in range(RING)]
        s_hi = sem("chunk_hi")
        s_lo = sem("chunk_lo")
        s_phase = sem("phase")
        s_act, s_dve, s_dvx = sem("act_chain"), sem("dve_chain"), sem("dve_for_others")
        ld = {n: sem("in_" + n) for n in ("small", "x", "ctx", "rope", "uch", "kfilt", "kread", "s5", "ytok",
                                          "hyp", "w3", "win", "hyb", "x2", "fnorm", "out")}
        mm = {n: sem("pe_" + n) for n in ("vec", "ada", "xT", "s5in", "uT", "proj", "nT", "q", "att", "merge",
                                          "s5", "glu", "hy", "out", "norm", "up", "down", "end")}
        s = {n: sem("s_" + n) for n in (
            "silu", "vc", "s5a", "sq", "var", "sqrt", "xh", "htmp", "hth", "htl", "mod", "us", "zn", "ntmp", "nth", "ntl",
            "qrope", "krope", "av", "rc", "diag", "oatt", "aqk", "exp", "max", "pTh", "oun", "oth", "otl", "sig", "s5row", "s5col",
            "s5c", "angle", "trig", "mag", "bb", "pm", "cl", "K2", "WTd", "rot", "Hs", "Yq", "gelu", "gtmp", "gth", "gtl",
            "hya", "hys", "hid", "zc", "zt", "cv", "hs", "hsh", "hsl", "yt", "yth", "ytl", "ut", "uth", "utl",
            "alt", "mg", "gsc", "nyq", "mh", "ml", "x1", "sq2", "vf", "sf", "h2t", "h2h", "h2l", "silf", "at", "ath",
            "atl", "x3", "yo", "fin")}

        chunks = []

        def add(src, kt, n, kind="split", dest=None):
            chunks.append((src, kt, n, kind, dest))

        def wcols(w, k0, kt, c0, n):
            return w[k0 * P:(k0 + kt) * P, c0:c0 + n].rearrange("(k p) n -> p k n", p=P)

        for g in range(4):
            for i in range(4):
                add(wcols(a["ada_w"], 2 * i, 2, g * T, T), 2, T, "plain")
        for i in range(4):
            add(wcols(a["w_in"], 2 * i, 2, O_S5, W5), 2, W5)
        for i in range(4):
            add(wcols(a["w_in"], 2 * i, 2, 0, 416), 2, 416)
        for k in range(2):
            add(wcols(a["mla_w_uq"], k, 1, 0, 768), 1, 768)
        add(wcols(a["mla_w_ukv"], 0, 1, 0, 1024), 1, 1024)
        branch_w = ["w_branch_mla", "w_branch_s5", "w_branch_hy"]

        def merge_chunks(j):
            for m in range(KD):
                add(wcols(a["w_in"], 0, KD, O_GATE + j * D + m * P, P), KD, P)
                add(wcols(a[branch_w[j]], 0, 4, m * P, P), 4, P)

        merge_chunks(0)
        for g in range(4, 12):
            for i in range(4):
                add(wcols(a["ada_w"], 2 * i, 2, g * T, T), 2, T, "plain")
        for m in range(4):
            add(wcols(a["s5_w_glu"], 0, 4, m * P, P), 4, P)
        merge_chunks(1)
        for part in range(3):
            for i in range(4):
                add(wcols(a["w_in"], 0, KD, O_HY + part * W5 + i * P, P), KD, P)
        for src, hi_, lo_ in ((a["dft_cos"], fc_hi, fc_lo), (a["dft_sin"], fs_hi, fs_lo)):
            for i in range(2):
                add(wcols(src, 2 * i, 2, 0, T), 2, T, "const",
                    (hi_[:, 2 * i:2 * i + 2, :].rearrange("p a b -> p (a b)"),
                     lo_[:, 2 * i:2 * i + 2, :].rearrange("p a b -> p (a b)")))
        merge_chunks(2)
        for m in range(KD):
            add(wcols(a["w_out"], 0, KD, m * P, P), KD, P)
        for f in range(FT):
            add(wcols(a["ffn_w_gu"], 0, KD, f * P, P), KD, P)
            add(wcols(a["ffn_w_gu"], 0, KD, FF + f * P, P), KD, P)
        DOWN = (6, 6, 5, 5)
        for m in range(KD):
            k0 = 0
            for kt in DOWN:
                add(wcols(a["ffn_w_down"], k0, kt, m * P, P), kt, P)
                k0 += kt
        nth_split = []
        n = 0
        for ch in chunks:
            nth_split.append(n)
            n += ch[3] != "plain"

        uses = [0] * 8
        ends = {}
        taken = {}
        counts = {}

        def close(ins, which, name):
            counts[which] = counts.get(which, 0) + 1
            ins.then_inc(mm[which], 1)
            ends[name] = (mm[which], counts[which])

        def wait(eng, at):
            eng.wait_ge(at[0], at[1])

        block = ctx.enter_context(nc.Block())

        @block.tensor
        def _(pe):
            nxt = [0]

            def open_(b, name):
                if uses[b]:
                    pe.wait_ge(bank_free[b], uses[b])
                uses[b] += 1
                taken[name] = (bank_free[b], uses[b])

            def chunk():
                c = nxt[0]
                nxt[0] += 1
                _, kt, n, kind, dest = chunks[c]
                i = c % RING
                if kind == "plain":
                    pe.wait_ge(raw_in[i], 16 * (c // RING + 1))
                    return c, raw[i][:, 0:kt * n].rearrange("p (k n) -> p k n", k=kt)
                pe.wait_ge(s_lo, nth_split[c] + 1)
                if kind == "const":
                    return c, None
                return c, tuple(w[i][:, 0:kt * n].rearrange("p (k n) -> p k n", k=kt) for w in (whi, wlo))

            def mm3(o, w, x, first, last):
                pe.matmul(o, w[0], x[0], start=first, stop=False)
                pe.matmul(o, w[0], x[1], start=False, stop=False)
                return pe.matmul(o, w[1], x[0], start=False, stop=last)

            def to_tokens(m):
                wait(pe, taken[("down", m)])
                open_(4 + m % 4, ("yo", m))
                for t in range(TT):
                    ins = pe.transpose(bank(4 + m % 4, P, t * P), xT[:, m, t * P:(t + 1) * P], ident)
                close(ins, "end", ("yo", m))

            def phase_end(k):
                pe.drain().then_inc(s_phase, 1)
                pe.wait_ge(s_phase, 3 * k)

            pe.wait_ge(ld["small"], 16 * NSMALL)
            open_(0, "vec")
            pe.transpose(bank(0, VROWS), vr1[:, :], cst[0:VROWS, C_ID:C_ID + VROWS])
            pe.transpose(bank(0, 36, 128), vr2[:, :], cst[0:36, C_ID:C_ID + 36])
            close(pe.transpose(bank(0, 3, 256)[0:64], vr3[:, :], cst[0:3, C_ID:C_ID + 3]), "vec", "vec")

            def ada_group(g, b):
                open_(b, ("ada", g))
                for i in range(4):
                    c, w = chunk()
                    for k in range(2):
                        kk = 2 * i + k
                        ins = pe.matmul(bank(b)[0:2], silc[:, kk:kk + 9:8], w[:, k, :], start=(kk == 0), stop=(kk == 7))
                    if i < 3:
                        close(ins, "ada", ("chunk", c))
                close(ins, "ada", ("ada", g))
                ends[("chunk", c)] = ends[("ada", g)]

            def ada_turned(g, b, first):
                wait(pe, taken[("ada", g)])
                if first:
                    open_(b, ("adaT", g))
                for i in range(4):
                    ins = pe.transpose(bank(b, 2, 2 * (4 * g + i)), tmp[g % 2][0:2, i * P:(i + 1) * P],
                                       cst[0:2, C_ID:C_ID + 2])
                close(ins, "ada", ("adaT", g))

            pe.wait_ge(s["silu"], 1)
            for g in range(4):
                ada_group(g, 2 + g % 2)
                if g:
                    ada_turned(g - 1, 1, g == 1)
            ada_turned(3, 1, False)
            taken["ada0"] = taken[("adaT", 0)]
            ends["ada0"] = ends[("adaT", 3)]

            def turned(k):
                for b, t0, t1 in ((6, 0, TT), (7, TT, KT)):
                    open_(b, ("xT", k, b - 6))
                    for t in range(t0, t1):
                        ins = pe.transpose(bank(b, P, (t - t0) * P), xt[:, t, k * P:(k + 1) * P], ident)
                    close(ins, "xT", ("xT", k, b - 6))

            def tokens(t, k):
                hi_, lo_, o = (h_hi, h_lo, t) if t < TT else (hc_hi, hc_lo, t - TT)
                return hi_[:, k, o * P:(o + 1) * P], lo_[:, k, o * P:(o + 1) * P]

            pe.wait_ge(s["xh"], TT + TTC)
            for k in range(3):
                turned(k)
            for i in range(4):
                c, w = chunk()
                pe.wait_ge(s["htl"], 4 * (i + 1))
                for t in range(KT):
                    if i == 0:
                        open_(t, ("us", t))
                    for k in range(2):
                        ins = mm3(bank(t), tokens(t, 2 * i + k), (w[0][:, k, :], w[1][:, k, :]),
                                  i == 0 and k == 0, i == 3 and k == 1)
                    if i == 3:
                        close(ins, "s5in", ("us", t))
                    if t == 2 and 2 * i + 3 < KD:
                        turned(2 * i + 3)
                if i < 3:
                    close(ins, "s5in", ("chunk", c))
                if 2 * i + 4 < KD:
                    turned(2 * i + 4)
            ends[("chunk", c)] = ends[("us", KT - 1)]

            for i in range(4):
                c, w = chunk()
                for t in range(KT):
                    o, n = (0, 416) if t < TT else (256, 160)
                    if i == 0:
                        open_(t, ("z", t))
                    for k in range(2):
                        ins = mm3(bank(t, n, o), tokens(t, 2 * i + k), (w[0][:, k, o:], w[1][:, k, o:]),
                                  i == 0 and k == 0, i == 3 and k == 1)
                    if i == 3:
                        close(ins, "proj", ("z", t))
                if i < 3:
                    close(ins, "proj", ("chunk", c))
            ends[("chunk", c)] = ends[("z", KT - 1)]

            pe.wait_ge(s["us"], 1)
            for i in range(8):
                b = 6 + i % 2
                open_(b, ("uT", i))
                for j in range(4):
                    g = 4 * i + j
                    ins = pe.transpose(bank(b, NCH, j * NCH), uch2[:, g].rearrange("c s m -> c (s m)"),
                                       cst[0:NCH, C_ID:C_ID + NCH])
                close(ins, "uT", ("uT", i))
            phase_end(1)

            pe.wait_ge(s["zn"], KT)
            for k in range(2):
                open_(k, ("nT", k))
                for t in range(TT):
                    ins = pe.transpose(bank(k, P, t * P), ztok[:, t, k * P:(k + 1) * P], ident)
                close(ins, "nT", ("nT", k))
            for k in range(2):
                open_(2 + k, ("nT", 2 + k))
                for t in range(*((0, TT) if k == 0 else (TT, KT))):
                    ins = pe.transpose(bank(2 + k, P, (t % TT) * P), ztok[:, t, QL:QL + KVL], ident)
                close(ins, "nT", ("nT", 2 + k))
            pe.wait_ge(s["ntl"], 4)
            c0, w0 = chunk()
            c1, w1 = chunk()
            for t in range(TT):
                for hf in range(2):
                    b = 4 + (2 * t + hf) % 4
                    open_(b, ("q", t, hf))
                    for k, w in enumerate((w0, w1)):
                        q = qnT_hi[:, k, t * P:(t + 1) * P], qnT_lo[:, k, t * P:(t + 1) * P]
                        ins = mm3(bank(b, 384), q, tuple(x[:, 0, hf * 384:(hf + 1) * 384] for x in w),
                                  k == 0, k == 1)
                    close(ins, "q", ("q", t, hf))
            ends[("chunk", c0)] = ends[("chunk", c1)] = ends[("q", TT - 1, 1)]
            phase_end(2)

            for part, (t0, t1) in enumerate(((0, TT), (TT, KT))):
                open_(part, ("kr", part))
                for t in range(t0, t1):
                    ins = pe.transpose(bank(part, P, (t - t0) * P)[0:ROPE], krtok[:, t, :], ident)
                close(ins, "att", ("kr", part))
            c, ukv = chunk()
            kv = kvT_hi, kvT_lo
            def head_in(h):
                open_(0, ("qT", h))
                for t in range(TT):
                    ins = pe.transpose(bank(0, P, t * P)[0:QK], qtok[:, t, h, :], ident)
                close(ins, "att", ("qT", h))
                for part, (k0, n) in enumerate(((0, T), (T, TC))):
                    open_(1 + part, ("k", h, part))
                    close(mm3(bank(1 + part, n), tuple(x[:, 0, h * P:(h + 1) * P] for x in ukv),
                              tuple(x[:, k0:k0 + n] for x in kv), True, True), "att", ("k", h, part))

            def values(p):
                for b, t0, t1 in ((1, 0, 4), (2, 4, KT)):
                    open_(b, ("v", p, b))
                    w = tuple(x[:, 0, 2 * p * P:(2 * p + 2) * P].rearrange("k (h c) -> k h c", h=2)[:, :, NOPE:]
                              for x in ukv)
                    for t in range(t0, t1):
                        ins = mm3(bank(b, P, (t - t0) * P), tuple(x[:, t * P:(t + 1) * P] for x in kv), w, True, True)
                    close(ins, "att", ("v", p, b))

            def weighted(h):
                for kt in range(KT):
                    wait(pe, taken[("pT", h, kt)])
                for b in (1, 2):
                    wait(pe, taken[("v", h // 2, b)])
                open_(3, ("o", h))
                for kt in range(KT):
                    pt = (pTa_hi[:, kt, :], pTa_lo[:, kt, :]) if kt < 4 else (pTb_hi[:, kt - 4, :], pTb_lo[:, kt - 4, :])
                    ins = mm3(bank(3), tuple(x[:, kt, :, :].rearrange("p g v -> p (g v)") for x in (v_hi, v_lo)), pt, kt == 0, kt == KT - 1)
                close(ins, "att", ("o", h))

            head_in(0)
            for h in range(HEADS):
                wait(pe, taken[("qT", h)])
                wait(pe, taken[("k", h, 0)])
                wait(pe, taken[("k", h, 1)])
                wait(pe, taken[("kr", 1)])
                for t in range(TT):
                    b = 4 + 2 * (t % 2)
                    open_(b, ("s", h, t))
                    q = qT_hi[:, t * P:(t + 1) * P], qT_lo[:, t * P:(t + 1) * P]
                    mm3(bank(b), q, (kT_hi[:, 0:T], kT_lo[:, 0:T]), True, True)
                    close(mm3(bank(b + 1, TC), q, (kT_hi[:, T:KEYS], kT_lo[:, T:KEYS]), True, True),
                          "att", ("s", h, t))
                if h:
                    weighted(h - 1)
                if h + 1 < HEADS:
                    head_in(h + 1)
                for t in range(TT):
                    wait(pe, taken[("s", h, t)])
                for kt in range(KT):
                    b = (4, 6, 0)[kt % 3]
                    open_(b, ("pT", h, kt))
                    for t in range(TT):
                        ins = pe.transpose(bank(b, P, t * P), prob[:, t, kt * P:(kt + 1) * P], ident)
                    close(ins, "att", ("pT", h, kt))
                    if kt == 2:
                        pe.wait_ge(s["diag"], h + 1)
                        open_(1, ("rc", h))
                        close(pe.matmul(bank(1), ones[:, :], tmp[0][:, :], start=True, stop=True), "att", ("rc", h))
                if h % 2 == 0:
                    values(h // 2)
            weighted(HEADS - 1)
            ends[("chunk", c)] = ends[("v", HEADS // 2 - 1, 2)]

            def hyena_setup(step):
                if step in (1, 4):
                    if step == 1:
                        pe.wait_ge(ld["hyp"], 16 * NHYP)
                    else:
                        pe.wait_ge(s["hid"], 1)
                    open_(0, ("hid", step // 4))
                    w, x = (w12[0:33, 0, :], zpos) if step == 1 else (w12[:, 1, :], hid1)
                    close(pe.matmul(bank(0)[0:64], w, x[:, :], start=True, stop=True), "hy", ("hid", step // 4))

            def s5_setup(step):
                if step == 0:
                    pe.wait_ge(ld["s5"], 16 * NS5)
                    for part in range(2):
                        for hf in range(2):
                            b = 4 + 2 * part + hf
                            open_(b, ("ct", part, hf))
                            for i in range(4):
                                ins = pe.transpose(bank(b, P, i * P)[0:ST], cld[:, part, 4 * hf + i, :], ident)
                            close(ins, "s5", ("ct", part, hf))
                elif step == 2:
                    pe.wait_ge(s["s5row"], 1)
                    open_(0, "s5row")
                    for i in range(4):
                        ins = pe.transpose(bank(0, NPD, i * NPD), row[:, 8 + i, :], cst[0:NPD, C_ID:C_ID + NPD])
                    close(ins, "s5", "s5row")

            def merge(j, x, ready, between=None):
                for m in range(KD):
                    b = 2 * (m % 4)
                    c, w = chunk()
                    open_(b, ("gate", j, m))
                    for k in range(KD):
                        ins = mm3(bank(b), (w[0][:, k, :], w[1][:, k, :]), (h_hi[:, k, :], h_lo[:, k, :]),
                                  k == 0, k == KD - 1)
                    close(ins, "merge", ("gate", j, m))
                    ends[("chunk", c)] = ends[("gate", j, m)]
                    c, w = chunk()
                    open_(b + 1, ("branch", j, m))
                    if m == 0:
                        pe.wait_ge(s["otl"], ready)
                    for k in range(4):
                        ins = mm3(bank(b + 1), (w[0][:, k, :], w[1][:, k, :]), (x[0][:, k, :], x[1][:, k, :]),
                                  k == 0, k == 3)
                    close(ins, "merge", ("branch", j, m))
                    ends[("chunk", c)] = ends[("branch", j, m)]
                    if between:
                        between(m)

            merge(0, (o_hi, o_lo), HEADS, s5_setup)
            phase_end(3)

            def s5_out(q, half):
                clr, cli = clr2[q % 2], cli2[q % 2]
                pe.wait_ge(ld["kread"], 16 * L * (q + 1))
                pe.wait_ge(s["Hs"], 2 * (q + 1))
                b = 1 + half
                open_(b, ("Y", q, half))
                for j in range(4):
                    gl, g2 = 2 * j + half, half
                    o = PS[0:NCX, 512 * b + P * j:512 * b + P * (j + 1)]
                    sl = slice(64 * g2, 64 * g2 + 64)
                    pe.matmul(o, U[:, 8 * q + gl, NCC:NCC + NCX], Mt[:, gl, :], start=True, stop=False)
                    for d in range(2):
                        l0 = 1 if d == 0 else 0
                        for part, cl in enumerate((clr, cli)):
                            ins = pe.matmul(o, H[sl, part, 4 * d + j, :], cl[sl, 4 * d + j, l0:l0 + 8, :],
                                            start=False, stop=(d == 1 and part == 1))
                close(ins, "s5", ("Y", q, half))

            for q in range(4):
                clr, cli = clr2[q % 2], cli2[q % 2]
                pe.wait_ge(s["pm"], 2 * q + 2)
                pe.wait_ge(s["cl"], q + 1)
                open_(3, ("K", q))
                for d in range(2):
                    l0 = 0 if d == 0 else 1
                    for j in range(4):
                        o = PS[32 * j:32 * j + 32, 512 * 3 + 128 * d:512 * 3 + 128 * d + 128]
                        pd = 4 * d + j
                        pe.matmul(o, bdr[:, pd, :], clr[:, pd, l0:l0 + 8, :], start=True, stop=False)
                        ins = pe.matmul(o, bdi[:, pd, :], cli[:, pd, l0:l0 + 8, :], start=False, stop=True)
                close(ins, "s5", ("K", q))
                for part, pm in enumerate((pmr, pmi)):
                    for d in range(2):
                        b = 4 + 2 * part + d
                        open_(b, ("WT", q, part, d))
                        for j in range(4):
                            ins = pe.transpose(bank(b, P, j * P), pm[:, 4 * d + j, :], ident)
                        close(ins, "s5", ("WT", q, part, d))
                if q:
                    s5_out(q - 1, 0)
                for part in range(2):
                    for d in range(2):
                        wait(pe, taken[("WT", q, part, d)])
                        b = 4 + 2 * part + d
                        open_(b, ("S", q, part, d))
                        for j in range(4):
                            for g2 in range(2):
                                o = PS[64 * g2:64 * g2 + 64, 512 * b + NCH * j:512 * b + NCH * (j + 1)]
                                c0 = 0 if d == 0 else NCC
                                ins = pe.matmul(o, WT[:, part, 4 * d + j, 64 * g2:64 * g2 + 64],
                                                U[:, 8 * q + 2 * j + g2, c0:c0 + NCH], start=True, stop=True)
                        close(ins, "s5", ("S", q, part, d))
                if q:
                    s5_out(q - 1, 1)
                ada_group(4 + 2 * q, 1)
                ada_group(5 + 2 * q, 2)
                ada_turned(4 + 2 * q, 0, q == 0)
                ada_turned(5 + 2 * q, 0, False)
                taken["ada1"] = taken[("adaT", 4)]
                ends["ada1"] = ends[("adaT", 5 + 2 * q)]
            s5_out(3, 0)
            s5_out(3, 1)
            pe.wait_ge(ld["ytok"], 16 * TT * 4)
            for k in range(4):
                open_(3 + k, ("yT", k))
                for t in range(TT):
                    ins = pe.transpose(bank(3 + k, P, t * P), y5tok[:, t, k * P:(k + 1) * P], ident)
                close(ins, "glu", ("yT", k))
            pe.wait_ge(s["gtl"], 4)
            for m in range(4):
                c, w = chunk()
                b = 7 * (m % 2)
                open_(b, ("glu", m))
                for k in range(4):
                    ins = mm3(bank(b), (w[0][:, k, :], w[1][:, k, :]), (yg_hi[:, k, :], yg_lo[:, k, :]),
                              k == 0, k == 3)
                close(ins, "glu", ("glu", m))
                ends[("chunk", c)] = ends[("glu", m)]
            merge(1, (o_hi, o_lo), HEADS + 4, hyena_setup)

            pe.wait_ge(s["alt"], 2)

            def taps(it, t):
                if t == 0:
                    pe.wait_ge(s["hid"], 2)
                    pe.wait_ge(ld["w3"], 16 * (it + 1))
                open_(5, ("f", it, t))
                close(pe.matmul(bank(5), hid2[:, t * P:(t + 1) * P], w3[:, :, :], start=True, stop=True),
                      "hy", ("f", it, t))

            def to_tokens_hy(n):
                wait(pe, taken[("hz", n)])
                b = 6 + n % 2
                open_(b, ("ht", n))
                for t in range(TT):
                    ins = pe.transpose(bank(b, P, t * P), tmp[n % 2][:, t * P:(t + 1) * P], ident)
                close(ins, "hy", ("ht", n))

            for n in range(12):
                c, w = chunk()
                open_(n % 4, ("hz", n))
                for k in range(KD):
                    ins = mm3(bank(n % 4), (w[0][:, k, :], w[1][:, k, :]), (h_hi[:, k, :], h_lo[:, k, :]),
                              k == 0, k == KD - 1)
                close(ins, "hy", ("hz", n))
                ends[("chunk", c)] = ends[("hz", n)]
                if 1 <= n <= 8:
                    to_tokens_hy(n - 1)
                if n >= 8:
                    taps(0, n - 8)
            for _ in range(4):
                cc, _w = chunk()
                assert chunks[cc][3] == "const"

            def spectrum(b, x_c, x_s, js):
                for k in range(TT):
                    mm3(bank(b, HC), (fc_hi[:, k, js], fc_lo[:, k, js]), tuple(x[:, k, :] for x in x_c), k == 0, k == 3)
                for k in range(TT):
                    ins = mm3(bank(b, HC, HC), (fs_hi[:, k, js], fs_lo[:, k, js]), tuple(x[:, k, :] for x in x_s),
                              k == 0, k == 3)
                return ins

            def nyquist(x, o):
                for k in range(TT):
                    pe.matmul(bank(4, HC, o), altr[:, :], x[0][:, k, :], start=(k == 0), stop=False)
                    ins = pe.matmul(bank(4, HC, o), altr[:, :], x[1][:, k, :], start=False, stop=(k == 3))
                return ins

            def filter_spectrum(it, j):
                if j == 0:
                    pe.wait_ge(s["hsl"], TT * (it + 1))
                open_(j % 2, ("G", it, j))
                y = ybuf[it]
                close(spectrum(j % 2, [x[:, :, 0:HC] for x in y], [x[:, :, HC:2 * HC] for x in y],
                               slice(j * P, (j + 1) * P)), "hy", ("G", it, j))

            filter_spectrum(0, 0)
            for it, (half, o) in enumerate(CONVS):
                y_hi, y_lo = ybuf[it]
                for j in range(1, 4):
                    filter_spectrum(it, j)
                    if it < 3:
                        taps(it + 1, j - 1)
                open_(4, ("Ny", it))
                close(nyquist([x[:, :, 0:HC] for x in (y_hi, y_lo)], 0), "hy", ("Gn", it))
                if it < 3:
                    taps(it + 1, 3)
                if o == 0:
                    wait(pe, taken[("ht", 2 * half)])
                    wait(pe, taken[("ht", 2 * half + 1)])
                else:
                    pe.wait_ge(s["utl"], TT * (half + 1))
                u = u_hi[half], u_lo[half]
                for j in range(4):
                    b = 2 + j % 2
                    open_(b, ("Us", it, j))
                    close(spectrum(b, u, u, slice(j * P, (j + 1) * P)), "hy", ("Us", it, j))
                close(nyquist(u, HC), "hy", ("Un", it))
                if it < 3:
                    filter_spectrum(it + 1, 0)
                pe.wait_ge(s["ytl"], 4 * (it + 1))
                pe.wait_ge(s["nyq"], it + 1)
                if o == 0:
                    for t in range(TT):
                        b = 6 + t % 2
                        open_(b, ("c", it, t))
                        ts = slice(t * P, (t + 1) * P)
                        for j in range(4):
                            mm3(bank(b, HC), (fc_hi[:, j, ts], fc_lo[:, j, ts]),
                                (y_hi[:, j, 0:HC], y_lo[:, j, 0:HC]), j == 0, False)
                            mm3(bank(b, HC), (fs_hi[:, j, ts], fs_lo[:, j, ts]),
                                (y_hi[:, j, HC:2 * HC], y_lo[:, j, HC:2 * HC]), False, False)
                        pe.matmul(bank(b, HC), alt_row[:, 0:P], nyh[:, :], start=False, stop=False)
                        close(pe.matmul(bank(b, HC), alt_row[:, 0:P], nyl[:, :], start=False, stop=True),
                              "hy", ("c", it, t))
                else:
                    for i in range(2):
                        b = 6 + i
                        open_(b, ("c", it, i))
                        cs, cs2 = slice(i * P, (i + 1) * P), slice(HC + i * P, HC + (i + 1) * P)
                        for j in range(4):
                            mm3(bank(b), (y_hi[:, j, cs], y_lo[:, j, cs]), (fc_hi[:, j, :], fc_lo[:, j, :]),
                                j == 0, False)
                            mm3(bank(b), (y_hi[:, j, cs2], y_lo[:, j, cs2]), (fs_hi[:, j, :], fs_lo[:, j, :]),
                                False, False)
                        pe.matmul(bank(b), nyh[:, cs], alt_row[:, :], start=False, stop=False)
                        close(pe.matmul(bank(b), nyl[:, cs], alt_row[:, :], start=False, stop=True),
                              "hy", ("c", it, i))
            merge(2, (e_hi, e_lo), HEADS + 8)

            pe.wait_ge(ld["x2"], 16)
            for k in range(KD):
                b = 4 + k % 4
                open_(b, ("x2T", k))
                for t in range(TT):
                    ins = pe.transpose(bank(b, P, t * P), x2t[:, t, k * P:(k + 1) * P], ident)
                close(ins, "out", ("x2T", k))

            def square_sum(k):
                if k == 0:
                    open_(4, "ss")
                pe.wait_ge(s["sq2"], k + 1)
                ins = pe.matmul(bank(4), onesq[:, :], sqk[k % 2][:, :], start=(k == 0), stop=(k == KD - 1))
                close(ins, "norm", ("ssk", k))

            for m in range(KD):
                c, w = chunk()
                b = m % 4
                open_(b, ("wo", m))
                for k in range(KD):
                    if m == 0:
                        pe.wait_ge(s["ml"], k + 1)
                    ins = mm3(bank(b), (w[0][:, k, :], w[1][:, k, :]), (m_hi[:, k, :], m_lo[:, k, :]),
                              k == 0, k == KD - 1)
                close(ins, "out", ("wo", m))
                ends[("chunk", c)] = ends[("wo", m)]
                if m:
                    square_sum(m - 1)
            square_sum(KD - 1)
            ends["ss"] = ends[("ssk", KD - 1)]

            for f in range(FT):
                for u in range(2):
                    c, w = chunk()
                    b = (2 * f + u) % 8
                    open_(b, ("gu", f, u))
                    for k in range(KD):
                        if f == 0 and u == 0:
                            pe.wait_ge(s["h2l"], k + 1)
                        ins = mm3(bank(b), (w[0][:, k, :], w[1][:, k, :]), (h_hi[:, k, :], h_lo[:, k, :]),
                                  k == 0, k == KD - 1)
                    close(ins, "up", ("gu", f, u))
                    ends[("chunk", c)] = ends[("gu", f, u)]
            pe.wait_ge(s["atl"], FT)
            for m in range(KD):
                b = m % 4
                open_(b, ("down", m))
                k0 = 0
                for i, kt in enumerate(DOWN):
                    c, w = chunk()
                    for k in range(kt):
                        ins = mm3(bank(b), (w[0][:, k, :], w[1][:, k, :]),
                                  (act_hi[:, k0 + k, :], act_lo[:, k0 + k, :]), k0 + k == 0, k0 + k == FT - 1)
                    k0 += kt
                    close(ins, "down", ("chunk", c))
                ends[("down", m)] = ends[("chunk", c)]
                if m:
                    to_tokens(m - 1)
            to_tokens(KD - 1)
            assert nxt[0] == len(chunks)

        @block.scalar
        def _(act):
            chain = [0]
            settled = [True]

            def after():
                if not settled[0]:
                    act.drain()
                settled[0] = False
                return act

            at = [0]

            def link(ins):
                chain[0] += 1
                ins.then_inc(s_act, 1)
                act.wait_ge(s_act, chain[0])
                settled[0] = True

            def split_to(c1):
                while at[0] <= min(c1, len(chunks) - 1):
                    c = at[0]
                    at[0] += 1
                    _, kt, n, kind, dest = chunks[c]
                    if kind == "plain":
                        continue
                    i = c % RING
                    act.wait_ge(raw_in[i], 16 * (c // RING + 1))
                    if kind == "const":
                        o = dest[0]
                    else:
                        o = whi[i][:, 0:kt * n]
                        if c >= RING and chunks[c - RING][3] != "const":
                            wait(act, ends[("chunk", c - RING)])
                    after().activation(o, raw[i][:, 0:kt * n], ACT.Copy).then_inc(s_hi, 1)

            def phase_end(k):
                act.drain().then_inc(s_phase, 1)
                act.wait_ge(s_phase, 3 * k)

            def copy(o, i):
                return after().activation(o, i, ACT.Copy)

            act.wait_ge(s["vc"], 1)
            after().activation(silc[:, :], vc1[:, 0:16], ACT.Silu).then_inc(s["silu"], 1)
            act.wait_ge(ld["x"], 16)
            act.wait_ge(ld["ctx"], 16)
            for t in range(KT):
                link(after().activation(sq0[:, :], xt[:, t, :], ACT.Square, accum_out=rs[:, 0, 0, t:t + 1]))
            act.drain().then_inc(s["sq"], 1)
            act.wait_ge(s["var"], 1)
            after().activation(rs[:, 0, 2, 0:KT], rs[:, 0, 1, 0:KT], ACT.Sqrt).then_inc(s["sqrt"], 1)

            def ada_rows(g, b):
                wait(act, ends[("ada", g)])
                if g >= 2:
                    wait(act, ends[("adaT", g - 2)])
                copy(tmp[g % 2][0:2, :], bank(b)[0:2]).then_inc(bank_free[b], 1)

            for g in range(4):
                ada_rows(g, 2 + g % 2)
            split_to(19)
            for j in range(2 * KD):
                k, x = j // 2, j % 2
                act.wait_ge(s["htmp"], j + 1)
                o = hc_hi[:, k, :] if x else h_hi[:, k, :]
                copy(o, tmp[j % 2][:, 0:TC if x else T]).then_inc(s["hth"], 1)
            split_to(22)
            for t in range(KT):
                wait(act, ends[("us", t)])
                copy(us[:, t, :], bank(t)).then_inc(bank_free[t], 1)
            act.wait_ge(ld["uch"], 16 * KT)
            copy(uch2[:, :, :, :], uch[:, :, :].rearrange("c s (g m) -> c g s m", g=G)).then_inc(s["us"], 1)
            split_to(23)
            for t in range(KT):
                wait(act, ends[("z", t)])
                if t < TT:
                    link(after().activation(sq1[:, :], bank(t, QL), ACT.Square, accum_out=rs[:, 1, 0, t:t + 1]))
                link(after().activation(sq1[:, 0:KVL], bank(t, KVL, QL), ACT.Square,
                                    accum_out=rs[:, 1, 0, TT + t:TT + t + 1]))
                act.drain().then_inc(s["sq"], 1)
            act.wait_ge(s["var"], 2)
            after().activation(rs[:, 1, 2, 0:10], rs[:, 1, 1, 0:10], ACT.Sqrt).then_inc(s["sqrt"], 1)
            for i in range(8):
                b = 6 + i % 2
                wait(act, ends[("uT", i)])
                src = bank(b, 4 * NCH).rearrange("p (g c) -> p g c", g=4)
                gs = slice(4 * i, 4 * i + 4)
                copy(U[:, gs, NCC:NCC + NCX], src[:, :, 0:NCX])
                copy(U[:, gs, 0:NCC], src[:, :, NCX:NCH])
                copy(U[:, gs, NCC + NCX:P], src[:, :, NCX:NCH]).then_inc(bank_free[b], 1)
            phase_end(1)
            split_to(26)
            for i in range(4):
                act.wait_ge(s["ntmp"], i + 1)
                o = (qnT_hi[:, 0, :], qnT_hi[:, 1, :], kvT_hi[:, 0:T], kvT_hi[:, T:KEYS])[i]
                copy(o, tmp[i % 2][:, 0:TC if i == 3 else T]).then_inc(s["nth"], 1)
            for t in range(TT):
                for hf in range(2):
                    b = 4 + (2 * t + hf) % 4
                    wait(act, ends[("q", t, hf)])
                    copy(qtok[:, t, 4 * hf:4 * hf + 4, :].rearrange("p h d -> p (h d)"), bank(b, 384))\
                        .then_inc(bank_free[b], 1)
            phase_end(2)

            split_to(29)
            for part, (k0, n) in enumerate(((0, T), (T, TC))):
                wait(act, ends[("kr", part)])
                copy(kT_hi[NOPE:QK, k0:k0 + n], bank(part, n)[0:ROPE]).then_inc(s["aqk"], 1)
            def head_in(h):
                wait(act, ends[("qT", h)])
                copy(qT_hi[:, :], bank(0)[0:QK]).then_inc(s["aqk"], 1)
                for part, (k0, n) in enumerate(((0, T), (T, TC))):
                    wait(act, ends[("k", h, part)])
                    copy(kT_hi[0:NOPE, k0:k0 + n], bank(1 + part, n)[0:NOPE]).then_inc(s["aqk"], 1)

            def weighted(h):
                rows = slice(64 * (h % 2), 64 * (h % 2) + 64)
                act.wait_ge(s["oatt"], h + 1)
                copy(o_hi[rows, h // 2, :], tmp[2][rows, :]).then_inc(s["oth"], 1)

            head_in(0)
            for h in range(HEADS):
                for t in range(TT):
                    i = TT * h + t
                    act.wait_ge(s["max"], i + 1)
                    after().activation(prob[:, t, :], bank(4 + 2 * (t % 2), KEYS), ACT.Exp, bias=mx[:, 2 * i + 1:2 * i + 2],
                                       scale=SCALE, accum_out=den[:, 0, h, t:t + 1])\
                        .then_inc(bank_free[4 + 2 * (t % 2)], 1)
                if h + 1 < HEADS:
                    head_in(h + 1)
                act.wait_ge(s["rc"], h + 1)
                if h:
                    wait(act, ends[("rc", h - 1)])
                for t in range(TT):
                    ins = after().activation(tmp[0][:, t * P:(t + 1) * P], ident, ACT.Copy, scale=den[:, 1, h, t:t + 1])
                ins.then_inc(s["diag"], 1)
                for kt in range(KT):
                    wait(act, ends[("pT", h, kt)])
                    o = pTa_hi[:, kt, :] if kt < 4 else pTb_hi[:, kt - 4, :]
                    copy(o, bank((4, 6, 0)[kt % 3])).then_inc(s["pTh"], 1)
                    if kt == 2 and h:
                        weighted(h - 1)
                wait(act, ends[("rc", h)])
                copy(tmp[1][:, :], bank(1)).then_inc(bank_free[1], 1)
                if h % 2 == 0:
                    for b, t0, t1 in ((1, 0, 4), (2, 4, KT)):
                        wait(act, ends[("v", h // 2, b)])
                        copy(v_hi[:, t0:t1, :, 0:VD], bank(b, (t1 - t0) * P).rearrange("p (k g v) -> p k g v", g=2, v=VD))\
                            .then_inc(s["av"], 1)
            weighted(HEADS - 1)

            def s5_setup(step):
                if step == 0:
                    act.wait_ge(ld["s5"], 16 * NS5)
                    after().activation(dt2[:, :], dt2[:, :], ACT.Exp).then_inc(s["s5c"], 1)
                elif step == 1:
                    for part, dst in enumerate((ctr, cti)):
                        for hf in range(2):
                            b = 4 + 2 * part + hf
                            wait(act, ends[("ct", part, hf)])
                            src = bank(b)[0:ST].rearrange("p (a g n) -> p a g n", g=2, n=GC)
                            for g2 in range(2):
                                ins = after().activation(dst[64 * g2:64 * g2 + 64, 16 * hf:16 * hf + 16, :],
                                                         src[:, :, g2, :], ACT.Copy, scale=1.0 - 2.0 * part)
                            ins.then_inc(bank_free[b], 1)
                    act.wait_ge(s["s5a"], 1)
                    link(after().activation(row[:, 6, :], row[:, 8, :], ACT.Exp))
                    link(after().activation(row[:, 7, :], row[:, 9, :], ACT.Sin))
                    after().activation(row[:, 5, :], row[:, 5, :], ACT.Sin).then_inc(s["s5c"], 1)
                elif step == 4:
                    act.wait_ge(s["s5a"], 2)
                    link(after().activation(lt[:, 2, :], lt[:, 2, :], ACT.Exp))
                    link(after().activation(lt[:, 0, :], lt[:, 0, :], ACT.Sin))
                    after().activation(lt[:, 1, :], lt[:, 1, :], ACT.Sin).then_inc(s["s5c"], 1)

            def hyena_setup(step):
                if step in (3, 6):
                    i = step // 3 - 1
                    act.wait_ge(s["hya"], i + 1)
                    after().activation((hid1, hid2)[i][:, :], harg[:, :], ACT.Sin).then_inc(s["hid"], 1)

            def merged_hi(m):
                act.wait_ge(s["mg"], m + 1)
                copy(m_hi[:, m, :], merged[:, m, :]).then_inc(s["mh"], 1)

            def merge(j, c0, between=None):
                for m in range(KD):
                    split_to(c0 + 2 * m + 3)
                    wait(act, ends[("gate", j, m)])
                    if m >= 2:
                        wait(act, taken[("branch", j, m - 2)])
                    after().activation(tmp[m % 2][:, :], bank(2 * (m % 4)), ACT.Sigmoid).then_inc(bank_free[2 * (m % 4)], 1)
                    if between:
                        between(m)

            merge(0, 27, s5_setup)
            phase_end(3)

            def trig(q):
                act.wait_ge(s["angle"], q + 1)
                if q >= 2:
                    act.wait_ge(s["Hs"], 2 * (q - 1))
                after().activation(tsin2[q % 2][:, :, :], ang_s[:, :, :], ACT.Sin)
                after().activation(tcos2[q % 2][:, :, :], ang_c[:, :, :], ACT.Sin).then_inc(s["trig"], 1)

            def s5_out(q, half):
                wait(act, ends[("Y", q, half)])
                if half == 0 and q:
                    act.wait_ge(ld["ytok"], 16 * TT * q)
                src = bank(1 + half)[0:NCX].rearrange("c (g t n) -> c g t n", g=4, t=L)
                o = Y2[:, :, :].rearrange("c t (g two n) -> c two g t n", g=4, two=2)[:, half]
                for g in range(4):
                    ins = copy(o[:, g], src[:, g])
                ins.then_inc(bank_free[1 + half], 1)
                wait(act, taken[("Y", q, half)])
                if half == 1:
                    for t in range(TT):
                        act.dma_start(y5tok[:, t, q * P:(q + 1) * P], Y2[16 * t:16 * t + 16, :, :])\
                            .then_inc(ld["ytok"], 16)

            trig(0)
            for q in range(4):
                for part in range(2):
                    for d in range(2):
                        b = 4 + 2 * part + d
                        wait(act, ends[("WT", q, part, d)])
                        copy(WT[:, part, 4 * d:4 * d + 4, :].rearrange("p a n -> p (a n)"), bank(b))\
                            .then_inc(bank_free[b], 1)
                if q < 3:
                    trig(q + 1)
                if q:
                    s5_out(q - 1, 0)
                    s5_out(q - 1, 1)
                wait(act, taken[("K", q)])
                act.dma_start(scratch[q], K2[:, :, :].rearrange("p l n -> p (l n)")).then_inc(ld["kfilt"], 16)
                act.wait_ge(ld["kfilt"], 16 * (q + 1))
                for st in range(L):
                    act.dma_start(Mt[GC * st:GC * (st + 1), :, :],
                                  scratch[q].rearrange("(g m) c -> m g c", m=GC)[:, :, (7 - st) * GC:(15 - st) * GC])\
                        .then_inc(ld["kread"], 16)
                ada_rows(4 + 2 * q, 1)
                ada_rows(5 + 2 * q, 2)
            s5_out(3, 0)
            s5_out(3, 1)
            for k in range(4):
                wait(act, ends[("yT", k)])
                after().activation(yg[:, k, :], bank(3 + k), ACT.Gelu_apprx_tanh).then_inc(bank_free[3 + k], 1)
                wait(act, taken[("yT", k)])
                copy(yg_hi[:, k, :], yg[:, k, :]).then_inc(s["gth"], 1)
            split_to(78)
            for m in range(4):
                wait(act, ends[("glu", m)])
                after().activation(tmp[m % 2][:, :], bank(7 * (m % 2)), ACT.Sigmoid).then_inc(bank_free[7 * (m % 2)], 1)
                act.wait_ge(s["oun"], m + 1)
                copy(o_hi[:, m, :], yg[:, m, :]).then_inc(s["oth"], 1)
            merge(1, 79, hyena_setup)
            split_to(94)

            wait(act, taken[("branch", 1, KD - 1)])
            def taps_hi(it, t):
                n = TT * it + t
                act.wait_ge(s["hs"], n + 1)
                copy(ybuf[it][0][:, t, :], tmp[t % 2][:, :]).then_inc(s["hsh"], 1)

            def filter_out(it, j):
                wait(act, ends[("G", it, j)])
                if it:
                    act.wait_ge(s["yt"], 4 * (it - 1) + j + 1)
                after().activation(Gs[:, j, :], bank(j % 2), ACT.Identity, scale=cst[:, C_GS + j:C_GS + j + 1])\
                    .then_inc(bank_free[j % 2], 1)

            def tokens_out(n):
                wait(act, ends[("ht", n)])
                part, half, i = n // 4, n % 4 // 2, n % 2
                src = bank(6 + n % 2).rearrange("p (t c) -> p t c", t=TT)
                cs = slice(i * P, (i + 1) * P)
                if part == 0:
                    copy(u_hi[half][:, :, cs], src).then_inc(s["zt"], 1)
                else:
                    copy(g1t[half][:, :, cs], src).then_inc(bank_free[6 + n % 2], 1)

            for n in range(12):
                split_to(95 + n + 2)
                wait(act, ends[("hz", n)])
                if 2 <= n < 8:
                    wait(act, ends[("ht", n - 2)])
                o = tmp[n % 2][:, :] if n < 8 else g2c[n % 4 // 2][:, n % 2, :]
                after().activation(o, bank(n % 4), ACT.Identity, scale=vc2[:, 12 + n:13 + n],
                                   bias=vc1[:, VOFF["hy_conv_b"] + n:VOFF["hy_conv_b"] + n + 1]).then_inc(s["zc"], 1)
                if 1 <= n <= 8:
                    tokens_out(n - 1)
                if n >= 9:
                    taps_hi(0, n - 9)
            taps_hi(0, 3)
            split_to(110)
            filter_out(0, 0)
            for it, (half, o) in enumerate(CONVS):
                y_hi = ybuf[it][0]
                for j in range(1, 4):
                    filter_out(it, j)
                    if it < 3:
                        taps_hi(it + 1, j - 1)
                if it < 3:
                    taps_hi(it + 1, 3)
                for j in range(4):
                    act.wait_ge(s["yt"], 4 * it + j + 1)
                    copy(y_hi[:, j, :], tmp[j % 2][:, :]).then_inc(s["yth"], 1)
                if it < 3:
                    filter_out(it + 1, 0)
                if o == 0:
                    for t in range(TT):
                        act.wait_ge(s["ut"], TT * half + t + 1)
                        copy(u_hi[half][:, t, :], tmp[t % 2][:, 0:HC]).then_inc(s["uth"], 1)
                else:
                    for i in range(2):
                        act.wait_ge(s["oun"], 4 + 2 * half + i + 1)
                        copy(e_hi[:, 2 * half + i, :], tmp[i][:, :]).then_inc(s["oth"], 1)
            merge(2, 111, lambda m: m and merged_hi(m - 1))
            merged_hi(KD - 1)

            for k in range(KD):
                wait(act, ends[("x2T", k)])
                act.wait_ge(s["ml"], k + 1)
                copy(xT[:, k, :], bank(4 + k % 4)).then_inc(bank_free[4 + k % 4], 1)
            for m in range(KD):
                split_to(127 + m + 2)
                wait(act, taken[("wo", m)])
                if m >= 2:
                    wait(act, ends[("ssk", m - 2)])
                after().activation(sqk[m % 2][:, :], xT[:, m, :], ACT.Square).then_inc(s["sq2"], 1)
            act.wait_ge(s["vf"], 1)
            after().activation(srow[:, :], vrow[:, :], ACT.Sqrt).then_inc(s["sf"], 1)
            for k in range(KD):
                act.wait_ge(s["h2t"], k + 1)
                copy(h_hi[:, k, :], tmp[k % 2][:, :]).then_inc(s["h2h"], 1)

            for f in range(FT):
                split_to(135 + 2 * f + 3)
                wait(act, ends[("gu", f, 0)])
                if f >= 3:
                    act.wait_ge(s["atl"], f - 2)
                elif f == 0:
                    act.wait_ge(s["h2l"], KD)
                after().activation(tmp[f % 3][:, :], bank((2 * f) % 8), ACT.Silu).then_inc(bank_free[(2 * f) % 8], 1)
                wait(act, taken[("gu", f, 1)])
                copy(act_hi[:, f, :], tmp[f % 3][:, :]).then_inc(s["ath"], 1)
            for m in range(KD):
                split_to(179 + 4 * m + 6)
                if m:
                    wait(act, ends[("yo", m - 1)])
                    copy(ytok[:, :, (m - 1) * P:m * P], bank(4 + (m - 1) % 4).rearrange("p (t c) -> p t c", t=TT))\
                        .then_inc(bank_free[4 + (m - 1) % 4], 1)
            wait(act, ends[("yo", KD - 1)])
            copy(ytok[:, :, D - P:D], bank(7).rearrange("p (t c) -> p t c", t=TT)).then_inc(bank_free[7], 1)
            wait(act, taken[("yo", KD - 1)])
            for t in range(TT):
                link(after().activation(fsq[:, :], ytok[:, t, :], ACT.Square, accum_out=rs[:, 2, 0, t:t + 1]))
            act.drain().then_inc(s["sq"], 1)
            act.wait_ge(s["var"], 3)
            after().activation(rs[:, 2, 2, 0:TT], rs[:, 2, 1, 0:TT], ACT.Sqrt).then_inc(s["sqrt"], 1)

        @block.vector
        def _(dve):
            chain = [0]
            settled = [True]

            def after():
                if not settled[0]:
                    dve.drain()
                settled[0] = False
                return dve

            at = [0]

            def link(ins):
                chain[0] += 1
                ins.then_inc(s_dve, 1)
                dve.wait_ge(s_dve, chain[0])
                settled[0] = True

            def tt(o, x, y, op):
                return after().tensor_tensor(o, x, y, op)

            def low(o, x, hi_):
                return after().tensor_tensor(o, x, hi_.bitcast(F32), ALU.subtract)

            def split_to(c1):
                while at[0] <= min(c1, len(chunks) - 1):
                    c = at[0]
                    at[0] += 1
                    _, kt, n, kind, dest = chunks[c]
                    if kind == "plain":
                        continue
                    i = c % RING
                    dve.wait_ge(s_hi, nth_split[c] + 1)
                    o, hi_ = (dest[1], dest[0]) if kind == "const" else (wlo[i][:, 0:kt * n], whi[i][:, 0:kt * n])
                    low(o, raw[i][:, 0:kt * n], hi_).then_inc(s_lo, 1)

            def phase_end(k):
                dve.drain().then_inc(s_phase, 1)
                dve.wait_ge(s_phase, 3 * k)

            def refine(v, sq, r_, t_, o):
                link(after().reciprocal(r_, sq))
                link(tt(t_, r_, r_, ALU.mult))
                link(tt(t_, t_, v, ALU.mult))
                link(after().tensor_scalar(t_, t_, -0.5, 1.5, ALU.mult, ALU.add))
                link(tt(o, r_, t_, ALU.mult))

            def reduce_angle(v, n):
                link(after().tensor_scalar(n, v, INV_2PI, ROUND, ALU.mult, ALU.add))
                link(after().tensor_scalar(n, n, ROUND, None, ALU.subtract))
                link(after().scalar_tensor_tensor(v, n, -TWO_PI_HI, v, ALU.mult, ALU.add))
                link(after().scalar_tensor_tensor(v, n, -TWO_PI_LO, v, ALU.mult, ALU.add))
                link(after().tensor_scalar(v, v, PI, -PI, ALU.min, ALU.max))

            wait(dve, ends["vec"])
            after().tensor_copy(vc1[:, :], bank(0, VROWS)).then_inc(s["vc"], 1)
            after().tensor_copy(vc2[:, :], bank(0, 36, 128))
            after().tensor_copy(vc3[:, :], bank(0, 3, 256)[0:64]).then_inc(bank_free[0], 1)
            dve.wait_ge(s["sq"], 1)
            link(after().tensor_scalar(rs[:, 0, 1, 0:KT], rs[:, 0, 0, 0:KT], 1.0 / D, EPS, ALU.mult, ALU.add))
            dve.drain().then_inc(s["var"], 1)
            dve.wait_ge(s["sqrt"], 1)
            refine(rs[:, 0, 1, 0:KT], rs[:, 0, 2, 0:KT], rs[:, 0, 3, 0:KT], rs[:, 0, 4, 0:KT], rs[:, 0, 5, 0:KT])
            for t in range(KT):
                after().tensor_scalar(xt[:, t, :], xt[:, t, :], rs[:, 0, 5, t:t + 1], None, ALU.mult).then_inc(s["xh"], 1)
            wait(dve, ends["ada0"])
            dve.wait_ge(s["vc"], 1)
            pv = bank(1, 32).rearrange("p (m x) -> p m x", x=2)
            ab = vc1[:, VOFF["ada_b"]:VOFF["ada_b"] + 48]
            nm = vc1[:, VOFF["norm_mix"]:VOFF["norm_mix"] + KD]
            link(tt(modx[:, 0:16], pv[:, :, 0], ab[:, 0:16], ALU.add))
            tt(modc[:, :], pv[:, :, 1], ab[:, 0:16], ALU.add).then_inc(bank_free[1], 1)
            wait(dve, taken["ada0"])
            after().scalar_tensor_tensor(amix[:, 0, :], modx[:, 8:16], 1.0, nm, ALU.add, ALU.mult)
            link(after().scalar_tensor_tensor(amix[:, 1, :], modc[:, 8:16], 1.0, nm, ALU.add, ALU.mult))
            split_to(18)

            def low_h(j):
                k, x = j // 2, j % 2
                dve.wait_ge(s["hth"], j + 1)
                n = TC if x else T
                low((hc_lo if x else h_lo)[:, k, :], tmp[j % 2][:, 0:n], (hc_hi if x else h_hi)[:, k, :])\
                    .then_inc(s["htl"], 1)

            for j in range(2 * KD):
                k, x = j // 2, j % 2
                n = TC if x else T
                b = 6 + x
                wait(dve, ends[("xT", k, x)])
                after().tensor_scalar(tmp[j % 2][:, 0:n], bank(b, n), amix[:, x, k:k + 1],
                                  (modc if x else modx)[:, k:k + 1], ALU.mult, ALU.add).then_inc(bank_free[b], 1)
                wait(dve, taken[("xT", k, x)])
                dve.drain().then_inc(s["htmp"], 1)
                if j:
                    low_h(j - 1)
            low_h(2 * KD - 1)
            split_to(23)
            for t in range(KT):
                dve.wait_ge(s["sq"], t + 2)
                o = 0 if t < TT else 256
                after().tensor_copy(ztok[:, t, o:416], bank(t, 416 - o, o)).then_inc(bank_free[t], 1)
            link(after().tensor_scalar(rs[:, 1, 1, 0:TT], rs[:, 1, 0, 0:TT], 1.0 / QL, EPS, ALU.mult, ALU.add))
            link(after().tensor_scalar(rs[:, 1, 1, TT:10], rs[:, 1, 0, TT:10], 1.0 / KVL, EPS, ALU.mult, ALU.add))
            dve.drain().then_inc(s["var"], 1)
            dve.wait_ge(s["sqrt"], 2)
            refine(rs[:, 1, 1, 0:10], rs[:, 1, 2, 0:10], rs[:, 1, 3, 0:10], rs[:, 1, 4, 0:10], rs[:, 1, 5, 0:10])
            for t in range(KT):
                wait(dve, taken[("z", t)])
                if t < TT:
                    after().tensor_scalar(ztok[:, t, 0:QL], ztok[:, t, 0:QL], rs[:, 1, 5, t:t + 1], None, ALU.mult)
                after().tensor_scalar(ztok[:, t, QL:QL + KVL], ztok[:, t, QL:QL + KVL],
                                  rs[:, 1, 5, TT + t:TT + t + 1], None, ALU.mult).then_inc(s["zn"], 1)
            phase_end(1)
            split_to(26)

            def low_n(i):
                dve.wait_ge(s["nth"], i + 1)
                o, hi_ = ((qnT_lo[:, 0, :], qnT_hi[:, 0, :]), (qnT_lo[:, 1, :], qnT_hi[:, 1, :]),
                          (kvT_lo[:, 0:T], kvT_hi[:, 0:T]), (kvT_lo[:, T:KEYS], kvT_hi[:, T:KEYS]))[i]
                low(o, tmp[i % 2][:, 0:TC if i == 3 else T], hi_).then_inc(s["ntl"], 1)

            for i in range(4):
                n = TC if i == 3 else T
                col = VOFF["mla_q_norm"] + i if i < 2 else VOFF["mla_kv_norm"]
                wait(dve, ends[("nT", i)])
                after().tensor_scalar(tmp[i % 2][:, 0:n], bank(i, n), vc1[:, col:col + 1], None, ALU.mult)\
                    .then_inc(bank_free[i], 1)
                wait(dve, taken[("nT", i)])
                dve.drain().then_inc(s["ntmp"], 1)
                if i:
                    low_n(i - 1)
            low_n(3)

            def rotate(x1, x2, cos, sin, n, shape):
                r_ = [x[:, 0:n].rearrange(shape[0], **shape[1]) for x in tmp]
                tt(r_[0], x1, cos, ALU.mult)
                tt(r_[1], x2, sin, ALU.mult)
                link(tt(r_[2], x1, sin, ALU.mult))
                link(tt(x1, r_[0], r_[1], ALU.subtract))
                link(tt(r_[0], x2, cos, ALU.mult))
                link(tt(x2, r_[2], r_[0], ALU.add))

            dve.wait_ge(ld["rope"], 16)
            link(after().tensor_copy(krtok[:, :, :], ztok[:, :, 384:416]))
            rotate(krtok[:, 0:TT, 0::2], krtok[:, 0:TT, 1::2], rope[:, :, 0, :], rope[:, :, 1, :], TT * 16,
                   ("p (t f) -> p t f", {"t": TT}))
            for t in range(TT):
                for hf in range(2):
                    wait(dve, taken[("q", t, hf)])
            shape4 = [P, TT, HEADS, 16]
            rotate(qtok[:, :, :, NOPE:QK:2], qtok[:, :, :, NOPE + 1:QK:2],
                   rope[:, :, 0, :].unsqueeze(2).to_broadcast(shape4), rope[:, :, 1, :].unsqueeze(2).to_broadcast(shape4),
                   T, ("p (t h f) -> p t h f", {"t": TT, "h": HEADS}))
            phase_end(2)

            split_to(29)
            link(after().memset(ones[:, :], 1.0))
            for part, (k0, n) in enumerate(((0, T), (T, TC))):
                dve.wait_ge(s["aqk"], part + 1)
                low(kT_lo[NOPE:QK, k0:k0 + n], bank(part, n)[0:ROPE], kT_hi[NOPE:QK, k0:k0 + n])\
                    .then_inc(bank_free[part], 1)
            def head_in(h):
                dve.wait_ge(s["aqk"], 3 + 3 * h)
                low(qT_lo[:, :], bank(0)[0:QK], qT_hi[:, :]).then_inc(bank_free[0], 1)
                for part, (k0, n) in enumerate(((0, T), (T, TC))):
                    dve.wait_ge(s["aqk"], 4 + 3 * h + part)
                    low(kT_lo[0:NOPE, k0:k0 + n], bank(1 + part, n)[0:NOPE], kT_hi[0:NOPE, k0:k0 + n])\
                        .then_inc(bank_free[1 + part], 1)

            def weighted(h):
                rows = slice(64 * (h % 2), 64 * (h % 2) + 64)
                wait(dve, ends[("o", h)])
                wait(dve, taken[("rc", h)])
                tt(tmp[2][rows, :], bank(3)[rows], tmp[1][rows, :], ALU.mult).then_inc(bank_free[3], 1)
                wait(dve, taken[("o", h)])
                dve.drain().then_inc(s["oatt"], 1)

            def weighted_low(h):
                rows = slice(64 * (h % 2), 64 * (h % 2) + 64)
                dve.wait_ge(s["oth"], h + 1)
                low(o_lo[rows, h // 2, :], tmp[2][rows, :], o_hi[rows, h // 2, :]).then_inc(s["otl"], 1)

            head_in(0)
            for h in range(HEADS):
                for t in range(TT):
                    i = TT * h + t
                    wait(dve, ends[("s", h, t)])
                    link(after().tensor_reduce(mx[:, 2 * i:2 * i + 1], bank(4 + 2 * (t % 2), KEYS), AX.X, ALU.max))
                    after().tensor_scalar(mx[:, 2 * i + 1:2 * i + 2], mx[:, 2 * i:2 * i + 1], -SCALE, None, ALU.mult)\
                        .then_inc(s["max"], 1)
                for t in range(TT):
                    wait(dve, taken[("s", h, t)])
                after().reciprocal(den[:, 1, h, :], den[:, 0, h, :]).then_inc(s["rc"], 1)
                if h + 1 < HEADS:
                    head_in(h + 1)
                if h:
                    weighted(h - 1)
                for kt in range(KT):
                    if kt == 3 and h:
                        weighted_low(h - 1)
                    dve.wait_ge(s["pTh"], KT * h + kt + 1)
                    hi_, lo_ = (pTa_hi, pTa_lo) if kt < 4 else (pTb_hi, pTb_lo)
                    b = (4, 6, 0)[kt % 3]
                    low(lo_[:, kt % 4, :], bank(b), hi_[:, kt % 4, :]).then_inc(bank_free[b], 1)
                if h % 2 == 0:
                    for i, (b, t0, t1) in enumerate(((1, 0, 4), (2, 4, KT))):
                        dve.wait_ge(s["av"], h + i + 1)
                        low(v_lo[:, t0:t1, :, 0:VD], bank(b, (t1 - t0) * P).rearrange("p (k g v) -> p k g v", g=2, v=VD),
                            v_hi[:, t0:t1, :, 0:VD]).then_inc(bank_free[b], 1)
            weighted(HEADS - 1)
            weighted_low(HEADS - 1)

            def s5_setup(step):
                def R(i):
                    return row[:, i, :]

                e9 = cst[:, C_E9:C_E9 + 9].unsqueeze(1).to_broadcast([P, NPD, 9])

                def v9(i):
                    return lt[:, i, :].rearrange("p (a e) -> p a e", e=9)

                def b9(x):
                    return x.unsqueeze(2).to_broadcast([P, NPD, 9])

                if step == 0:
                    dve.wait_ge(ld["s5"], 16 * NS5)
                    dve.wait_ge(s["s5c"], 1)

                    dtb = dt2[:, :].unsqueeze(2).to_broadcast([NPD, 2, 64])
                    link(tt(R(8).rearrange("r (g p) -> r g p", g=2), R(0).rearrange("r (g p) -> r g p", g=2), dtb, ALU.mult))
                    link(tt(R(9).rearrange("r (g p) -> r g p", g=2), R(1).rearrange("r (g p) -> r g p", g=2), dtb, ALU.mult))
                    reduce_angle(R(9), R(4))
                    link(after().tensor_scalar(R(5), R(9), PI / 2, None, ALU.add))
                    reduce_angle(R(5), R(4))
                    dve.drain().then_inc(s["s5a"], 1)
                    link(tt(R(2), R(0), R(0), ALU.mult))
                    link(tt(R(3), R(1), R(1), ALU.mult))
                    link(tt(R(2), R(2), R(3), ALU.add))
                    link(after().reciprocal(R(3), R(2)))
                elif step == 1:
                    dve.wait_ge(s["s5c"], 2)
                    link(tt(R(5), R(6), R(5), ALU.mult))
                    link(after().tensor_scalar(R(5), R(5), 1.0, None, ALU.subtract))
                    link(tt(R(6), R(6), R(7), ALU.mult))
                    link(tt(R(2), R(5), R(0), ALU.mult))
                    link(tt(R(4), R(6), R(1), ALU.mult))
                    link(tt(R(2), R(2), R(4), ALU.add))
                    link(tt(R(10), R(2), R(3), ALU.mult))
                    link(tt(R(2), R(6), R(0), ALU.mult))
                    link(tt(R(4), R(5), R(1), ALU.mult))
                    link(tt(R(2), R(2), R(4), ALU.subtract))
                    link(tt(R(11), R(2), R(3), ALU.mult))
                    dve.drain().then_inc(s["s5row"], 1)
                elif step == 2:
                    wait(dve, ends["s5row"])
                    after().tensor_copy(base4[:, :, :].rearrange("p a n -> p (a n)"), bank(0, 4 * NPD)).then_inc(bank_free[0], 1)
                    wait(dve, taken["s5row"])
                    link(tt(v9(2), b9(base4[:, 0, :]), e9, ALU.mult))
                    link(tt(v9(0), b9(base4[:, 1, :]), e9, ALU.mult))
                    reduce_angle(lt[:, 0, :], lt[:, 3, :])
                    link(after().tensor_copy(th8[:, :], v9(0)[:, :, 8]))
                    link(after().tensor_scalar(lt[:, 1, :], lt[:, 0, :], PI / 2, None, ALU.add))
                    reduce_angle(lt[:, 1, :], lt[:, 3, :])
                    dve.drain().then_inc(s["s5a"], 1)
                elif step == 4:
                    dve.wait_ge(s["s5c"], 3)
                    tt(lpr[:, :, :], v9(2), v9(1), ALU.mult)
                    tt(lpi[:, :, :], v9(2), v9(0), ALU.mult)
                    link(after().tensor_copy(rho8[:, :], v9(2)[:, :, 8]))
                    w1_, w2_ = (lt[:, :, :].rearrange("p i c -> p (i c)")[:, i * T:i * T + T].rearrange("p (a n) -> p a n", n=GC)
                                for i in range(2))

                    def b16(x):
                        return x.unsqueeze(2).to_broadcast([P, NPD, GC])

                    cr_, ci_ = b16(base4[:, 2, :]), b16(base4[:, 3, :])
                    link(tt(w1_, cr_, bld[:, 0], ALU.mult))
                    link(tt(w2_, ci_, bld[:, 1], ALU.mult))
                    link(tt(bbr[:, :, :], w1_, w2_, ALU.subtract))
                    link(tt(w1_, cr_, bld[:, 1], ALU.mult))
                    link(tt(w2_, ci_, bld[:, 0], ALU.mult))
                    link(tt(bbi[:, :, :], w1_, w2_, ALU.add))

            def hyena_setup(step):
                if step == 1:
                    dve.wait_ge(ld["hyp"], 16 * NHYP)
                    after().tensor_copy(altr[:, :], cst[:, C_ALT:C_ALT + P]).then_inc(s["alt"], 1)
                    after().tensor_copy(alt_row[:, :], hrnd[0:1, :]).then_inc(s["alt"], 1)
                    dve.wait_ge(s["alt"], 2)
                elif step in (2, 5):
                    i = step // 3
                    wait(dve, ends[("hid", i)])
                    after().tensor_scalar(harg[:, :], bank(0)[0:64], vc3[:, i:i + 1], vc3[:, 2:3], ALU.add, ALU.mult)\
                        .then_inc(bank_free[0], 1)
                    wait(dve, taken[("hid", i)])
                    reduce_angle(harg[:, :], hrnd[:, :])
                    dve.drain().then_inc(s["hya"], 1)

            def merge(j, c0, between=None):
                for m in range(KD):
                    split_to(c0 + 2 * m + 3)
                    b = 2 * (m % 4)
                    wait(dve, ends[("branch", j, m)])
                    wait(dve, taken[("gate", j, m)])
                    if j == 0:
                        tt(merged[:, m, :], bank(b + 1), tmp[m % 2][:, :], ALU.mult).then_inc(bank_free[b + 1], 1)
                    else:
                        tt(tmp[2][:, :], bank(b + 1), tmp[m % 2][:, :], ALU.mult).then_inc(bank_free[b + 1], 1)
                        wait(dve, taken[("branch", j, m)])
                        link(tt(merged[:, m, :], merged[:, m, :], tmp[2][:, :], ALU.add))
                    if between:
                        between(m)

            merge(0, 27, s5_setup)
            phase_end(3)

            def angles(q):
                kb = cst[:, C_K:C_K + NCH].unsqueeze(1).to_broadcast([P, 4, NCH])
                n = t5w[:, 0:8 * NCH]
                A, B = (x[:, :, :].rearrange("p a c -> p (a c)") for x in (ang_s, ang_c))
                if q:
                    dve.wait_ge(s["trig"], q)
                for d in range(2):
                    tb = th8[:, 16 * d + 4 * q:16 * d + 4 * q + 4].unsqueeze(2).to_broadcast([P, 4, NCH])
                    ins = tt(ang_s[:, 4 * d:4 * d + 4, :], tb, kb, ALU.mult)
                link(ins)
                reduce_angle(A, n)
                link(after().tensor_scalar(B, A, PI / 2, None, ALU.add))
                reduce_angle(B, n)
                dve.drain().then_inc(s["angle"], 1)

            angles(0)
            for q in range(4):
                tsin, tcos = tsin2[q % 2], tcos2[q % 2]
                for d in range(2):
                    gl = slice(16 * d + 4 * q, 16 * d + 4 * q + 4)
                    ds = slice(4 * d, 4 * d + 4)
                    sl = slice(7, None, -1) if d == 0 else slice(0, 8)
                    sh = [P, 4, 8, GC]
                    pr = lpr[:, gl, sl].unsqueeze(3).to_broadcast(sh)
                    pi = lpi[:, gl, sl].unsqueeze(3).to_broadcast(sh)
                    br = bbr[:, gl, :].unsqueeze(2).to_broadcast(sh)
                    bi = bbi[:, gl, :].unsqueeze(2).to_broadcast(sh)
                    x0, x1 = (t[:, 0:512].rearrange("p (a e n) -> p a e n", a=4, e=8) for t in t5)
                    o_r, o_i = (x[:, ds, :].rearrange("p a (e n) -> p a e n", e=8) for x in (pmr, pmi))
                    link(tt(x0, pr, br, ALU.mult))
                    link(tt(x1, pi, bi, ALU.mult))
                    link(tt(pmr[:, ds, :].rearrange("p a m -> p (a m)"), t5[0][:, 0:512], t5[1][:, 0:512], ALU.subtract))
                    link(tt(x0, pr, bi, ALU.mult))
                    link(tt(x1, pi, br, ALU.mult))
                    link(tt(pmi[:, ds, :].rearrange("p a m -> p (a m)"), t5[0][:, 0:512], t5[1][:, 0:512], ALU.add))
                    dve.drain().then_inc(s["pm"], 1)
                if q < 3:
                    angles(q + 1)
                wait(dve, ends[("K", q)])
                if q:
                    dve.wait_ge(ld["kfilt"], 16 * q)
                kf = bank(3, 128).rearrange("p (l n) -> p l n", n=GC)
                kb_ = bank(3, 128, 128).rearrange("p (l n) -> p l n", n=GC)
                dcol = VOFF["s5_d"] + q
                link(after().scalar_tensor_tensor(K2[:, 7, :], cst[:, C_EYE16:C_EYE16 + GC], vc1[:, dcol:dcol + 1],
                                              kf[:, 0, :], ALU.mult, ALU.add))
                link(tt(K2[:, 7, :], kb_[:, 7, :], K2[:, 7, :], ALU.add))
                after().tensor_copy(K2[:, 0:7, :], kb_[:, 0:7, :])
                after().tensor_copy(K2[:, 8:15, :], kf[:, 1:8, :]).then_inc(bank_free[3], 1)
                for d in range(2):
                    gl0 = 16 * d + 4 * q
                    ds = slice(4 * d, 4 * d + 4)
                    wait(dve, ends[("S", q, 1, d)])
                    dve.wait_ge(s["trig"], q + 1)
                    sr, si = (bank(4 + 2 * p_ + d, 4 * NCH).rearrange("p (a c) -> p a c", a=4) for p_ in range(2))
                    if d:
                        sr, si = sr[:, :, ::-1], si[:, :, ::-1]
                    x0, x1 = (t[:, 0:4 * NCH].rearrange("p (a c) -> p a c", a=4) for t in t5)
                    tc_, ts_ = tcos[:, ds, :], tsin[:, ds, :]
                    link(tt(x0, sr, tc_, ALU.mult))
                    link(tt(x1, si, ts_, ALU.mult))
                    link(tt(gr[:, ds, :], x0, x1, ALU.add))
                    tt(x0, si, tc_, ALU.mult).then_inc(bank_free[6 + d], 1)
                    tt(x1, sr, ts_, ALU.mult).then_inc(bank_free[4 + d], 1)
                    wait(dve, taken[("S", q, 0, d)])
                    wait(dve, taken[("S", q, 1, d)])
                    link(tt(gi[:, ds, :], x0, x1, ALU.subtract))
                wait(dve, ends[("S", q, 1, 1)])
                for d in range(2):
                    gl0 = 16 * d + 4 * q
                    ds = slice(4 * d, 4 * d + 4)
                    for j in range(4):
                        rb = rho8[:, gl0 + j:gl0 + j + 1].to_broadcast([P, NCH])
                        for dst, src in ((sgr, gr), (sgi, gi)):
                            ins = after().tensor_tensor_scan(dst[:, 4 * d + j, :], rb, src[:, 4 * d + j, :], 0.0,
                                                         ALU.mult, ALU.add)
                    link(ins)
                    w = slice(NCC - 1, NCH - 1)
                    x0, x1 = (t[:, 0:4 * NCX].rearrange("p (a c) -> p a c", a=4) for t in t5)
                    if q and d == 0:
                        wait(dve, ends[("Y", q - 1, 1)])
                    tc_, ts_ = tcos[:, ds, w], tsin[:, ds, w]
                    a_, b_ = sgr[:, ds, w], sgi[:, ds, w]
                    hr, hi_ = H[:, 0, ds, :], H[:, 1, ds, :]
                    if d:
                        hr, hi_ = hr[:, :, ::-1], hi_[:, :, ::-1]
                    link(tt(x0, a_, tc_, ALU.mult))
                    link(tt(x1, b_, ts_, ALU.mult))
                    link(tt(hr, x0, x1, ALU.subtract))
                    link(tt(x0, a_, ts_, ALU.mult))
                    link(tt(x1, b_, tc_, ALU.mult))
                    tt(hi_, x0, x1, ALU.add).then_inc(s["Hs"], 1)
            wait(dve, ends["ada1"])
            pv = bank(0, 64, 32).rearrange("p (m x) -> p m x", x=2)
            tt(modx[:, 16:48], pv[:, :, 0], ab[:, 16:48], ALU.add).then_inc(bank_free[0], 1)
            wait(dve, taken["ada1"])
            nf = vc1[:, VOFF["norm_ffn"]:VOFF["norm_ffn"] + KD]
            link(after().scalar_tensor_tensor(affn[:, :], modx[:, 32:40], 1.0, nf, ALU.add, ALU.mult))
            for k in range(4):
                dve.wait_ge(s["gth"], k + 1)
                low(yg_lo[:, k, :], yg[:, k, :], yg_hi[:, k, :]).then_inc(s["gtl"], 1)
            split_to(78)
            for m in range(4):
                wait(dve, taken[("glu", m)])
                tt(yg[:, m, :], yg[:, m, :], tmp[m % 2][:, :], ALU.mult).then_inc(s["oun"], 1)
                dve.wait_ge(s["oth"], HEADS + m + 1)
                low(o_lo[:, m, :], yg[:, m, :], o_hi[:, m, :]).then_inc(s["otl"], 1)
            merge(1, 79, hyena_setup)

            def taps_out(it, t):
                n = TT * it + t
                p = tmp[t % 2]
                wait(dve, ends[("f", it, t)])
                dve.wait_ge(ld["win"], 16 * (n + 1))
                tt(tmp[2][:, :], bank(5), win[:, :, :].rearrange("p a c -> p (a c)"), ALU.mult)\
                    .then_inc(bank_free[5], 1)
                wait(dve, taken[("f", it, t)])
                tt(p[:, HC:T], tmp[2][:, 0:HC], tmp[2][:, HC:T], ALU.subtract)
                ins = tt(p[:, 0:HC], tmp[2][:, 0:HC], tmp[2][:, HC:T], ALU.add)
                if t == 0:
                    dve.wait_ge(ld["hyb"], 16 * (it + 1))
                    link(ins)
                    ins = tt(p[0:1, 0:HC], p[0:1, 0:HC], hyb[:, :], ALU.add)
                ins.then_inc(s["hs"], 1)

            def taps_low(it, t):
                dve.wait_ge(s["hsh"], TT * it + t + 1)
                low(ybuf[it][1][:, t, :], tmp[t % 2][:, :], ybuf[it][0][:, t, :]).then_inc(s["hsl"], 1)

            for n in range(12):
                split_to(95 + n + 2)
                z = bank(n % 4)
                dve.wait_ge(s["zc"], n + 1)
                o = tmp[n % 2][:, :] if n < 8 else g2c[n % 4 // 2][:, n % 2, :]
                link(after().scalar_tensor_tensor(o[:, 1:T], z[:, 0:T - 1], vc2[:, n:n + 1], o[:, 1:T],
                                                  ALU.mult, ALU.add))
                after().scalar_tensor_tensor(o[:, 0:T - 1], z[:, 1:T], vc2[:, 24 + n:25 + n], o[:, 0:T - 1],
                                             ALU.mult, ALU.add).then_inc(bank_free[n % 4], 1)
                if 1 <= n <= 4:
                    v = n - 1
                    cs = slice(v % 2 * P, (v % 2 + 1) * P)
                    dve.wait_ge(s["zt"], n)
                    low(u_lo[v // 2][:, :, cs], bank(6 + v % 2).rearrange("p (t c) -> p t c", t=TT),
                        u_hi[v // 2][:, :, cs]).then_inc(bank_free[6 + v % 2], 1)
                if n >= 9:
                    taps_low(0, n - 9)
                if n >= 8:
                    if n in (8, 9):
                        wait(dve, ends[("ht", n - 2)])
                    taps_out(0, n - 8)
            taps_low(0, 3)
            split_to(110)
            for it, (half, o) in enumerate(CONVS):
                y_hi, y_lo = ybuf[it]
                if it < 3:
                    for t in range(TT):
                        taps_out(it + 1, t)
                        if t:
                            taps_low(it + 1, t - 1)
                    taps_low(it + 1, 3)

                def product_low(j):
                    dve.wait_ge(s["yth"], 4 * it + j + 1)
                    low(y_lo[:, j, :], tmp[j % 2][:, :], y_hi[:, j, :]).then_inc(s["ytl"], 1)

                for j in range(4):
                    b, p = 2 + j % 2, tmp[j % 2]
                    wait(dve, ends[("Us", it, j)])
                    wait(dve, taken[("G", it, j)])
                    g = Gs[:, j, :].rearrange("p (r c) -> p r c", r=2)
                    uu = bank(b).rearrange("p (r c) -> p r c", r=2)
                    tt(p[:, :], bank(b), Gs[:, j, :], ALU.mult)
                    tt(tmp[2][:, :].rearrange("p (r c) -> p r c", r=2), uu, g[:, ::-1, :], ALU.mult)\
                        .then_inc(bank_free[b], 1)
                    wait(dve, taken[("Us", it, j)])
                    tt(p[:, 0:HC], p[:, 0:HC], p[:, HC:T], ALU.subtract)
                    tt(p[:, HC:T], tmp[2][:, 0:HC], tmp[2][:, HC:T], ALU.add).then_inc(s["yt"], 1)
                    if j:
                        product_low(j - 1)
                wait(dve, ends[("Un", it)])
                link(after().tensor_scalar(nyg[:, :], bank(4, HC)[0:1], 1.0 / 1024, None, ALU.mult))
                tt(nyg[:, :], bank(4, HC, HC)[0:1], nyg[:, :], ALU.mult).then_inc(bank_free[4], 1)
                wait(dve, taken[("Ny", it)])
                if it:
                    wait(dve, ends[("c", it - 1, TT - 1 if it < 3 else 1)])
                link(after().tensor_copy(nyh[:, :], nyg[:, :]))
                low(nyl[:, :], nyg[:, :], nyh[:, :]).then_inc(s["nyq"], 1)
                product_low(3)
                if o == 0:
                    def signal_low(t):
                        dve.wait_ge(s["uth"], TT * half + t + 1)
                        low(u_lo[half][:, t, :], tmp[t % 2][:, 0:HC], u_hi[half][:, t, :]).then_inc(s["utl"], 1)

                    for t in range(TT):
                        b = 6 + t % 2
                        wait(dve, ends[("c", it, t)])
                        tt(tmp[t % 2][:, 0:HC], bank(b, HC), g1t[half][:, t, :], ALU.mult).then_inc(bank_free[b], 1)
                        wait(dve, taken[("c", it, t)])
                        dve.drain().then_inc(s["ut"], 1)
                        if t:
                            signal_low(t - 1)
                    signal_low(3)
                else:
                    for i in range(2):
                        wait(dve, ends[("c", it, i)])
                        tt(tmp[i][:, :], bank(6 + i), g2c[half][:, i, :], ALU.mult).then_inc(bank_free[6 + i], 1)
                        wait(dve, taken[("c", it, i)])
                        dve.drain().then_inc(s["oun"], 1)
                        dve.wait_ge(s["oth"], HEADS + 4 + 2 * half + i + 1)
                        low(e_lo[:, 2 * half + i, :], tmp[i][:, :], e_hi[:, 2 * half + i, :])\
                            .then_inc(s["otl"], 1)
            def merged_low(m):
                dve.wait_ge(s["mh"], m + 1)
                low(m_lo[:, m, :], merged[:, m, :], m_hi[:, m, :]).then_inc(s["ml"], 1)

            def merged_out(m):
                dve.drain().then_inc(s["mg"], 1)
                if m:
                    merged_low(m - 1)

            merge(2, 111, merged_out)
            merged_low(KD - 1)

            link(after().memset(onesq[:, :], 1.0))
            for m in range(KD):
                split_to(127 + m + 2)
                wait(dve, ends[("wo", m)])
                wait(dve, taken[("x2T", m)])
                after().scalar_tensor_tensor(xT[:, m, :], bank(m % 4), modx[:, 16 + m:17 + m], xT[:, m, :],
                                         ALU.mult, ALU.add).then_inc(bank_free[m % 4], 1)
            wait(dve, ends["ss"])
            after().tensor_scalar(vrow[:, :], bank(4), 1.0 / D, EPS, ALU.mult, ALU.add).then_inc(bank_free[4], 1)
            wait(dve, taken["ss"])
            dve.drain().then_inc(s["vf"], 1)
            dve.wait_ge(s["sf"], 1)
            refine(vrow[:, :], srow[:, :], sqk[0][:, :], sqk[1][:, :], srow[:, :])

            def low_h2(k):
                dve.wait_ge(s["h2h"], k + 1)
                low(h_lo[:, k, :], tmp[k % 2][:, :], h_hi[:, k, :]).then_inc(s["h2l"], 1)

            for k in range(KD):
                link(tt(tmp[k % 2][:, :], xT[:, k, :], srow[:, :], ALU.mult))
                after().tensor_scalar(tmp[k % 2][:, :], tmp[k % 2][:, :], affn[:, k:k + 1], modx[:, 24 + k:25 + k],
                                  ALU.mult, ALU.add).then_inc(s["h2t"], 1)
                if k:
                    low_h2(k - 1)
            low_h2(KD - 1)

            for f in range(FT):
                split_to(135 + 2 * f + 3)
                wait(dve, ends[("gu", f, 1)])
                wait(dve, taken[("gu", f, 0)])
                b = (2 * f + 1) % 8
                tt(tmp[f % 3][:, :], bank(b), tmp[f % 3][:, :], ALU.mult).then_inc(bank_free[b], 1)
                dve.wait_ge(s["ath"], f + 1)
                low(act_lo[:, f, :], tmp[f % 3][:, :], act_hi[:, f, :]).then_inc(s["atl"], 1)
            for m in range(KD):
                split_to(179 + 4 * m + 6)
                wait(dve, ends[("down", m)])
                after().scalar_tensor_tensor(xT[:, m, :], bank(m % 4), modx[:, 40 + m:41 + m], xT[:, m, :],
                                         ALU.mult, ALU.add).then_inc(bank_free[m % 4], 1)
            dve.wait_ge(s["sq"], 8)
            link(after().tensor_scalar(rs[:, 2, 1, 0:TT], rs[:, 2, 0, 0:TT], 1.0 / D, EPS, ALU.mult, ALU.add))
            dve.drain().then_inc(s["var"], 1)
            dve.wait_ge(s["sqrt"], 3)
            refine(rs[:, 2, 1, 0:TT], rs[:, 2, 2, 0:TT], rs[:, 2, 3, 0:TT], rs[:, 2, 4, 0:TT], rs[:, 2, 5, 0:TT])
            dve.wait_ge(ld["fnorm"], 16)
            for t in range(TT):
                after().scalar_tensor_tensor(ytok[:, t, :], ytok[:, t, :], rs[:, 2, 5, t:t + 1], fnorm[:, :],
                                         ALU.mult, ALU.mult).then_inc(s["fin"], 1)

        @block.gpsimd
        def _(pool):
            def product(o, x, y, op=ALU.mult):
                pool.drain()
                return pool.tensor_tensor(o, x, y, op)

            pool.wait_ge(s_phase, 9)
            pool.memset(bdr[:, :, :], 0.0)
            pool.memset(bdi[:, :, :], 0.0)
            for q in range(4):
                clr, cli = clr2[q % 2], cli2[q % 2]
                if q:
                    wait(pool, ends[("K", q - 1)])
                for d in range(2):
                    gl, ds = slice(16 * d + 4 * q, 16 * d + 4 * q + 4), slice(4 * d, 4 * d + 4)
                    for dst, src in ((bdr, bbr), (bdi, bbi)):
                        pool.drain()
                        pool.tensor_copy(dst[0:64, ds, 0:GC], src[0:64, gl, :])
                        pool.tensor_copy(dst[64:P, ds, GC:2 * GC], src[64:P, gl, :])
                if q >= 2:
                    wait(pool, ends[("Y", q - 2, 1)])
                for d in range(2):
                    gl, ds = slice(16 * d + 4 * q, 16 * d + 4 * q + 4), slice(4 * d, 4 * d + 4)
                    sl = slice(0, 9) if d == 0 else slice(None, None, -1)
                    sh = [P, 4, 9, GC]
                    pr = lpr[:, gl, sl].unsqueeze(3).to_broadcast(sh)
                    pi = lpi[:, gl, sl].unsqueeze(3).to_broadcast(sh)
                    cr = ctr[:, gl, :].unsqueeze(2).to_broadcast(sh)
                    ci = cti[:, gl, :].unsqueeze(2).to_broadcast(sh)
                    x0, x1 = (t[:, :, :, :] for t in t5g)
                    product(x0, pr, cr)
                    product(x1, pi, ci)
                    product(clr[:, ds], x0, x1, ALU.add)
                    product(x0, pr, ci)
                    product(x1, pi, cr)
                    product(cli[:, ds], x0, x1, ALU.subtract)
                pool.drain().then_inc(s["cl"], 1)

        @block.sync
        def _(sp):
            at = [0]

            def load(o, i, which, n=16):
                sp.dma_start(o, i).then_inc(ld[which], 16)

            def ring_to(c1):
                while at[0] <= min(c1, len(chunks) - 1):
                    c = at[0]
                    at[0] += 1
                    src, kt, n, kind, dest = chunks[c]
                    i = c % RING
                    if c >= RING:
                        p = c - RING
                        if chunks[p][3] == "plain":
                            wait(sp, ends[("chunk", p)])
                        else:
                            sp.wait_ge(s_lo, nth_split[p] + 1)
                    sp.dma_start(raw[i][:, 0:kt * n].rearrange("p (k n) -> p k n", k=kt), src).then_inc(raw_in[i], 16)

            load(cst[:, :], a["cst"], "small")
            for name, rows in VECS:
                o = VOFF[name]
                src = a[name]
                load(vr1[o:o + rows, :], src.rearrange("(r p) -> r p", p=P), "small")
            load(vr2[:, :], a["hy_conv_w"].rearrange("j (r p) -> (j r) p", p=P), "small")
            for i, name in enumerate(("hy_f_b1", "hy_f_b2", "hy_f_freq")):
                load(vr3[i:i + 1, :], a[name].rearrange("(r p) -> r p", p=64), "small")
            load(xt[:, 0:TT, :], a["x"].rearrange("(t p) d -> p t d", p=P), "x")
            load(xt[:, TT:KT, :], a["ctx"].rearrange("(t p) d -> p t d", p=P), "ctx")
            ring_to(23)
            for t in range(KT):
                wait(sp, taken[("us", t)])
                load(uch[16 * t:16 * t + 16, :, :], us[:, t, :], "uch")
            wait(sp, ends[("us", KT - 1)])
            sp.wait_ge(s["htl"], 2 * KD)
            load(rope[:, :, :, :], a["rope"].rearrange("(t p) x f -> p t x f", p=P), "rope")
            ring_to(29)
            sp.wait_ge(s["otl"], HEADS)
            load(row[:, 0, :], a["s5_lam_re"], "s5")
            load(row[:, 1, :], a["s5_lam_im"], "s5")
            load(dt2[:, :], a["s5_log_dt"], "s5")
            for part, name in enumerate(("s5_b_re", "s5_b_im")):
                load(bld[:, part], a[name], "s5")
            for part, name in enumerate(("s5_c_re", "s5_c_im")):
                load(cld[:, part], a[name], "s5")
            ring_to(82)
            sp.wait_ge(s["otl"], HEADS + 4)
            load(w12[0:33, 0, :], a["hy_f_w1"], "hyp")
            load(w12[:, 1, :], a["hy_f_w2"], "hyp")
            load(zpos[:, :], a["zpos"], "hyp")
            load(hrnd[0:1, :], a["alt_row"], "hyp")
            ring_to(98)
            for it, (half, o) in enumerate(CONVS):
                hs = slice(half * HC, (half + 1) * HC)
                if it:
                    wait(sp, ends[("f", it - 1, TT - 1)])
                    sp.wait_ge(s["hs"], TT * (it - 1) + 1)
                load(w3[:, :, :], a["hy_f_w3"].rearrange("h (o d c) -> h o d c", o=2, d=2)[:, o, :, hs], "w3")
                load(hyb[:, :], a["hy_bias"][o:o + 1, hs], "hyb")
                for t in range(TT):
                    n = TT * it + t
                    if n:
                        sp.wait_ge(s["hs"], n)
                    load(win[:, :, :], a["window"][t * P:(t + 1) * P].rearrange("p (o d c) -> p o d c", o=2, d=2)
                         [:, o, :, hs], "win")
                    if n == 0:
                        ring_to(110)
                if it == 0:
                    ring_to(114)
            wait(sp, taken[("c", 3, 1)])
            load(x2t[:, :, :], a["x"].rearrange("(t p) d -> p t d", p=P), "x2")
            ring_to(len(chunks) - 1)
            wait(sp, ends[("gu", FT - 1, 1)])
            load(fnorm[:, :], a["final_norm"].rearrange("(r n) -> r n", r=1).to_broadcast([P, D]), "fnorm")
            for t in range(TT):
                sp.wait_ge(s["fin"], t + 1)
                load(out[t * P:(t + 1) * P, :], ytok[:, t, :], "out")
            sp.wait_ge(ld["out"], 16 * TT)


def _constants():
    import math

    import numpy as np
    c = np.zeros((P, C_N), np.float64)
    c[:, C_ID:C_ID + P] = np.eye(P)
    c[:, C_EYE16:C_EYE16 + GC] = np.tile(np.eye(GC), (P // GC, 1))
    c[:, C_GS:C_GS + 4] = 2.0 / 1024
    c[0, C_GS] = 1.0 / 1024
    c[:, C_ALT:C_ALT + P] = np.where(np.arange(P) % 2, -1.0, 1.0)[:, None]
    c[:, C_E9:C_E9 + 9] = np.arange(9)
    c[:, C_K:C_K + NCH] = np.arange(1, NCH + 1)
    n = np.arange(T)
    ang = 2 * np.pi * (np.outer(n, n) % 1024) / 1024
    t = np.linspace(0.0, 1.0, T)[:, None]
    w = 2 * np.pi * n[:, None] / T
    bands = np.linspace(1e-4, 15, 16)[None, :]
    zpos = np.concatenate([t, np.cos(bands * w), -np.sin(bands * w)], axis=-1).T
    deltas = np.abs(np.linspace(math.log(1e-2) / 0.3, math.log(1e-2) / 1.5, 4 * W5))
    window = np.exp(-t * deltas) + 0.05
    inv = 10000.0 ** (-np.arange(8) / 8)
    ang2 = np.concatenate([(n // 64)[:, None] * inv, (n % 64)[:, None] * inv], axis=-1)
    rope = np.stack([np.cos(ang2), np.sin(ang2)], axis=1)
    alt = np.where(n % 2, -1.0, 1.0)[None, :]
    got = {"cst": c, "dft_cos": np.cos(ang), "dft_sin": -np.sin(ang), "zpos": zpos, "window": window,
           "rope": rope, "alt_row": alt}
    return {k: np.ascontiguousarray(v.astype(np.float32)) for k, v in got.items()}


def make(nc, arrays, dt_of):
    a = {}
    for name, v in arrays.items():
        ap = nc.dram_tensor("in_" + name, v.shape, dt_of(v.dtype), kind="ExternalInput").ap()
        a[name] = ap
    for name in list(a):
        if name in ("x", "ctx", "c"):
            a[name] = a[name][0]
        elif len(a[name].shape) > 1 and name not in ("cst", "dft_cos", "dft_sin", "zpos", "window", "rope", "alt_row"):
            a[name] = a[name][0]
    for name in ("s5_lam_re", "s5_lam_im"):
        a[name] = a[name].rearrange("d (a g) p -> (d a) (g p)", g=2)
    a["s5_log_dt"] = a["s5_log_dt"].rearrange("d (a g) -> (d a) g", g=2)
    for name in ("s5_b_re", "s5_b_im"):
        a[name] = a[name].rearrange("d (a g) p n -> (g p) (d a) n", g=2)
    for name in ("s5_c_re", "s5_c_im"):
        a[name] = a[name].rearrange("d (b r) n p -> (r n) (d b) p", r=8)
    scratch = nc.dram_tensor("lag_kernels", (4, P, 15 * GC), F32, kind="Internal").ap()
    out = nc.dram_tensor("out_x", (1, T, D), F32, kind="ExternalOutput").ap()
    build(nc, a, scratch, out[0])


def kernel(**inputs):
    import numpy as np
    from concourse import bacc
    from concourse.bass_utils import run_bass_kernel_spmd

    nc = bacc.Bacc("TRN2", target_bir_lowering=False, num_devices=1)
    arrays = {k: np.ascontiguousarray(v) for k, v in inputs.items()}
    arrays.update(_constants())
    make(nc, arrays, mybir.dt.from_np)
    r = run_bass_kernel_spmd(nc, [{"in_" + k: v for k, v in arrays.items()}], core_ids=[0])
    return r.results[0]["out_x"]
```

```python
from contextlib import ExitStack

import concourse.bass as bass
from concourse import mybir

F32 = mybir.dt.float32
F32R = mybir.dt.float32r
ACT = mybir.ActivationFunctionType
ALU = mybir.AluOpType
AX = mybir.AxisListType

P = 128
D = 1024
KD = D // P
T = 512
TT = T // P
TC = 256
TTC = TC // P
EPS = 1e-6
HEADS, NOPE, ROPE, VD = 8, 64, 32, 64
QK = NOPE + ROPE
QL, KVL = 256, 128
KEYS = T + TC
KT = KEYS // P
SCALE = float(QK) ** -0.5
G, GC, ST = 32, 16, 64
PAIRS = G // 2
L = 8
NCX, NCC = T // L, TC // L
NCH = NCX + NCC
W5 = 512
HC = 256
CONVS = [(0, 0), (1, 0), (0, 1), (1, 1)]
FF = 2816
FT = FF // P
O_KV, O_KR, O_S5, O_HY, O_GATE = 256, 384, 416, 928, 2464
IN_W = 5536
TWO_PI_HI = 6.28125
TWO_PI_LO = 0.0019353071795864769
INV_2PI = 0.15915494309189535
ROUND = 12582912.0
PI = 3.1415925

C_ID, C_EYE16, C_GS, C_ALT, C_E9, C_K = 0, 128, 144, 148, 276, 285
C_N = C_K + NCH

VECS = [("c", 8), ("c_ctx", 8), ("norm_mix", 8), ("norm_ffn", 8), ("final_norm", 8), ("ada_b", 48),
        ("mla_q_norm", 2), ("mla_kv_norm", 1), ("s5_d", 4), ("hy_conv_b", 12)]
VOFF = {}
_at = 0
for _n, _r in VECS:
    VOFF[_n] = _at
    _at += _r
VROWS = _at


NSMALL = 1 + len(VECS) + 1 + 3
NS5 = 3 + 2 + 2
NHYP = 4


def build(nc, a, scratch, out):
    base = (nc.sbuf_base + 31) // 32 * 32
    ctx = ExitStack()
    with ctx:
        def sem(name):
            return ctx.enter_context(nc.semaphore(name))

        class Region:

            def __init__(self, start, end):
                self.at, self.end = start, end

            def __call__(self, name, shape, dt=F32):
                n = 4
                for s in shape[1:]:
                    n *= s
                n = (n + 31) // 32 * 32
                t = nc.alloc_sbuf_tensor_at(name, shape, dt, offset=base + self.at)
                self.at += n
                assert self.at <= self.end, (name, self.at, self.end)
                return t

        PS = ctx.enter_context(nc.psum_tensor("PS", [P, 8 * 512], F32))

        def bank(b, n=512, o=0):
            return PS[:, 512 * b + o:512 * b + o + n]

        K = 1024
        r = Region(0, 14 * K)
        cst = r("cst", [P, C_N])
        ident = cst[:, C_ID:C_ID + P]
        vc1 = r("vc1", [P, VROWS])
        vc2 = r("vc2", [P, 36])
        vc3 = r("vc3", [64, 3])
        modx = r("modx", [P, 48])
        modc = r("modc", [P, 16])
        amix = r("amix", [P, 2, KD])
        affn = r("affn", [P, KD])
        silc = r("silc", [P, 16])
        rs = r("rs", [P, 3, 6, 16])
        altr = r("altr", [P, P], F32R)
        alt_row = r("alt_row", [1, T], F32R)
        tmp = [r(f"tmp{i}", [P, T]) for i in range(3)]
        nyl = r("nyl", [1, HC], F32R)
        junk = r("junk", [1, 8])
        mx = r("mx", [P, 2 * TT * HEADS])
        ones = r("ones", [P, P])
        RING = 4
        r = Region(14 * K, 62 * K)
        raw = [r(f"raw{i}", [P, 1024]) for i in range(RING)]
        whi = [r(f"whi{i}", [P, 1024], F32R) for i in range(RING)]
        wlo = [r(f"wlo{i}", [P, 1024], F32R) for i in range(RING)]
        r = Region(62 * K, 94 * K)
        h_hi = r("h_hi", [P, KD, T], F32R)
        h_lo = r("h_lo", [P, KD, T], F32R)
        r = Region(62 * K, 94 * K)
        ytok = r("ytok", [P, TT, D])
        fnorm = r("fnorm", [P, D])
        fsq = r("fsq", [P, P])
        fsum = r("fsum", [P, TT, KD])
        Z = 94 * K
        ZEND = 207 * K + 512
        r = Region(Z + 97 * K, ZEND)
        U = r("U", [P, G, P])
        r = Region(Z + 81 * K, Z + 97 * K)
        o_hi = r("o_hi", [P, TT, T], F32R)
        o_lo = r("o_lo", [P, TT, T], F32R)
        r = Region(Z, Z + 81 * K)
        hc_hi = r("hc_hi", [P, KD, TC], F32R)
        hc_lo = r("hc_lo", [P, KD, TC], F32R)
        a_at = r.at
        vr1 = r("vr1", [VROWS, P])
        vr2 = r("vr2", [36, P])
        vr3 = r("vr3", [3, 64])
        xt = r("xt", [P, TT + TTC, D])
        ada = [r(f"ada{i}", [P, KD, P]) for i in range(3)]
        sq0 = r("sq0", [P, D])
        r = Region(a_at, Z + 81 * K)
        us = r("us", [P, KT, W5])
        uch = r("uch", [NCH, L, W5])
        uch2 = r("uch2", [NCH, G, L, GC])
        c_at = r.at
        r = Region(a_at, Z + 81 * K)
        qtok = r("qtok", [P, TT, HEADS, QK])
        kvT_hi = r("kvT_hi", [P, KEYS], F32R)
        kvT_lo = r("kvT_lo", [P, KEYS], F32R)
        krtok = r("krtok", [P, KT, ROPE])
        b_at = r.at
        r = Region(c_at, Z + 97 * K)
        rope = r("rope", [P, TT, 2, 16])
        ztok = r("ztok", [P, KT, 416])
        qnT_hi = r("qnT_hi", [P, 2, T], F32R)
        qnT_lo = r("qnT_lo", [P, 2, T], F32R)
        sq1 = r("sq1", [P, 256])
        r = Region(b_at, Z + 81 * K)
        prob = r("prob", [P, TT, KEYS])
        kT2 = [(r(f"kT_hi{i}", [QK, KEYS], F32R), r(f"kT_lo{i}", [QK, KEYS], F32R)) for i in range(2)]
        qT2 = [(r(f"qT_hi{i}", [QK, T], F32R), r(f"qT_lo{i}", [QK, T], F32R)) for i in range(2)]
        v_hi = r("v_hi", [P, KT, 2, VD], F32R)
        v_lo = r("v_lo", [P, KT, 2, VD], F32R)
        den = r("den", [P, 2, HEADS, TT])
        b_at_end = r.at
        r = Region(Z, a_at)
        pTa_hi = r("pTa_hi", [P, 4, T], F32R)
        pTa_lo = r("pTa_lo", [P, 4, T], F32R)
        r = Region(b_at_end, Z + 81 * K)
        pTb_hi = r("pTb_hi", [P, 2, T], F32R)
        pTb_lo = r("pTb_lo", [P, 2, T], F32R)
        r = Region(Z, Z + 16 * K)
        merged = r("merged", [P, KD, T])
        r = Region(Z + 16 * K, Z + 81 * K)
        NPD = 2 * PAIRS
        lpr = r("lpr", [P, NPD, 9])
        lpi = r("lpi", [P, NPD, 9])
        th8 = r("th8", [P, NPD])
        rho8 = r("rho8", [P, NPD])
        base4 = r("base4", [P, 4, NPD])
        bbr = r("bbr", [P, NPD, GC])
        bbi = r("bbi", [P, NPD, GC])
        ctr = r("ctr", [P, NPD, GC])
        cti = r("cti", [P, NPD, GC])
        y5tok = r("y5tok", [P, TT, W5])
        s5_at = r.at
        row = r("row", [NPD, 12, P])
        dt2 = r("dt2", [NPD, 2])
        bld = r("bld", [P, 2, NPD, GC])
        cld = r("cld", [P, 2, 8, ST])
        lt = r("lt", [P, 4, NPD * 9])
        r = Region(r.at, Z + 81 * K)
        clr0, cli0 = r("clr0", [P, 8, 9, GC]), r("cli0", [P, 8, 9, GC])
        t5g = [r(f"t5g_{i}", [P, 4, 9, GC]) for i in range(2)]
        bdr = r("bdr", [P, 8, 32])
        bdi = r("bdi", [P, 8, 32])
        ang_s, ang_c = (r(n, [P, 8, NCH]) for n in ("ang_s", "ang_c"))
        t5w = r("t5", [P, 2 * 4 * 9 * GC])
        t5 = [t5w[:, i * 4 * 9 * GC:(i + 1) * 4 * 9 * GC] for i in range(2)]
        r = Region(r.at, Z + 97 * K)
        Mt = r("Mt", [P, 8, P])
        sgr = r("sgr", [P, 8, NCH])
        sgi = r("sgi", [P, 8, NCH])
        H = r("H", [P, 2, 8, NCX])
        r = Region(s5_at, s5_at + 18 * K)
        pmr = r("pmr", [P, 8, P])
        pmi = r("pmi", [P, 8, P])
        WT = r("WT", [P, 2, 8, P])
        K2 = r("K2", [P, 15, GC])
        r = Region(30 * K, 62 * K)
        clr2, cli2 = [clr0, r("clr1", [P, 8, 9, GC])], [cli0, r("cli1", [P, 8, 9, GC])]
        tsin2, tcos2 = ([r(f"{n}{i}", [P, 8, NCH]) for i in range(2)] for n in ("tsin", "tcos"))
        gr = r("gr", [P, 8, NCH])
        gi = r("gi", [P, 8, NCH])
        Y2 = r("Y2", [NCX, L, P])
        r = Region(s5_at, Z + 81 * K)
        yg = r("yg", [P, TT, T])
        yg_hi = r("yg_hi", [P, TT, T], F32R)
        yg_lo = r("yg_lo", [P, TT, T], F32R)
        r = Region(Z + 16 * K, ZEND)
        fc_hi = r("fc_hi", [P, 4, T], F32R)
        fc_lo = r("fc_lo", [P, 4, T], F32R)
        fs_hi = r("fs_hi", [P, 4, T], F32R)
        fs_lo = r("fs_lo", [P, 4, T], F32R)
        e_at = r.at
        e_hi = r("e_hi", [P, TT, T], F32R)
        e_lo = r("e_lo", [P, TT, T], F32R)
        u_hi, u_lo, g1t, g2c = [], [], [], []
        for half in range(2):
            u_hi.append(r(f"u_hi{half}", [P, TT, HC], F32R))
            u_lo.append(r(f"u_lo{half}", [P, TT, HC], F32R))
            g1t.append(r(f"g1t{half}", [P, TT, HC]))
            g2c.append(r(f"g2c{half}", [P, 2, T]))
        Gs = r("Gs", [P, 4, 2 * HC])
        hid2 = r("hid2", [64, T])
        w3 = r("w3", [64, 2, HC])
        win = r("win", [P, 2, HC])
        nyg = r("nyg", [1, HC])
        nyh = r("nyh", [1, HC], F32R)
        hyb = r("hyb", [1, HC])
        ybuf = []
        for i, at_ in enumerate((e_at, 30 * K, 46 * K)):
            r = Region(at_, at_ + 16 * K)
            ybuf.append((r(f"y_hi{i}", [P, TT, 2 * HC], F32R), r(f"y_lo{i}", [P, TT, 2 * HC], F32R)))
        ybuf.append(ybuf[1])
        r = Region(e_at, e_at + 16 * K)
        hid1 = r("hid1", [64, T])
        harg = r("harg", [64, T])
        hrnd = r("hrnd", [64, T])
        zpos = r("zpos", [33, T])
        w12 = r("w12", [64, 2, 64])
        wins = [win, Region(60 * K, 62 * K)("win_b", [P, 2, HC]), Region(e_at + 14 * K, e_at + 16 * K)("win_e", [P, 2, HC])]

        def window(n):
            if n < 4 or n % 2 == 0:
                return wins[0], "win", n if n < 4 else 4 + (n - 4) // 2
            return wins[1 if n < 8 else 2], "win2", (n - 5) // 2

        r = Region(Z + 16 * K, Z + 104 * K)
        act_hi = r("act_hi", [P, FT, T], F32R)
        act_lo = r("act_lo", [P, FT, T], F32R)
        r = Region(Z + 16 * K, Z + 104 * K)
        m_hi = r("m_hi", [P, KD, T], F32R)
        m_lo = r("m_lo", [P, KD, T], F32R)
        r = Region(Z + 64 * K, Z + 104 * K)
        x2t = r("x2t", [P, TT, D])
        xT = merged
        r = Region(Z + 104 * K, ZEND)
        sqk = [r(f"sqk{i}", [P, T]) for i in range(2)]
        vrow = r("vrow", [P, T])
        srow = r("srow", [P, T])
        onesq = r("onesq", [P, P])

        bank_free = [sem(f"bank_free{b}") for b in range(8)]
        raw_in = [sem(f"raw_in{i}") for i in range(RING)]
        s_hi = sem("chunk_hi")
        s_lo = sem("chunk_lo")
        s_phase = sem("phase")
        s_act, s_dve, s_dvx = sem("act_chain"), sem("dve_chain"), sem("dve_for_others")
        ld = {n: sem("in_" + n) for n in ("small", "x", "ctx", "rope", "uch", "kfilt", "kread", "s5", "ytok",
                                          "hyp", "w3", "win", "win2", "hyb", "x2", "fnorm", "out")}
        mm = {n: sem("pe_" + n) for n in ("vec", "ada", "xT", "s5in", "uT", "proj", "nT", "q", "att", "merge",
                                          "s5", "glu", "hy", "out", "norm", "up", "down", "end")}
        s = {n: sem("s_" + n) for n in (
            "silu",
            "vc",
            "s5a",
            "sq",
            "var",
            "sqrt",
            "xh",
            "htmp",
            "hth",
            "htl",
            "us",
            "zn",
            "ntmp",
            "nth",
            "ntl",
            "av",
            "rc",
            "akr",
            "diag",
            "oatt",
            "aqk",
            "max",
            "pTh",
            "oun",
            "oth",
            "otl",
            "s5row",
            "s5c",
            "angle",
            "trig",
            "pm",
            "cl",
            "s5r",
            "Hs",
            "gth",
            "gtl",
            "hya",
            "hid",
            "zc",
            "zt",
            "hs",
            "hsh",
            "hsl",
            "yt",
            "yth",
            "ytl",
            "ut",
            "uth",
            "utl",
            "alt",
            "mg",
            "nyq",
            "mh",
            "ml",
            "sq2",
            "vf",
            "sf",
            "h2t",
            "h2h",
            "h2l",
            "ath",
            "atl",
            "fr",
            "fin_a",
            "fin",
        )}

        chunks = []
        begin = {}

        def add(src, kt, n, kind="split", dest=None):
            chunks.append((src, kt, n, kind, dest))

        def wcols(w, k0, kt, c0, n):
            return w[k0 * P:(k0 + kt) * P, c0:c0 + n].rearrange("(k p) n -> p k n", p=P)

        for g in range(4):
            for i in range(4):
                add(wcols(a["ada_w"], 2 * i, 2, g * T, T), 2, T, "plain")
        begin["s5_in"] = len(chunks)
        for i in range(4):
            add(wcols(a["w_in"], 2 * i, 2, O_S5, W5), 2, W5)
        begin["mla_in"] = len(chunks)
        for i in range(4):
            add(wcols(a["w_in"], 2 * i, 2, 0, 416), 2, 416)
        begin["uq"] = len(chunks)
        for k in range(2):
            add(wcols(a["mla_w_uq"], k, 1, 0, 768), 1, 768)
        begin["ukv"] = len(chunks)
        add(wcols(a["mla_w_ukv"], 0, 1, 0, 1024), 1, 1024)
        branch_w = ["w_branch_mla", "w_branch_s5", "w_branch_hy"]

        def merge_chunks(j):
            for m in range(KD):
                add(wcols(a["w_in"], 0, KD, O_GATE + j * D + m * P, P), KD, P)
                add(wcols(a[branch_w[j]], 0, 4, m * P, P), 4, P)

        begin["merge0"] = len(chunks)
        merge_chunks(0)
        for g in range(4, 12):
            for i in range(4):
                add(wcols(a["ada_w"], 2 * i, 2, g * T, T), 2, T, "plain")
        begin["glu"] = len(chunks)
        for m in range(4):
            add(wcols(a["s5_w_glu"], 0, 4, m * P, P), 4, P)
        begin["merge1"] = len(chunks)
        merge_chunks(1)

        def hyena_chunks(n0, n1):
            for n in range(n0, n1):
                add(wcols(a["w_in"], 0, KD, O_HY + n * P, P), KD, P)

        begin["hyena"] = len(chunks)
        hyena_chunks(0, 8)
        for src, hi_, lo_ in ((a["dft_cos"], fc_hi, fc_lo), (a["dft_sin"], fs_hi, fs_lo)):
            for i in range(2):
                add(wcols(src, 2 * i, 2, 0, T), 2, T, "const",
                    (hi_[:, 2 * i:2 * i + 2, :].rearrange("p a b -> p (a b)"),
                     lo_[:, 2 * i:2 * i + 2, :].rearrange("p a b -> p (a b)")))
        hyena_chunks(8, 12)
        begin["merge2"] = len(chunks)
        merge_chunks(2)
        begin["w_out"] = len(chunks)
        for m in range(KD):
            add(wcols(a["w_out"], 0, KD, m * P, P), KD, P)
        begin["up"] = len(chunks)
        for f in range(FT):
            add(wcols(a["ffn_w_gu"], 0, KD, f * P, P), KD, P)
            add(wcols(a["ffn_w_gu"], 0, KD, FF + f * P, P), KD, P)
        begin["down"] = len(chunks)
        DOWN = (6, 6, 5, 5)
        for m in range(KD):
            k0 = 0
            for kt in DOWN:
                add(wcols(a["ffn_w_down"], k0, kt, m * P, P), kt, P)
                k0 += kt
        nth_split = []
        n = 0
        for ch in chunks:
            nth_split.append(n)
            n += ch[3] != "plain"

        uses = [0] * 8
        ends = {}
        taken = {}
        counts = {}

        def close(ins, which, name):
            counts[which] = counts.get(which, 0) + 1
            ins.then_inc(mm[which], 1)
            ends[name] = (mm[which], counts[which])

        def wait(eng, at):
            eng.wait_ge(at[0], at[1])

        block = ctx.enter_context(nc.Block())

        @block.tensor
        def _(pe):
            nxt = [0]

            def open_(b, name):
                if uses[b]:
                    pe.wait_ge(bank_free[b], uses[b])
                uses[b] += 1
                taken[name] = (bank_free[b], uses[b])

            def chunk():
                c = nxt[0]
                nxt[0] += 1
                _, kt, n, kind, dest = chunks[c]
                i = c % RING
                if kind == "plain":
                    pe.wait_ge(raw_in[i], 16 * (c // RING + 1))
                    return c, raw[i][:, 0:kt * n].rearrange("p (k n) -> p k n", k=kt)
                pe.wait_ge(s_lo, nth_split[c] + 1)
                if kind == "const":
                    return c, None
                return c, tuple(w[i][:, 0:kt * n].rearrange("p (k n) -> p k n", k=kt) for w in (whi, wlo))

            def mm3(o, w, x, first, last):
                pe.matmul(o, w[0], x[0], start=first, stop=False)
                pe.matmul(o, w[0], x[1], start=False, stop=False)
                return pe.matmul(o, w[1], x[0], start=False, stop=last)

            def to_tokens(m):
                wait(pe, taken[("down", m)])
                open_(4 + m % 4, ("yo", m))
                for t in range(TT):
                    ins = pe.transpose(bank(4 + m % 4, P, t * P), xT[:, m, t * P:(t + 1) * P], ident)
                close(ins, "end", ("yo", m))

            def phase_end(k):
                pe.drain().then_inc(s_phase, 1)
                pe.wait_ge(s_phase, 3 * k)

            pe.wait_ge(ld["small"], 16 * NSMALL)
            open_(0, "vec")
            pe.transpose(bank(0, VROWS), vr1[:, :], cst[0:VROWS, C_ID:C_ID + VROWS])
            pe.transpose(bank(0, 36, 128), vr2[:, :], cst[0:36, C_ID:C_ID + 36])
            close(pe.transpose(bank(0, 3, 256)[0:64], vr3[:, :], cst[0:3, C_ID:C_ID + 3]), "vec", "vec")

            def ada_group(g, b):
                open_(b, ("ada", g))
                for i in range(4):
                    c, w = chunk()
                    for k in range(2):
                        kk = 2 * i + k
                        ins = pe.matmul(bank(b)[0:2], silc[:, kk:kk + 9:8], w[:, k, :], start=(kk == 0), stop=(kk == 7))
                    if i < 3:
                        close(ins, "ada", ("chunk", c))
                close(ins, "ada", ("ada", g))
                ends[("chunk", c)] = ends[("ada", g)]

            def ada_turned(g, b, first):
                wait(pe, taken[("ada", g)])
                if first:
                    open_(b, ("adaT", g))
                for i in range(4):
                    ins = pe.transpose(bank(b, 2, 2 * (4 * g + i)), tmp[g % 2][0:2, i * P:(i + 1) * P],
                                       cst[0:2, C_ID:C_ID + 2])
                close(ins, "ada", ("adaT", g))

            pe.wait_ge(s["silu"], 1)
            for g in range(4):
                ada_group(g, 2 + g % 2)
                if g:
                    ada_turned(g - 1, 1, g == 1)
            ada_turned(3, 1, False)
            taken["ada0"] = taken[("adaT", 0)]
            ends["ada0"] = ends[("adaT", 3)]

            def turned(k):
                for b, t0, t1 in ((6, 0, TT), (7, TT, KT)):
                    open_(b, ("xT", k, b - 6))
                    for t in range(t0, t1):
                        ins = pe.transpose(bank(b, P, (t - t0) * P), xt[:, t, k * P:(k + 1) * P], ident)
                    close(ins, "xT", ("xT", k, b - 6))

            def tokens(t, k):
                hi_, lo_, o = (h_hi, h_lo, t) if t < TT else (hc_hi, hc_lo, t - TT)
                return hi_[:, k, o * P:(o + 1) * P], lo_[:, k, o * P:(o + 1) * P]

            pe.wait_ge(s["xh"], TT + TTC)
            for k in range(3):
                turned(k)
            for i in range(4):
                c, w = chunk()
                pe.wait_ge(s["htl"], 4 * (i + 1))
                for t in range(KT):
                    if i == 0:
                        open_(t, ("us", t))
                    for k in range(2):
                        ins = mm3(bank(t), tokens(t, 2 * i + k), (w[0][:, k, :], w[1][:, k, :]),
                                  i == 0 and k == 0, i == 3 and k == 1)
                    if i == 3:
                        close(ins, "s5in", ("us", t))
                    if t == 2 and 2 * i + 3 < KD:
                        turned(2 * i + 3)
                if i < 3:
                    close(ins, "s5in", ("chunk", c))
                if 2 * i + 4 < KD:
                    turned(2 * i + 4)
            ends[("chunk", c)] = ends[("us", KT - 1)]

            for i in range(4):
                c, w = chunk()
                for t in range(KT):
                    o, n = (0, 416) if t < TT else (256, 160)
                    if i == 0:
                        open_(t, ("z", t))
                    for k in range(2):
                        ins = mm3(bank(t, n, o), tokens(t, 2 * i + k), (w[0][:, k, o:], w[1][:, k, o:]),
                                  i == 0 and k == 0, i == 3 and k == 1)
                    if i == 3:
                        close(ins, "proj", ("z", t))
                if i < 3:
                    close(ins, "proj", ("chunk", c))
            ends[("chunk", c)] = ends[("z", KT - 1)]

            def chunks_turned(i0, i1):
                for i in range(i0, i1):
                    b = 6 + i % 2
                    open_(b, ("uT", i))
                    for j in range(4):
                        g = 4 * i + j
                        ins = pe.transpose(bank(b, NCH, j * NCH), uch2[:, g].rearrange("c s m -> c (s m)"),
                                           cst[0:NCH, C_ID:C_ID + NCH])
                    close(ins, "uT", ("uT", i))

            pe.wait_ge(s["us"], 1)
            chunks_turned(0, 4)

            pe.wait_ge(s["zn"], KT)
            for k in range(2):
                open_(k, ("nT", k))
                for t in range(TT):
                    ins = pe.transpose(bank(k, P, t * P), ztok[:, t, k * P:(k + 1) * P], ident)
                close(ins, "nT", ("nT", k))
            for k in range(2):
                open_(2 + k, ("nT", 2 + k))
                for t in range(*((0, TT) if k == 0 else (TT, KT))):
                    ins = pe.transpose(bank(2 + k, P, (t % TT) * P), ztok[:, t, QL:QL + KVL], ident)
                close(ins, "nT", ("nT", 2 + k))
            chunks_turned(4, 6)
            pe.wait_ge(s["ntl"], 4)
            c0, w0 = chunk()
            c1, w1 = chunk()
            for t in range(TT):
                for hf in range(2):
                    b = 4 + (2 * t + hf) % 4
                    open_(b, ("q", t, hf))
                    for k, w in enumerate((w0, w1)):
                        q = qnT_hi[:, k, t * P:(t + 1) * P], qnT_lo[:, k, t * P:(t + 1) * P]
                        ins = mm3(bank(b, 384), q, tuple(x[:, 0, hf * 384:(hf + 1) * 384] for x in w),
                                  k == 0, k == 1)
                    close(ins, "q", ("q", t, hf))
                if t < 2:
                    chunks_turned(6 + t, 7 + t)
            ends[("chunk", c0)] = ends[("chunk", c1)] = ends[("q", TT - 1, 1)]
            phase_end(1)

            for part, (t0, t1) in enumerate(((0, TT), (TT, KT))):
                open_(part, ("kr", part))
                for t in range(t0, t1):
                    ins = pe.transpose(bank(part, P, (t - t0) * P)[0:ROPE], krtok[:, t, :], ident)
                close(ins, "att", ("kr", part))
            c, ukv = chunk()
            kv = kvT_hi, kvT_lo
            def head_in(h):
                open_(0, ("qT", h))
                for t in range(TT):
                    ins = pe.transpose(bank(0, P, t * P)[0:QK], qtok[:, t, h, :], ident)
                close(ins, "att", ("qT", h))
                for part, (k0, n) in enumerate(((0, T), (T, TC))):
                    open_(1 + part, ("k", h, part))
                    close(mm3(bank(1 + part, n), tuple(x[:, 0, h * P:(h + 1) * P] for x in ukv),
                              tuple(x[:, k0:k0 + n] for x in kv), True, True), "att", ("k", h, part))

            def values(p):
                for b, t0, t1 in ((1, 0, 4), (2, 4, KT)):
                    open_(b, ("v", p, b))
                    w = tuple(x[:, 0, 2 * p * P:(2 * p + 2) * P].rearrange("k (h c) -> k h c", h=2)[:, :, NOPE:]
                              for x in ukv)
                    for t in range(t0, t1):
                        ins = mm3(bank(b, P, (t - t0) * P), tuple(x[:, t * P:(t + 1) * P] for x in kv), w, True, True)
                    close(ins, "att", ("v", p, b))

            def weighted(h, k0, k1):
                if k0 == 0:
                    for b in (1, 2):
                        wait(pe, taken[("v", h // 2, b)])
                    open_(3, ("o", h))
                for kt in range(k0, k1):
                    wait(pe, taken[("pT", h, kt)])
                    pt = (pTa_hi[:, kt, :], pTa_lo[:, kt, :]) if kt < 4 else (pTb_hi[:, kt - 4, :], pTb_lo[:, kt - 4, :])
                    ins = mm3(bank(3), tuple(x[:, kt, :, :].rearrange("p g v -> p (g v)") for x in (v_hi, v_lo)), pt, kt == 0, kt == KT - 1)
                if k1 == KT:
                    close(ins, "att", ("o", h))

            head_in(0)
            for h in range(HEADS):
                wait(pe, taken[("qT", h)])
                wait(pe, taken[("k", h, 0)])
                wait(pe, taken[("k", h, 1)])
                wait(pe, taken[("kr", 1)])
                for t in range(TT):
                    b = 4 + 2 * (t % 2)
                    open_(b, ("s", h, t))
                    q = tuple(x[:, t * P:(t + 1) * P] for x in qT2[h % 2])
                    mm3(bank(b), q, tuple(x[:, 0:T] for x in kT2[h % 2]), True, True)
                    close(mm3(bank(b + 1, TC), q, tuple(x[:, T:KEYS] for x in kT2[h % 2]), True, True),
                          "att", ("s", h, t))
                    if t == 0 and h + 1 < HEADS:
                        head_in(h + 1)
                    if h and t:
                        weighted(h - 1, 2 * t - 2, 2 * t)
                for t in range(TT):
                    wait(pe, taken[("s", h, t)])
                for kt in range(KT):
                    b = (4, 6, 0)[kt % 3]
                    open_(b, ("pT", h, kt))
                    for t in range(TT):
                        ins = pe.transpose(bank(b, P, t * P), prob[:, t, kt * P:(kt + 1) * P], ident)
                    close(ins, "att", ("pT", h, kt))
                    if kt == 2:
                        pe.wait_ge(s["diag"], h + 1)
                        open_(1, ("rc", h))
                        close(pe.matmul(bank(1), ones[:, :], tmp[0][:, :], start=True, stop=True), "att", ("rc", h))
                if h % 2 == 0:
                    values(h // 2)
            weighted(HEADS - 1, 0, KT)
            ends[("chunk", c)] = ends[("v", HEADS // 2 - 1, 2)]

            def hyena_setup(step):
                if step in (1, 4):
                    if step == 1:
                        pe.wait_ge(ld["hyp"], 16 * NHYP)
                    else:
                        pe.wait_ge(s["hid"], 1)
                    open_(0, ("hid", step // 4))
                    w, x = (w12[0:33, 0, :], zpos) if step == 1 else (w12[:, 1, :], hid1)
                    close(pe.matmul(bank(0)[0:64], w, x[:, :], start=True, stop=True), "hy", ("hid", step // 4))

            def s5_setup(step):
                if step == 0:
                    pe.wait_ge(ld["s5"], 16 * NS5)
                    for part in range(2):
                        for hf in range(2):
                            b = 4 + 2 * part + hf
                            open_(b, ("ct", part, hf))
                            for i in range(4):
                                ins = pe.transpose(bank(b, P, i * P)[0:ST], cld[:, part, 4 * hf + i, :], ident)
                            close(ins, "s5", ("ct", part, hf))
                elif step == 2:
                    pe.wait_ge(s["s5row"], 1)
                    open_(0, "s5row")
                    for i in range(4):
                        ins = pe.transpose(bank(0, NPD, i * NPD), row[:, 8 + i, :], cst[0:NPD, C_ID:C_ID + NPD])
                    close(ins, "s5", "s5row")

            def merge(j, x, ready, between=None):
                for m in range(KD):
                    b = 2 * (m % 4)
                    c, w = chunk()
                    open_(b, ("gate", j, m))
                    for k in range(KD):
                        ins = mm3(bank(b), (w[0][:, k, :], w[1][:, k, :]), (h_hi[:, k, :], h_lo[:, k, :]),
                                  k == 0, k == KD - 1)
                    close(ins, "merge", ("gate", j, m))
                    ends[("chunk", c)] = ends[("gate", j, m)]
                    c, w = chunk()
                    open_(b + 1, ("branch", j, m))
                    if m == 0:
                        pe.wait_ge(s["otl"], ready)
                    for k in range(4):
                        ins = mm3(bank(b + 1), (w[0][:, k, :], w[1][:, k, :]), (x[0][:, k, :], x[1][:, k, :]),
                                  k == 0, k == 3)
                    close(ins, "merge", ("branch", j, m))
                    ends[("chunk", c)] = ends[("branch", j, m)]
                    if between:
                        between(m)

            merge(0, (o_hi, o_lo), HEADS, s5_setup)
            phase_end(2)

            def s5_out(q, half):
                clr, cli = clr2[q % 2], cli2[q % 2]
                pe.wait_ge(ld["kread"], 16 * L * (q + 1))
                pe.wait_ge(s["Hs"], 2 * (q + 1))
                b = 1 + half
                open_(b, ("Y", q, half))
                for j in range(4):
                    gl, g2 = 2 * j + half, half
                    o = PS[0:NCX, 512 * b + P * j:512 * b + P * (j + 1)]
                    sl = slice(64 * g2, 64 * g2 + 64)
                    pe.matmul(o, U[:, 8 * q + gl, NCC:NCC + NCX], Mt[:, gl, :], start=True, stop=False)
                    for d in range(2):
                        l0 = 1 if d == 0 else 0
                        for part, cl in enumerate((clr, cli)):
                            ins = pe.matmul(o, H[sl, part, 4 * d + j, :], cl[sl, 4 * d + j, l0:l0 + 8, :],
                                            start=False, stop=(d == 1 and part == 1))
                close(ins, "s5", ("Y", q, half))

            for q in range(4):
                clr, cli = clr2[q % 2], cli2[q % 2]
                pe.wait_ge(s["pm"], 2 * q + 2)
                pe.wait_ge(s["cl"], q + 1)
                open_(3, ("K", q))
                for d in range(2):
                    l0 = 0 if d == 0 else 1
                    for j in range(4):
                        o = PS[32 * j:32 * j + 32, 512 * 3 + 128 * d:512 * 3 + 128 * d + 128]
                        pd = 4 * d + j
                        pe.matmul(o, bdr[:, pd, :], clr[:, pd, l0:l0 + 8, :], start=True, stop=False)
                        ins = pe.matmul(o, bdi[:, pd, :], cli[:, pd, l0:l0 + 8, :], start=False, stop=True)
                close(ins, "s5", ("K", q))
                for part, pm in enumerate((pmr, pmi)):
                    for d in range(2):
                        b = 4 + 2 * part + d
                        open_(b, ("WT", q, part, d))
                        for j in range(4):
                            ins = pe.transpose(bank(b, P, j * P), pm[:, 4 * d + j, :], ident)
                        close(ins, "s5", ("WT", q, part, d))
                if q:
                    s5_out(q - 1, 0)
                for part in range(2):
                    for d in range(2):
                        wait(pe, taken[("WT", q, part, d)])
                        b = 4 + 2 * part + d
                        open_(b, ("S", q, part, d))
                        for j in range(4):
                            for g2 in range(2):
                                o = PS[64 * g2:64 * g2 + 64, 512 * b + NCH * j:512 * b + NCH * (j + 1)]
                                c0 = 0 if d == 0 else NCC
                                ins = pe.matmul(o, WT[:, part, 4 * d + j, 64 * g2:64 * g2 + 64],
                                                U[:, 8 * q + 2 * j + g2, c0:c0 + NCH], start=True, stop=True)
                        close(ins, "s5", ("S", q, part, d))
                if q:
                    s5_out(q - 1, 1)
                ada_group(4 + 2 * q, 1)
                ada_group(5 + 2 * q, 2)
                ada_turned(4 + 2 * q, 0, q == 0)
                ada_turned(5 + 2 * q, 0, False)
                taken["ada1"] = taken[("adaT", 4)]
                ends["ada1"] = ends[("adaT", 5 + 2 * q)]
            s5_out(3, 0)
            s5_out(3, 1)
            for k in range(4):
                pe.wait_ge(ld["ytok"], 16 * TT * (k + 1))
                open_(3 + k, ("yT", k))
                for t in range(TT):
                    ins = pe.transpose(bank(3 + k, P, t * P), y5tok[:, t, k * P:(k + 1) * P], ident)
                close(ins, "glu", ("yT", k))
            for m in range(4):
                c, w = chunk()
                b = 7 * (m % 2)
                open_(b, ("glu", m))
                for k in range(4):
                    if m == 0:
                        pe.wait_ge(s["gtl"], k + 1)
                    ins = mm3(bank(b), (w[0][:, k, :], w[1][:, k, :]), (yg_hi[:, k, :], yg_lo[:, k, :]),
                              k == 0, k == 3)
                close(ins, "glu", ("glu", m))
                ends[("chunk", c)] = ends[("glu", m)]
            merge(1, (o_hi, o_lo), HEADS + 4, hyena_setup)

            pe.wait_ge(s["alt"], 2)

            def taps(it, t):
                if t == 0:
                    pe.wait_ge(s["hid"], 2)
                    pe.wait_ge(ld["w3"], 16 * (it + 1))
                open_(5, ("f", it, t))
                close(pe.matmul(bank(5), hid2[:, t * P:(t + 1) * P], w3[:, :, :], start=True, stop=True),
                      "hy", ("f", it, t))

            def to_tokens_hy(n):
                wait(pe, taken[("hz", n)])
                b = 6 + n % 2
                open_(b, ("ht", n))
                for t in range(TT):
                    ins = pe.transpose(bank(b, P, t * P), tmp[n % 2][:, t * P:(t + 1) * P], ident)
                close(ins, "hy", ("ht", n))

            for n in range(12):
                if n == 8:
                    for _ in range(4):
                        cc, _w = chunk()
                        assert chunks[cc][3] == "const"
                c, w = chunk()
                open_(n % 4, ("hz", n))
                for k in range(KD):
                    ins = mm3(bank(n % 4), (w[0][:, k, :], w[1][:, k, :]), (h_hi[:, k, :], h_lo[:, k, :]),
                              k == 0, k == KD - 1)
                close(ins, "hy", ("hz", n))
                ends[("chunk", c)] = ends[("hz", n)]
                if 1 <= n <= 8:
                    to_tokens_hy(n - 1)
                if 7 <= n < 11:
                    taps(0, n - 7)

            def spectrum(b, x_c, x_s, js):
                for k in range(TT):
                    mm3(bank(b, HC), (fc_hi[:, k, js], fc_lo[:, k, js]), tuple(x[:, k, :] for x in x_c), k == 0, k == 3)
                for k in range(TT):
                    ins = mm3(bank(b, HC, HC), (fs_hi[:, k, js], fs_lo[:, k, js]), tuple(x[:, k, :] for x in x_s),
                              k == 0, k == 3)
                return ins

            def nyquist(x, o):
                for k in range(TT):
                    pe.matmul(bank(4, HC, o), altr[:, :], x[0][:, k, :], start=(k == 0), stop=False)
                    ins = pe.matmul(bank(4, HC, o), altr[:, :], x[1][:, k, :], start=False, stop=(k == 3))
                return ins

            def filter_spectrum(it, j):
                if j == 0:
                    pe.wait_ge(s["hsl"], TT * (it + 1))
                open_(j % 2, ("G", it, j))
                y = ybuf[it]
                close(spectrum(j % 2, [x[:, :, 0:HC] for x in y], [x[:, :, HC:2 * HC] for x in y],
                               slice(j * P, (j + 1) * P)), "hy", ("G", it, j))

            filter_spectrum(0, 0)
            filter_spectrum(0, 1)
            for it, (half, o) in enumerate(CONVS):
                y_hi, y_lo = ybuf[it]
                for j in range(2, 4):
                    filter_spectrum(it, j)
                    if it < 3:
                        taps(it + 1, j - 2)
                open_(4, ("Ny", it))
                close(nyquist([x[:, :, 0:HC] for x in (y_hi, y_lo)], 0), "hy", ("Gn", it))
                if it < 3:
                    taps(it + 1, 2)
                if o == 0:
                    wait(pe, taken[("ht", 2 * half)])
                    wait(pe, taken[("ht", 2 * half + 1)])
                else:
                    pe.wait_ge(s["utl"], TT * (half + 1))
                u = u_hi[half], u_lo[half]
                for j in range(4):
                    b = (2, 3, 6, 7)[j]
                    open_(b, ("Us", it, j))
                    close(spectrum(b, u, u, slice(j * P, (j + 1) * P)), "hy", ("Us", it, j))
                    if j == 0 and it < 3:
                        taps(it + 1, 3)
                close(nyquist(u, HC), "hy", ("Un", it))
                if it < 3:
                    filter_spectrum(it + 1, 0)
                    filter_spectrum(it + 1, 1)
                pe.wait_ge(s["ytl"], 4 * (it + 1))
                pe.wait_ge(s["nyq"], it + 1)
                if o == 0:
                    for t in range(TT):
                        b = 6 + t % 2
                        open_(b, ("c", it, t))
                        ts = slice(t * P, (t + 1) * P)
                        for j in range(4):
                            mm3(bank(b, HC), (fc_hi[:, j, ts], fc_lo[:, j, ts]),
                                (y_hi[:, j, 0:HC], y_lo[:, j, 0:HC]), j == 0, False)
                            mm3(bank(b, HC), (fs_hi[:, j, ts], fs_lo[:, j, ts]),
                                (y_hi[:, j, HC:2 * HC], y_lo[:, j, HC:2 * HC]), False, False)
                        pe.matmul(bank(b, HC), alt_row[:, 0:P], nyh[:, :], start=False, stop=False)
                        close(pe.matmul(bank(b, HC), alt_row[:, 0:P], nyl[:, :], start=False, stop=True),
                              "hy", ("c", it, t))
                else:
                    for i in range(2):
                        b = 6 + i
                        open_(b, ("c", it, i))
                        cs, cs2 = slice(i * P, (i + 1) * P), slice(HC + i * P, HC + (i + 1) * P)
                        for j in range(4):
                            mm3(bank(b), (y_hi[:, j, cs], y_lo[:, j, cs]), (fc_hi[:, j, :], fc_lo[:, j, :]),
                                j == 0, False)
                            mm3(bank(b), (y_hi[:, j, cs2], y_lo[:, j, cs2]), (fs_hi[:, j, :], fs_lo[:, j, :]),
                                False, False)
                        pe.matmul(bank(b), nyh[:, cs], alt_row[:, :], start=False, stop=False)
                        close(pe.matmul(bank(b), nyl[:, cs], alt_row[:, :], start=False, stop=True),
                              "hy", ("c", it, i))
            merge(2, (e_hi, e_lo), HEADS + 8)

            pe.wait_ge(ld["x2"], 16)
            for k in range(KD):
                b = 4 + k % 4
                open_(b, ("x2T", k))
                for t in range(TT):
                    ins = pe.transpose(bank(b, P, t * P), x2t[:, t, k * P:(k + 1) * P], ident)
                close(ins, "out", ("x2T", k))

            def square_sum(k):
                if k == 0:
                    open_(4, "ss")
                pe.wait_ge(s["sq2"], k + 1)
                ins = pe.matmul(bank(4), onesq[:, :], sqk[k % 2][:, :], start=(k == 0), stop=(k == KD - 1))
                close(ins, "norm", ("ssk", k))

            for m in range(KD):
                c, w = chunk()
                b = m % 4
                open_(b, ("wo", m))
                for k in range(KD):
                    if m == 0:
                        pe.wait_ge(s["ml"], k + 1)
                    ins = mm3(bank(b), (w[0][:, k, :], w[1][:, k, :]), (m_hi[:, k, :], m_lo[:, k, :]),
                              k == 0, k == KD - 1)
                close(ins, "out", ("wo", m))
                ends[("chunk", c)] = ends[("wo", m)]
                if m:
                    square_sum(m - 1)
            square_sum(KD - 1)
            ends["ss"] = ends[("ssk", KD - 1)]

            for f in range(FT):
                for u in range(2):
                    c, w = chunk()
                    b = (2 * f + u) % 8
                    open_(b, ("gu", f, u))
                    for k in range(KD):
                        if f == 0 and u == 0:
                            pe.wait_ge(s["h2l"], k + 1)
                        ins = mm3(bank(b), (w[0][:, k, :], w[1][:, k, :]), (h_hi[:, k, :], h_lo[:, k, :]),
                                  k == 0, k == KD - 1)
                    close(ins, "up", ("gu", f, u))
                    ends[("chunk", c)] = ends[("gu", f, u)]
            pe.wait_ge(s["atl"], FT)
            for m in range(KD):
                b = m % 4
                open_(b, ("down", m))
                k0 = 0
                for i, kt in enumerate(DOWN):
                    c, w = chunk()
                    for k in range(kt):
                        ins = mm3(bank(b), (w[0][:, k, :], w[1][:, k, :]),
                                  (act_hi[:, k0 + k, :], act_lo[:, k0 + k, :]), k0 + k == 0, k0 + k == FT - 1)
                    k0 += kt
                    close(ins, "down", ("chunk", c))
                ends[("down", m)] = ends[("chunk", c)]
                if m:
                    to_tokens(m - 1)
            to_tokens(KD - 1)
            assert nxt[0] == len(chunks)

        @block.scalar
        def _(act):
            chain = [0]
            settled = [True]

            def after():
                if not settled[0]:
                    act.drain()
                settled[0] = False
                return act

            at = [0]

            def link(ins):
                chain[0] += 1
                ins.then_inc(s_act, 1)
                act.wait_ge(s_act, chain[0])
                settled[0] = True

            def split_to(c1):
                while at[0] <= min(c1, len(chunks) - 1):
                    c = at[0]
                    at[0] += 1
                    _, kt, n, kind, dest = chunks[c]
                    if kind == "plain":
                        continue
                    i = c % RING
                    act.wait_ge(raw_in[i], 16 * (c // RING + 1))
                    if kind == "const":
                        o = dest[0]
                    else:
                        o = whi[i][:, 0:kt * n]
                        if c >= RING and chunks[c - RING][3] != "const":
                            wait(act, ends[("chunk", c - RING)])
                    after().activation(o, raw[i][:, 0:kt * n], ACT.Copy).then_inc(s_hi, 1)

            def phase_end(k):
                act.drain().then_inc(s_phase, 1)
                act.wait_ge(s_phase, 3 * k)

            def copy(o, i):
                return after().activation(o, i, ACT.Copy)

            def warm(f):
                after().activation(junk[0:1, 0:1], cst[0:1, 0:1], f)

            def load_now(o, i, which):
                act.dma_start(o, i).then_inc(ld[which], 16)

            load_now(cst[:, :], a["cst"], "small")
            for name, rows in VECS:
                o = VOFF[name]
                src = a[name]
                load_now(vr1[o:o + rows, :], src.rearrange("(r p) -> r p", p=P), "small")
            load_now(vr2[:, :], a["hy_conv_w"].rearrange("j (r p) -> (j r) p", p=P), "small")
            for i, name in enumerate(("hy_f_b1", "hy_f_b2", "hy_f_freq")):
                load_now(vr3[i:i + 1, :], a[name].rearrange("(r p) -> r p", p=64), "small")
            load_now(xt[:, 0:TT, :], a["x"].rearrange("(t p) d -> p t d", p=P), "x")
            load_now(xt[:, TT:KT, :], a["ctx"].rearrange("(t p) d -> p t d", p=P), "ctx")
            act.wait_ge(s["vc"], 1)
            after().activation(silc[:, :], vc1[:, 0:16], ACT.Silu).then_inc(s["silu"], 1)
            act.wait_ge(ld["x"], 16)
            act.wait_ge(ld["ctx"], 16)
            for t in range(KT):
                link(after().activation(sq0[:, :], xt[:, t, :], ACT.Square, accum_out=rs[:, 0, 0, t:t + 1]))
            act.drain().then_inc(s["sq"], 1)
            act.wait_ge(s["var"], 1)
            after().activation(rs[:, 0, 2, 0:KT], rs[:, 0, 1, 0:KT], ACT.Sqrt).then_inc(s["sqrt"], 1)

            def ada_rows(g, b):
                wait(act, ends[("ada", g)])
                if g >= 2:
                    wait(act, ends[("adaT", g - 2)])
                copy(tmp[g % 2][0:2, :], bank(b)[0:2]).then_inc(bank_free[b], 1)

            for g in range(4):
                ada_rows(g, 2 + g % 2)
            for j in range(2 * KD):
                k, x = j // 2, j % 2
                if j % 3 == 0 and j:
                    split_to(begin["s5_in"] - 1 + j // 3)
                act.wait_ge(s["htmp"], j + 1)
                o = hc_hi[:, k, :] if x else h_hi[:, k, :]
                copy(o, tmp[j % 2][:, 0:TC if x else T]).then_inc(s["hth"], 1)
            split_to(begin["uq"] - 2)
            for t in range(KT):
                wait(act, ends[("us", t)])
                copy(us[:, t, :], bank(t)).then_inc(bank_free[t], 1)
            act.wait_ge(ld["uch"], 16 * KT)
            copy(uch2[:, :, :, :], uch[:, :, :].rearrange("c s (g m) -> c g s m", g=G)).then_inc(s["us"], 1)
            split_to(begin["uq"] - 1)
            for t in range(KT):
                wait(act, ends[("z", t)])
                if t < TT:
                    link(after().activation(sq1[:, :], bank(t, QL), ACT.Square, accum_out=rs[:, 1, 0, t:t + 1]))
                link(after().activation(sq1[:, 0:KVL], bank(t, KVL, QL), ACT.Square,
                                    accum_out=rs[:, 1, 0, TT + t:TT + t + 1]))
                act.drain().then_inc(s["sq"], 1)
            warm(ACT.Sqrt)
            act.wait_ge(s["var"], 2)
            after().activation(rs[:, 1, 2, 0:10], rs[:, 1, 1, 0:10], ACT.Sqrt).then_inc(s["sqrt"], 1)

            def chunks_turned(i0, i1):
                for i in range(i0, i1):
                    b = 6 + i % 2
                    wait(act, ends[("uT", i)])
                    src = bank(b, 4 * NCH).rearrange("p (g c) -> p g c", g=4)
                    gs = slice(4 * i, 4 * i + 4)
                    copy(U[:, gs, NCC:NCC + NCX], src[:, :, 0:NCX])
                    act.activation(U[:, gs, 0:NCC], src[:, :, NCX:NCH], ACT.Copy)
                    act.activation(U[:, gs, NCC + NCX:P], src[:, :, NCX:NCH], ACT.Copy).then_inc(bank_free[b], 1)

            chunks_turned(0, 4)
            split_to(begin["ukv"])
            for i in range(4):
                act.wait_ge(s["ntmp"], i + 1)
                o = (qnT_hi[:, 0, :], qnT_hi[:, 1, :], kvT_hi[:, 0:T], kvT_hi[:, T:KEYS])[i]
                copy(o, tmp[i % 2][:, 0:TC if i == 3 else T]).then_inc(s["nth"], 1)
            chunks_turned(4, 6)
            for t in range(TT):
                for hf in range(2):
                    b = 4 + (2 * t + hf) % 4
                    wait(act, ends[("q", t, hf)])
                    copy(qtok[:, t, 4 * hf:4 * hf + 4, :].rearrange("p h d -> p (h d)"), bank(b, 384))\
                        .then_inc(bank_free[b], 1)
                if t < 2:
                    chunks_turned(6 + t, 7 + t)
            phase_end(1)

            split_to(begin["merge0"] + 2)
            for part, (k0, n) in enumerate(((0, T), (T, TC))):
                wait(act, ends[("kr", part)])
                for kT_hi, _ in kT2:
                    copy(kT_hi[NOPE:QK, k0:k0 + n], bank(part, n)[0:ROPE]).then_inc(s["akr"], 1)
            def queries_in(h):
                wait(act, ends[("qT", h)])
                copy(qT2[h % 2][0][:, :], bank(0)[0:QK]).then_inc(s["aqk"], 1)

            def keys_in(h):
                for part, (k0, n) in enumerate(((0, T), (T, TC))):
                    wait(act, ends[("k", h, part)])
                    copy(kT2[h % 2][0][0:NOPE, k0:k0 + n], bank(1 + part, n)[0:NOPE]).then_inc(s["aqk"], 1)

            def weighted(h):
                rows = slice(64 * (h % 2), 64 * (h % 2) + 64)
                act.wait_ge(s["oatt"], h + 1)
                copy(o_hi[rows, h // 2, :], tmp[2][rows, :]).then_inc(s["oth"], 1)

            queries_in(0)
            keys_in(0)
            for h in range(HEADS):
                for t in range(TT):
                    i = TT * h + t
                    act.wait_ge(s["max"], i + 1)
                    after().activation(prob[:, t, :], bank(4 + 2 * (t % 2), KEYS), ACT.Exp, bias=mx[:, 2 * i + 1:2 * i + 2],
                                       scale=SCALE, accum_out=den[:, 0, h, t:t + 1])\
                        .then_inc(bank_free[4 + 2 * (t % 2)], 1)
                    if t < 2 and h + 1 < HEADS:
                        (queries_in, keys_in)[t](h + 1)
                for kt in range(KT):
                    wait(act, ends[("pT", h, kt)])
                    o = pTa_hi[:, kt, :] if kt < 4 else pTb_hi[:, kt - 4, :]
                    copy(o, bank((4, 6, 0)[kt % 3])).then_inc(s["pTh"], 1)
                    if kt == 2 and h:
                        weighted(h - 1)
                    if kt == 3:
                        wait(act, ends[("rc", h)])
                        copy(tmp[1][:, :], bank(1)).then_inc(bank_free[1], 1)
                if h % 2 == 0:
                    for b, t0, t1 in ((1, 0, 4), (2, 4, KT)):
                        wait(act, ends[("v", h // 2, b)])
                        copy(v_hi[:, t0:t1, :, 0:VD], bank(b, (t1 - t0) * P).rearrange("p (k g v) -> p k g v", g=2, v=VD))\
                            .then_inc(s["av"], 1)
            weighted(HEADS - 1)

            def s5_setup(step):
                if step == 0:
                    act.wait_ge(ld["s5"], 16 * NS5)
                    after().activation(dt2[:, :], dt2[:, :], ACT.Exp).then_inc(s["s5c"], 1)
                elif step == 1:
                    for part, dst in enumerate((ctr, cti)):
                        for hf in range(2):
                            b = 4 + 2 * part + hf
                            wait(act, ends[("ct", part, hf)])
                            src = bank(b)[0:ST].rearrange("p (a g n) -> p a g n", g=2, n=GC)
                            for g2 in range(2):
                                ins = after().activation(dst[64 * g2:64 * g2 + 64, 16 * hf:16 * hf + 16, :],
                                                         src[:, :, g2, :], ACT.Copy, scale=1.0 - 2.0 * part)
                            ins.then_inc(bank_free[b], 1)
                    act.wait_ge(s["s5a"], 1)
                    link(after().activation(row[:, 6, :], row[:, 8, :], ACT.Exp))
                    link(after().activation(row[:, 7, :], row[:, 9, :], ACT.Sin))
                    after().activation(row[:, 5, :], row[:, 5, :], ACT.Sin).then_inc(s["s5c"], 1)
                elif step == 4:
                    act.wait_ge(s["s5a"], 2)
                    link(after().activation(lt[:, 2, :], lt[:, 2, :], ACT.Exp))
                    link(after().activation(lt[:, 0, :], lt[:, 0, :], ACT.Sin))
                    after().activation(lt[:, 1, :], lt[:, 1, :], ACT.Sin).then_inc(s["s5c"], 1)

            def hyena_setup(step):
                if step in (3, 6):
                    i = step // 3 - 1
                    act.wait_ge(s["hya"], i + 1)
                    after().activation((hid1, hid2)[i][:, :], harg[:, :], ACT.Sin).then_inc(s["hid"], 1)

            def merged_hi(m):
                act.wait_ge(s["mg"], m + 1)
                copy(m_hi[:, m, :], merged[:, m, :]).then_inc(s["mh"], 1)

            def merge(j, between=None):
                for m in range(KD):
                    split_to(begin["merge%d" % j] + 2 * m + 3)
                    wait(act, ends[("gate", j, m)])
                    if m >= 2:
                        wait(act, taken[("branch", j, m - 2)])
                    after().activation(tmp[m % 2][:, :], bank(2 * (m % 4)), ACT.Sigmoid).then_inc(bank_free[2 * (m % 4)], 1)
                    if between:
                        between(m)

            merge(0, s5_setup)
            phase_end(2)

            def trig(q):
                act.wait_ge(s["angle"], q + 1)
                if q >= 2:
                    act.wait_ge(s["Hs"], 2 * (q - 1))
                after().activation(tsin2[q % 2][:, :, :], ang_s[:, :, :], ACT.Sin)
                after().activation(tcos2[q % 2][:, :, :], ang_c[:, :, :], ACT.Sin).then_inc(s["trig"], 1)

            def s5_out(q, half):
                wait(act, ends[("Y", q, half)])
                if half == 0 and q:
                    act.wait_ge(ld["ytok"], 16 * TT * q)
                src = bank(1 + half)[0:NCX].rearrange("c (g t n) -> c g t n", g=4, t=L)
                o = Y2[:, :, :].rearrange("c t (g two n) -> c two g t n", g=4, two=2)[:, half]
                after()
                for g in range(4):
                    ins = act.activation(o[:, g], src[:, g], ACT.Copy)
                ins.then_inc(bank_free[1 + half], 1)
                wait(act, taken[("Y", q, half)])
                if half == 1:
                    for t in range(TT):
                        act.dma_start(y5tok[:, t, q * P:(q + 1) * P], Y2[16 * t:16 * t + 16, :, :])\
                            .then_inc(ld["ytok"], 16)

            trig(0)
            for q in range(4):
                for part in range(2):
                    for d in range(2):
                        b = 4 + 2 * part + d
                        wait(act, ends[("WT", q, part, d)])
                        copy(WT[:, part, 4 * d:4 * d + 4, :].rearrange("p a n -> p (a n)"), bank(b))\
                            .then_inc(bank_free[b], 1)
                if q < 3:
                    trig(q + 1)
                if q:
                    s5_out(q - 1, 0)
                    s5_out(q - 1, 1)
                wait(act, taken[("K", q)])
                act.dma_start(scratch[q], K2[:, :, :].rearrange("p l n -> p (l n)")).then_inc(ld["kfilt"], 16)
                act.wait_ge(ld["kfilt"], 16 * (q + 1))
                for st in range(L):
                    act.dma_start(Mt[GC * st:GC * (st + 1), :, :],
                                  scratch[q].rearrange("(g m) c -> m g c", m=GC)[:, :, (7 - st) * GC:(15 - st) * GC])\
                        .then_inc(ld["kread"], 16)
                ada_rows(4 + 2 * q, 1)
                ada_rows(5 + 2 * q, 2)
            s5_out(3, 0)
            s5_out(3, 1)
            for k in range(4):
                wait(act, ends[("yT", k)])
                after().activation(yg[:, k, :], bank(3 + k), ACT.Gelu_apprx_tanh).then_inc(bank_free[3 + k], 1)
                wait(act, taken[("yT", k)])
                copy(yg_hi[:, k, :], yg[:, k, :]).then_inc(s["gth"], 1)
            split_to(begin["merge1"] - 1)
            for m in range(4):
                wait(act, ends[("glu", m)])
                after().activation(tmp[m % 2][:, :], bank(7 * (m % 2)), ACT.Sigmoid).then_inc(bank_free[7 * (m % 2)], 1)
                act.wait_ge(s["oun"], m + 1)
                copy(o_hi[:, m, :], yg[:, m, :]).then_inc(s["oth"], 1)
            merge(1, hyena_setup)
            split_to(begin["hyena"] - 1)

            wait(act, taken[("branch", 1, KD - 1)])
            def taps_hi(it, t):
                n = TT * it + t
                act.wait_ge(s["hs"], n + 1)
                copy(ybuf[it][0][:, t, :], tmp[t % 2][:, :]).then_inc(s["hsh"], 1)

            def filter_out(it, j):
                wait(act, ends[("G", it, j)])
                if it:
                    act.wait_ge(s["yt"], 4 * (it - 1) + j + 1)
                after().activation(Gs[:, j, :], bank(j % 2), ACT.Identity, scale=cst[:, C_GS + j:C_GS + j + 1])\
                    .then_inc(bank_free[j % 2], 1)

            def tokens_out(n):
                wait(act, ends[("ht", n)])
                part, half, i = n // 4, n % 4 // 2, n % 2
                src = bank(6 + n % 2).rearrange("p (t c) -> p t c", t=TT)
                cs = slice(i * P, (i + 1) * P)
                if part == 0:
                    copy(u_hi[half][:, :, cs], src).then_inc(s["zt"], 1)
                else:
                    copy(g1t[half][:, :, cs], src).then_inc(bank_free[6 + n % 2], 1)

            for n in range(12):
                split_to(min(begin["hyena"] + n + 2 + (4 if n >= 6 else 0), begin["merge2"] - 1))
                wait(act, ends[("hz", n)])
                if 2 <= n < 8:
                    wait(act, ends[("ht", n - 2)])
                o = tmp[n % 2][:, :] if n < 8 else g2c[n % 4 // 2][:, n % 2, :]
                after().activation(o, bank(n % 4), ACT.Identity, scale=vc2[:, 12 + n:13 + n],
                                   bias=vc1[:, VOFF["hy_conv_b"] + n:VOFF["hy_conv_b"] + n + 1]).then_inc(s["zc"], 1)
                if 1 <= n <= 8:
                    tokens_out(n - 1)
                if n >= 8:
                    taps_hi(0, n - 8)
            split_to(begin["merge2"] - 1)
            filter_out(0, 0)
            filter_out(0, 1)
            for it, (half, o) in enumerate(CONVS):
                y_hi = ybuf[it][0]
                for j in range(2, 4):
                    filter_out(it, j)
                    if it < 3:
                        taps_hi(it + 1, j - 2)
                if it < 3:
                    taps_hi(it + 1, 2)
                    taps_hi(it + 1, 3)
                for j in range(4):
                    act.wait_ge(s["yt"], 4 * it + j + 1)
                    copy(y_hi[:, j, :], tmp[j % 2][:, :]).then_inc(s["yth"], 1)
                if it < 3:
                    filter_out(it + 1, 0)
                    filter_out(it + 1, 1)
                if o == 0:
                    for t in range(TT):
                        act.wait_ge(s["ut"], TT * half + t + 1)
                        copy(u_hi[half][:, t, :], tmp[t % 2][:, 0:HC]).then_inc(s["uth"], 1)
                else:
                    for i in range(2):
                        act.wait_ge(s["oun"], 4 + 2 * half + i + 1)
                        copy(e_hi[:, 2 * half + i, :], tmp[i][:, :]).then_inc(s["oth"], 1)
            merge(2, lambda m: m and merged_hi(m - 1))
            merged_hi(KD - 1)

            for k in range(KD):
                wait(act, ends[("x2T", k)])
                act.wait_ge(s["ml"], k + 1)
                copy(xT[:, k, :], bank(4 + k % 4)).then_inc(bank_free[4 + k % 4], 1)
            for m in range(KD):
                split_to(begin["w_out"] + m + 2)
                wait(act, taken[("wo", m)])
                if m >= 2:
                    wait(act, ends[("ssk", m - 2)])
                after().activation(sqk[m % 2][:, :], xT[:, m, :], ACT.Square).then_inc(s["sq2"], 1)
            warm(ACT.Sqrt)
            act.wait_ge(s["vf"], 1)
            after().activation(srow[:, :], vrow[:, :], ACT.Sqrt).then_inc(s["sf"], 1)
            for k in range(KD):
                act.wait_ge(s["h2t"], k + 1)
                copy(h_hi[:, k, :], tmp[k % 2][:, :]).then_inc(s["h2h"], 1)

            warm(ACT.Silu)
            for f in range(FT):
                split_to(begin["up"] + 2 * f + 3)
                wait(act, ends[("gu", f, 0)])
                if f >= 3:
                    act.wait_ge(s["atl"], f - 2)
                elif f == 0:
                    act.wait_ge(s["h2l"], KD)
                after().activation(tmp[f % 3][:, :], bank((2 * f) % 8), ACT.Silu).then_inc(bank_free[(2 * f) % 8], 1)
                wait(act, taken[("gu", f, 1)])
                copy(act_hi[:, f, :], tmp[f % 3][:, :]).then_inc(s["ath"], 1)

            def finished(m):
                wait(act, ends[("yo", m)])
                link(copy(ytok[:, :, m * P:(m + 1) * P], bank(4 + m % 4).rearrange("p (t c) -> p t c", t=TT)))
                for t in range(TT):
                    ins = after().activation(fsq[:, :], bank(4 + m % 4, P, t * P), ACT.Square,
                                             accum_out=fsum[:, t, m:m + 1])
                ins.then_inc(bank_free[4 + m % 4], 1)

            for m in range(KD):
                split_to(begin["down"] + 4 * m + 6)
                if m:
                    finished(m - 1)
            finished(KD - 1)
            warm(ACT.Sqrt)
            act.wait_ge(s["var"], 3)
            after().activation(rs[:, 2, 2, 0:TT], rs[:, 2, 1, 0:TT], ACT.Sqrt).then_inc(s["sqrt"], 1)
            act.wait_ge(s["fr"], 1)
            for t in (2, 3):
                after().activation(ytok[:, t, :], ytok[:, t, :], ACT.Copy, scale=rs[:, 2, 5, t:t + 1])\
                    .then_inc(s["fin_a"], 1)

        @block.vector
        def _(dve):
            chain = [0]
            settled = [True]

            def after():
                if not settled[0]:
                    dve.drain()
                settled[0] = False
                return dve

            at = [0]

            def link(ins):
                chain[0] += 1
                ins.then_inc(s_dve, 1)
                dve.wait_ge(s_dve, chain[0])
                settled[0] = True

            def tt(o, x, y, op):
                return after().tensor_tensor(o, x, y, op)

            def low(o, x, hi_):
                return after().tensor_tensor(o, x, hi_.bitcast(F32), ALU.subtract)

            def split_to(c1):
                while at[0] <= min(c1, len(chunks) - 1):
                    c = at[0]
                    at[0] += 1
                    _, kt, n, kind, dest = chunks[c]
                    if kind == "plain":
                        continue
                    i = c % RING
                    dve.wait_ge(s_hi, nth_split[c] + 1)
                    o, hi_ = (dest[1], dest[0]) if kind == "const" else (wlo[i][:, 0:kt * n], whi[i][:, 0:kt * n])
                    low(o, raw[i][:, 0:kt * n], hi_).then_inc(s_lo, 1)

            def phase_end(k):
                dve.drain().then_inc(s_phase, 1)
                dve.wait_ge(s_phase, 3 * k)

            def refine(v, sq, r_, t_, o):
                link(after().reciprocal(r_, sq))
                link(tt(t_, r_, r_, ALU.mult))
                link(tt(t_, t_, v, ALU.mult))
                link(after().tensor_scalar(t_, t_, -0.5, 1.5, ALU.mult, ALU.add))
                link(tt(o, r_, t_, ALU.mult))

            def reduce_angle(v, n):
                link(after().tensor_scalar(n, v, INV_2PI, ROUND, ALU.mult, ALU.add))
                link(after().tensor_scalar(n, n, ROUND, None, ALU.subtract))
                link(after().scalar_tensor_tensor(v, n, -TWO_PI_HI, v, ALU.mult, ALU.add))
                link(after().scalar_tensor_tensor(v, n, -TWO_PI_LO, v, ALU.mult, ALU.add))
                link(after().tensor_scalar(v, v, PI, -PI, ALU.min, ALU.max))

            wait(dve, ends["vec"])
            after().tensor_copy(vc1[:, :], bank(0, VROWS)).then_inc(s["vc"], 1)
            after().tensor_copy(vc2[:, :], bank(0, 36, 128))
            after().tensor_copy(vc3[:, :], bank(0, 3, 256)[0:64]).then_inc(bank_free[0], 1)
            dve.wait_ge(s["sq"], 1)
            link(after().tensor_scalar(rs[:, 0, 1, 0:KT], rs[:, 0, 0, 0:KT], 1.0 / D, EPS, ALU.mult, ALU.add))
            dve.drain().then_inc(s["var"], 1)
            dve.wait_ge(s["sqrt"], 1)
            refine(rs[:, 0, 1, 0:KT], rs[:, 0, 2, 0:KT], rs[:, 0, 3, 0:KT], rs[:, 0, 4, 0:KT], rs[:, 0, 5, 0:KT])
            for t in range(KT):
                after().tensor_scalar(xt[:, t, :], xt[:, t, :], rs[:, 0, 5, t:t + 1], None, ALU.mult).then_inc(s["xh"], 1)
            wait(dve, ends["ada0"])
            dve.wait_ge(s["vc"], 1)
            pv = bank(1, 32).rearrange("p (m x) -> p m x", x=2)
            ab = vc1[:, VOFF["ada_b"]:VOFF["ada_b"] + 48]
            nm = vc1[:, VOFF["norm_mix"]:VOFF["norm_mix"] + KD]
            link(tt(modx[:, 0:16], pv[:, :, 0], ab[:, 0:16], ALU.add))
            tt(modc[:, :], pv[:, :, 1], ab[:, 0:16], ALU.add).then_inc(bank_free[1], 1)
            wait(dve, taken["ada0"])
            after().scalar_tensor_tensor(amix[:, 0, :], modx[:, 8:16], 1.0, nm, ALU.add, ALU.mult)
            link(after().scalar_tensor_tensor(amix[:, 1, :], modc[:, 8:16], 1.0, nm, ALU.add, ALU.mult))

            def low_h(j):
                k, x = j // 2, j % 2
                dve.wait_ge(s["hth"], j + 1)
                n = TC if x else T
                low((hc_lo if x else h_lo)[:, k, :], tmp[j % 2][:, 0:n], (hc_hi if x else h_hi)[:, k, :])\
                    .then_inc(s["htl"], 1)

            for j in range(2 * KD):
                k, x = j // 2, j % 2
                n = TC if x else T
                b = 6 + x
                wait(dve, ends[("xT", k, x)])
                after().tensor_scalar(tmp[j % 2][:, 0:n], bank(b, n), amix[:, x, k:k + 1],
                                  (modc if x else modx)[:, k:k + 1], ALU.mult, ALU.add).then_inc(bank_free[b], 1)
                wait(dve, taken[("xT", k, x)])
                dve.drain().then_inc(s["htmp"], 1)
                if j:
                    low_h(j - 1)
                if j % 3 == 0 and j:
                    split_to(begin["s5_in"] - 1 + j // 3)
            low_h(2 * KD - 1)
            split_to(begin["uq"] - 1)
            for t in range(KT):
                dve.wait_ge(s["sq"], t + 2)
                o = 0 if t < TT else 256
                after().tensor_copy(ztok[:, t, o:416], bank(t, 416 - o, o)).then_inc(bank_free[t], 1)
            link(after().tensor_scalar(rs[:, 1, 1, 0:TT], rs[:, 1, 0, 0:TT], 1.0 / QL, EPS, ALU.mult, ALU.add))
            link(after().tensor_scalar(rs[:, 1, 1, TT:10], rs[:, 1, 0, TT:10], 1.0 / KVL, EPS, ALU.mult, ALU.add))
            dve.drain().then_inc(s["var"], 1)
            dve.wait_ge(s["sqrt"], 2)
            refine(rs[:, 1, 1, 0:10], rs[:, 1, 2, 0:10], rs[:, 1, 3, 0:10], rs[:, 1, 4, 0:10], rs[:, 1, 5, 0:10])
            for t in range(KT):
                wait(dve, taken[("z", t)])
                if t < TT:
                    after().tensor_scalar(ztok[:, t, 0:QL], ztok[:, t, 0:QL], rs[:, 1, 5, t:t + 1], None, ALU.mult)
                after().tensor_scalar(ztok[:, t, QL:QL + KVL], ztok[:, t, QL:QL + KVL],
                                  rs[:, 1, 5, TT + t:TT + t + 1], None, ALU.mult).then_inc(s["zn"], 1)
            split_to(begin["ukv"])

            def low_n(i):
                dve.wait_ge(s["nth"], i + 1)
                o, hi_ = ((qnT_lo[:, 0, :], qnT_hi[:, 0, :]), (qnT_lo[:, 1, :], qnT_hi[:, 1, :]),
                          (kvT_lo[:, 0:T], kvT_hi[:, 0:T]), (kvT_lo[:, T:KEYS], kvT_hi[:, T:KEYS]))[i]
                low(o, tmp[i % 2][:, 0:TC if i == 3 else T], hi_).then_inc(s["ntl"], 1)

            for i in range(4):
                n = TC if i == 3 else T
                col = VOFF["mla_q_norm"] + i if i < 2 else VOFF["mla_kv_norm"]
                wait(dve, ends[("nT", i)])
                after().tensor_scalar(tmp[i % 2][:, 0:n], bank(i, n), vc1[:, col:col + 1], None, ALU.mult)\
                    .then_inc(bank_free[i], 1)
                wait(dve, taken[("nT", i)])
                dve.drain().then_inc(s["ntmp"], 1)
                if i:
                    low_n(i - 1)
            low_n(3)

            def rotate(x1, x2, cos, sin, n, shape):
                r_ = [x[:, 0:n].rearrange(shape[0], **shape[1]) for x in tmp]
                tt(r_[0], x1, cos, ALU.mult)
                tt(r_[1], x2, sin, ALU.mult)
                link(tt(r_[2], x1, sin, ALU.mult))
                link(tt(x1, r_[0], r_[1], ALU.subtract))
                link(tt(r_[0], x2, cos, ALU.mult))
                link(tt(x2, r_[2], r_[0], ALU.add))

            dve.wait_ge(ld["rope"], 16)
            link(after().tensor_copy(krtok[:, :, :], ztok[:, :, 384:416]))
            rotate(krtok[:, 0:TT, 0::2], krtok[:, 0:TT, 1::2], rope[:, :, 0, :], rope[:, :, 1, :], TT * 16,
                   ("p (t f) -> p t f", {"t": TT}))
            for t in range(TT):
                for hf in range(2):
                    wait(dve, taken[("q", t, hf)])
            shape4 = [P, TT, HEADS, 16]
            rotate(qtok[:, :, :, NOPE:QK:2], qtok[:, :, :, NOPE + 1:QK:2],
                   rope[:, :, 0, :].unsqueeze(2).to_broadcast(shape4), rope[:, :, 1, :].unsqueeze(2).to_broadcast(shape4),
                   T, ("p (t h f) -> p t h f", {"t": TT, "h": HEADS}))
            phase_end(1)

            split_to(begin["merge0"] + 2)
            link(after().memset(ones[:, :], 1.0))
            for part, (k0, n) in enumerate(((0, T), (T, TC))):
                dve.wait_ge(s["akr"], 2 * part + 2)
                for kT_hi, kT_lo in kT2:
                    ins = low(kT_lo[NOPE:QK, k0:k0 + n], bank(part, n)[0:ROPE], kT_hi[NOPE:QK, k0:k0 + n])
                ins.then_inc(bank_free[part], 1)
            def queries_low(h):
                dve.wait_ge(s["aqk"], 3 * h + 1)
                low(qT2[h % 2][1][:, :], bank(0)[0:QK], qT2[h % 2][0][:, :]).then_inc(bank_free[0], 1)

            def keys_low(h, part):
                k0, n = ((0, T), (T, TC))[part]
                dve.wait_ge(s["aqk"], 3 * h + 2 + part)
                low(kT2[h % 2][1][0:NOPE, k0:k0 + n], bank(1 + part, n)[0:NOPE], kT2[h % 2][0][0:NOPE, k0:k0 + n])\
                    .then_inc(bank_free[1 + part], 1)

            def weighted(h):
                rows = slice(64 * (h % 2), 64 * (h % 2) + 64)
                wait(dve, ends[("o", h)])
                wait(dve, taken[("rc", h)])
                tt(tmp[2][rows, :], bank(3)[rows], tmp[1][rows, :], ALU.mult).then_inc(bank_free[3], 1)
                wait(dve, taken[("o", h)])
                dve.drain().then_inc(s["oatt"], 1)

            def weighted_low(h):
                rows = slice(64 * (h % 2), 64 * (h % 2) + 64)
                dve.wait_ge(s["oth"], h + 1)
                low(o_lo[rows, h // 2, :], tmp[2][rows, :], o_hi[rows, h // 2, :]).then_inc(s["otl"], 1)

            def turned_low(h, kt):
                dve.wait_ge(s["pTh"], KT * h + kt + 1)
                hi_, lo_ = (pTa_hi, pTa_lo) if kt < 4 else (pTb_hi, pTb_lo)
                b = (4, 6, 0)[kt % 3]
                low(lo_[:, kt % 4, :], bank(b), hi_[:, kt % 4, :]).then_inc(bank_free[b], 1)

            def values_low(p):
                for i, (b, t0, t1) in enumerate(((1, 0, 4), (2, 4, KT))):
                    dve.wait_ge(s["av"], 2 * p + i + 1)
                    low(v_lo[:, t0:t1, :, 0:VD], bank(b, (t1 - t0) * P).rearrange("p (k g v) -> p k g v", g=2, v=VD),
                        v_hi[:, t0:t1, :, 0:VD]).then_inc(bank_free[b], 1)

            queries_low(0)
            keys_low(0, 0)
            keys_low(0, 1)
            for h in range(HEADS):
                for t in range(TT):
                    i = TT * h + t
                    wait(dve, ends[("s", h, t)])
                    link(dve.tensor_reduce(mx[:, 2 * i:2 * i + 1], bank(4 + 2 * (t % 2), KEYS), AX.X, ALU.max))
                    after().tensor_scalar(mx[:, 2 * i + 1:2 * i + 2], mx[:, 2 * i:2 * i + 1], -SCALE, None, ALU.mult)\
                        .then_inc(s["max"], 1)
                    if t == 1 and h + 1 < HEADS:
                        queries_low(h + 1)
                        keys_low(h + 1, 0)
                    if t == 2 and h + 1 < HEADS:
                        keys_low(h + 1, 1)
                for t in range(TT):
                    wait(dve, taken[("s", h, t)])
                after().reciprocal(den[:, 1, h, :], den[:, 0, h, :]).then_inc(s["rc"], 1)
                if h:
                    weighted(h - 1)
                for kt in range(KT):
                    if kt == 3 and h:
                        weighted_low(h - 1)
                    turned_low(h, kt)
                if h % 2 == 0:
                    values_low(h // 2)
            weighted(HEADS - 1)
            weighted_low(HEADS - 1)

            def angles(q):
                kb = cst[:, C_K:C_K + NCH].unsqueeze(1).to_broadcast([P, 4, NCH])
                n = t5w[:, 0:8 * NCH]
                A, B = (x[:, :, :].rearrange("p a c -> p (a c)") for x in (ang_s, ang_c))
                if q:
                    dve.wait_ge(s["trig"], q)
                for d in range(2):
                    tb = th8[:, 16 * d + 4 * q:16 * d + 4 * q + 4].unsqueeze(2).to_broadcast([P, 4, NCH])
                    ins = tt(ang_s[:, 4 * d:4 * d + 4, :], tb, kb, ALU.mult)
                link(ins)
                reduce_angle(A, n)
                link(after().tensor_scalar(B, A, PI / 2, None, ALU.add))
                reduce_angle(B, n)
                dve.drain().then_inc(s["angle"], 1)

            def input_matrices(d):
                gl = slice(16 * d, 16 * d + 4)
                ds = slice(4 * d, 4 * d + 4)
                sl = slice(7, None, -1) if d == 0 else slice(0, 8)
                sh = [P, 4, 8, GC]
                pr = lpr[:, gl, sl].unsqueeze(3).to_broadcast(sh)
                pi = lpi[:, gl, sl].unsqueeze(3).to_broadcast(sh)
                br = bbr[:, gl, :].unsqueeze(2).to_broadcast(sh)
                bi = bbi[:, gl, :].unsqueeze(2).to_broadcast(sh)
                x0, x1 = (t[:, 0:512].rearrange("p (a e n) -> p a e n", a=4, e=8) for t in t5)
                link(tt(x0, pr, br, ALU.mult))
                link(tt(x1, pi, bi, ALU.mult))
                link(tt(pmr[:, ds, :].rearrange("p a m -> p (a m)"), t5[0][:, 0:512], t5[1][:, 0:512], ALU.subtract))
                link(tt(x0, pr, bi, ALU.mult))
                link(tt(x1, pi, br, ALU.mult))
                link(tt(pmi[:, ds, :].rearrange("p a m -> p (a m)"), t5[0][:, 0:512], t5[1][:, 0:512], ALU.add))
                dve.drain().then_inc(s["pm"], 1)

            def s5_setup(step):
                def R(i):
                    return row[:, i, :]

                e9 = cst[:, C_E9:C_E9 + 9].unsqueeze(1).to_broadcast([P, NPD, 9])

                def v9(i):
                    return lt[:, i, :].rearrange("p (a e) -> p a e", e=9)

                def b9(x):
                    return x.unsqueeze(2).to_broadcast([P, NPD, 9])

                if step == 0:
                    dve.wait_ge(ld["s5"], 16 * NS5)
                    dve.wait_ge(s["s5c"], 1)

                    dtb = dt2[:, :].unsqueeze(2).to_broadcast([NPD, 2, 64])
                    link(tt(R(8).rearrange("r (g p) -> r g p", g=2), R(0).rearrange("r (g p) -> r g p", g=2), dtb, ALU.mult))
                    link(tt(R(9).rearrange("r (g p) -> r g p", g=2), R(1).rearrange("r (g p) -> r g p", g=2), dtb, ALU.mult))
                    reduce_angle(R(9), R(4))
                    link(after().tensor_scalar(R(5), R(9), PI / 2, None, ALU.add))
                    reduce_angle(R(5), R(4))
                    dve.drain().then_inc(s["s5a"], 1)
                    link(tt(R(2), R(0), R(0), ALU.mult))
                    link(tt(R(3), R(1), R(1), ALU.mult))
                    link(tt(R(2), R(2), R(3), ALU.add))
                    link(after().reciprocal(R(3), R(2)))
                elif step == 1:
                    dve.wait_ge(s["s5c"], 2)
                    link(tt(R(5), R(6), R(5), ALU.mult))
                    link(after().tensor_scalar(R(5), R(5), 1.0, None, ALU.subtract))
                    link(tt(R(6), R(6), R(7), ALU.mult))
                    link(tt(R(2), R(5), R(0), ALU.mult))
                    link(tt(R(4), R(6), R(1), ALU.mult))
                    link(tt(R(2), R(2), R(4), ALU.add))
                    link(tt(R(10), R(2), R(3), ALU.mult))
                    link(tt(R(2), R(6), R(0), ALU.mult))
                    link(tt(R(4), R(5), R(1), ALU.mult))
                    link(tt(R(2), R(2), R(4), ALU.subtract))
                    link(tt(R(11), R(2), R(3), ALU.mult))
                    dve.drain().then_inc(s["s5row"], 1)
                elif step == 2:
                    wait(dve, ends["s5row"])
                    after().tensor_copy(base4[:, :, :].rearrange("p a n -> p (a n)"), bank(0, 4 * NPD)).then_inc(bank_free[0], 1)
                    wait(dve, taken["s5row"])
                    link(tt(v9(2), b9(base4[:, 0, :]), e9, ALU.mult))
                    link(tt(v9(0), b9(base4[:, 1, :]), e9, ALU.mult))
                    reduce_angle(lt[:, 0, :], lt[:, 3, :])
                    link(after().tensor_copy(th8[:, :], v9(0)[:, :, 8]))
                    link(after().tensor_scalar(lt[:, 1, :], lt[:, 0, :], PI / 2, None, ALU.add))
                    reduce_angle(lt[:, 1, :], lt[:, 3, :])
                    dve.drain().then_inc(s["s5a"], 1)
                elif step == 4:
                    dve.wait_ge(s["s5c"], 3)
                    tt(lpr[:, :, :], v9(2), v9(1), ALU.mult)
                    tt(lpi[:, :, :], v9(2), v9(0), ALU.mult)
                    link(after().tensor_copy(rho8[:, :], v9(2)[:, :, 8]))
                    w1_, w2_ = (lt[:, :, :].rearrange("p i c -> p (i c)")[:, i * T:i * T + T].rearrange("p (a n) -> p a n", n=GC)
                                for i in range(2))

                    def b16(x):
                        return x.unsqueeze(2).to_broadcast([P, NPD, GC])

                    cr_, ci_ = b16(base4[:, 2, :]), b16(base4[:, 3, :])
                    link(tt(w1_, cr_, bld[:, 0], ALU.mult))
                    link(tt(w2_, ci_, bld[:, 1], ALU.mult))
                    link(tt(bbr[:, :, :], w1_, w2_, ALU.subtract))
                    link(tt(w1_, cr_, bld[:, 1], ALU.mult))
                    link(tt(w2_, ci_, bld[:, 0], ALU.mult))
                    link(tt(bbi[:, :, :], w1_, w2_, ALU.add))
                    dve.drain().then_inc(s["s5r"], 1)
                elif step == 5:
                    input_matrices(0)
                elif step == 6:
                    input_matrices(1)

            def hyena_setup(step):
                if step == 1:
                    dve.wait_ge(ld["hyp"], 16 * NHYP)
                    after().tensor_copy(altr[:, :], cst[:, C_ALT:C_ALT + P]).then_inc(s["alt"], 1)
                    after().tensor_copy(alt_row[:, :], hrnd[0:1, :]).then_inc(s["alt"], 1)
                    dve.wait_ge(s["alt"], 2)
                elif step in (2, 5):
                    i = step // 3
                    wait(dve, ends[("hid", i)])
                    after().tensor_scalar(harg[:, :], bank(0)[0:64], vc3[:, i:i + 1], vc3[:, 2:3], ALU.add, ALU.mult)\
                        .then_inc(bank_free[0], 1)
                    wait(dve, taken[("hid", i)])
                    reduce_angle(harg[:, :], hrnd[:, :])
                    dve.drain().then_inc(s["hya"], 1)

            def merge(j, between=None):
                for m in range(KD):
                    split_to(begin["merge%d" % j] + 2 * m + 3)
                    b = 2 * (m % 4)
                    wait(dve, ends[("branch", j, m)])
                    wait(dve, taken[("gate", j, m)])
                    if j == 0:
                        tt(merged[:, m, :], bank(b + 1), tmp[m % 2][:, :], ALU.mult).then_inc(bank_free[b + 1], 1)
                    else:
                        tt(tmp[2][:, :], bank(b + 1), tmp[m % 2][:, :], ALU.mult).then_inc(bank_free[b + 1], 1)
                        wait(dve, taken[("branch", j, m)])
                        link(tt(merged[:, m, :], merged[:, m, :], tmp[2][:, :], ALU.add))
                    if between:
                        between(m)

            merge(0, s5_setup)
            phase_end(2)

            angles(0)
            for q in range(4):
                tsin, tcos = tsin2[q % 2], tcos2[q % 2]
                if q < 3:
                    angles(q + 1)
                wait(dve, ends[("K", q)])
                if q:
                    dve.wait_ge(ld["kfilt"], 16 * q)
                kf = bank(3, 128).rearrange("p (l n) -> p l n", n=GC)
                kb_ = bank(3, 128, 128).rearrange("p (l n) -> p l n", n=GC)
                dcol = VOFF["s5_d"] + q
                link(after().scalar_tensor_tensor(K2[:, 7, :], cst[:, C_EYE16:C_EYE16 + GC], vc1[:, dcol:dcol + 1],
                                              kf[:, 0, :], ALU.mult, ALU.add))
                link(tt(K2[:, 7, :], kb_[:, 7, :], K2[:, 7, :], ALU.add))
                after().tensor_copy(K2[:, 0:7, :], kb_[:, 0:7, :])
                after().tensor_copy(K2[:, 8:15, :], kf[:, 1:8, :]).then_inc(bank_free[3], 1)
                for d in range(2):
                    ds = slice(4 * d, 4 * d + 4)
                    wait(dve, ends[("S", q, 1, d)])
                    dve.wait_ge(s["trig"], q + 1)
                    sr, si = (bank(4 + 2 * p_ + d, 4 * NCH).rearrange("p (a c) -> p a c", a=4) for p_ in range(2))
                    if d:
                        sr, si = sr[:, :, ::-1], si[:, :, ::-1]
                    x0, x1 = (t[:, 0:4 * NCH].rearrange("p (a c) -> p a c", a=4) for t in t5)
                    tc_, ts_ = tcos[:, ds, :], tsin[:, ds, :]
                    tt(x0, sr, tc_, ALU.mult)
                    link(dve.tensor_tensor(x1, si, ts_, ALU.mult))
                    link(tt(gr[:, ds, :], x0, x1, ALU.add))
                    tt(x0, si, tc_, ALU.mult).then_inc(bank_free[6 + d], 1)
                    tt(x1, sr, ts_, ALU.mult).then_inc(bank_free[4 + d], 1)
                    wait(dve, taken[("S", q, 0, d)])
                    wait(dve, taken[("S", q, 1, d)])
                    link(tt(gi[:, ds, :], x0, x1, ALU.subtract))
                wait(dve, ends[("S", q, 1, 1)])
                for d in range(2):
                    gl0 = 16 * d + 4 * q
                    ds = slice(4 * d, 4 * d + 4)
                    for j in range(4):
                        rb = rho8[:, gl0 + j:gl0 + j + 1].to_broadcast([P, NCH])
                        for dst, src in ((sgr, gr), (sgi, gi)):
                            ins = dve.tensor_tensor_scan(dst[:, 4 * d + j, :], rb, src[:, 4 * d + j, :], 0.0,
                                                         ALU.mult, ALU.add)
                    link(ins)
                    w = slice(NCC - 1, NCH - 1)
                    x0, x1 = (t[:, 0:4 * NCX].rearrange("p (a c) -> p a c", a=4) for t in t5)
                    if q and d == 0:
                        wait(dve, ends[("Y", q - 1, 1)])
                    tc_, ts_ = tcos[:, ds, w], tsin[:, ds, w]
                    a_, b_ = sgr[:, ds, w], sgi[:, ds, w]
                    hr, hi_ = H[:, 0, ds, :], H[:, 1, ds, :]
                    if d:
                        hr, hi_ = hr[:, :, ::-1], hi_[:, :, ::-1]
                    tt(x0, a_, tc_, ALU.mult)
                    link(dve.tensor_tensor(x1, b_, ts_, ALU.mult))
                    link(tt(hr, x0, x1, ALU.subtract))
                    tt(x0, a_, ts_, ALU.mult)
                    link(dve.tensor_tensor(x1, b_, tc_, ALU.mult))
                    tt(hi_, x0, x1, ALU.add).then_inc(s["Hs"], 1)
            wait(dve, ends["ada1"])
            pv = bank(0, 64, 32).rearrange("p (m x) -> p m x", x=2)
            tt(modx[:, 16:48], pv[:, :, 0], ab[:, 16:48], ALU.add).then_inc(bank_free[0], 1)
            wait(dve, taken["ada1"])
            nf = vc1[:, VOFF["norm_ffn"]:VOFF["norm_ffn"] + KD]
            link(after().scalar_tensor_tensor(affn[:, :], modx[:, 32:40], 1.0, nf, ALU.add, ALU.mult))
            for k in range(4):
                dve.wait_ge(s["gth"], k + 1)
                low(yg_lo[:, k, :], yg[:, k, :], yg_hi[:, k, :]).then_inc(s["gtl"], 1)
            split_to(begin["merge1"] - 1)
            for m in range(4):
                wait(dve, taken[("glu", m)])
                tt(yg[:, m, :], yg[:, m, :], tmp[m % 2][:, :], ALU.mult).then_inc(s["oun"], 1)
                dve.wait_ge(s["oth"], HEADS + m + 1)
                low(o_lo[:, m, :], yg[:, m, :], o_hi[:, m, :]).then_inc(s["otl"], 1)
            merge(1, hyena_setup)

            def taps_out(it, t):
                n = TT * it + t
                p = tmp[t % 2]
                wait(dve, ends[("f", it, t)])
                w, which, before = window(n)
                dve.wait_ge(ld[which], 16 * (before + 1))
                tt(tmp[2][:, :], bank(5), w[:, :, :].rearrange("p a c -> p (a c)"), ALU.mult)\
                    .then_inc(bank_free[5], 1)
                wait(dve, taken[("f", it, t)])
                tt(p[:, HC:T], tmp[2][:, 0:HC], tmp[2][:, HC:T], ALU.subtract)
                ins = tt(p[:, 0:HC], tmp[2][:, 0:HC], tmp[2][:, HC:T], ALU.add)
                if t == 0:
                    dve.wait_ge(ld["hyb"], 16 * (it + 1))
                    link(ins)
                    ins = tt(p[0:1, 0:HC], p[0:1, 0:HC], hyb[:, :], ALU.add)
                ins.then_inc(s["hs"], 1)

            def taps_low(it, t):
                dve.wait_ge(s["hsh"], TT * it + t + 1)
                low(ybuf[it][1][:, t, :], tmp[t % 2][:, :], ybuf[it][0][:, t, :]).then_inc(s["hsl"], 1)

            for n in range(12):
                split_to(min(begin["hyena"] + n + 2 + (4 if n >= 6 else 0), begin["merge2"] - 1))
                z = bank(n % 4)
                dve.wait_ge(s["zc"], n + 1)
                o = tmp[n % 2][:, :] if n < 8 else g2c[n % 4 // 2][:, n % 2, :]
                link(after().scalar_tensor_tensor(o[:, 1:T], z[:, 0:T - 1], vc2[:, n:n + 1], o[:, 1:T],
                                                  ALU.mult, ALU.add))
                after().scalar_tensor_tensor(o[:, 0:T - 1], z[:, 1:T], vc2[:, 24 + n:25 + n], o[:, 0:T - 1],
                                             ALU.mult, ALU.add).then_inc(bank_free[n % 4], 1)
                if 1 <= n <= 4:
                    v = n - 1
                    cs = slice(v % 2 * P, (v % 2 + 1) * P)
                    dve.wait_ge(s["zt"], n)
                    low(u_lo[v // 2][:, :, cs], bank(6 + v % 2).rearrange("p (t c) -> p t c", t=TT),
                        u_hi[v // 2][:, :, cs]).then_inc(bank_free[6 + v % 2], 1)
                if n >= 8:
                    taps_low(0, n - 8)
                if 7 <= n < 11:
                    if n < 9:
                        wait(dve, ends[("ht", n - 1)])
                    taps_out(0, n - 7)
            split_to(begin["merge2"] - 1)
            for it, (half, o) in enumerate(CONVS):
                y_hi, y_lo = ybuf[it]
                if it < 3:
                    for t in range(TT):
                        taps_out(it + 1, t)
                        if t:
                            taps_low(it + 1, t - 1)
                    taps_low(it + 1, 3)

                def product_low(j):
                    dve.wait_ge(s["yth"], 4 * it + j + 1)
                    low(y_lo[:, j, :], tmp[j % 2][:, :], y_hi[:, j, :]).then_inc(s["ytl"], 1)

                for j in range(4):
                    b, p = (2, 3, 6, 7)[j], tmp[j % 2]
                    wait(dve, ends[("Us", it, j)])
                    wait(dve, taken[("G", it, j)])
                    if j >= 2:
                        dve.wait_ge(s["ytl"], 4 * it + j - 1)
                    g = Gs[:, j, :].rearrange("p (r c) -> p r c", r=2)
                    uu = bank(b).rearrange("p (r c) -> p r c", r=2)
                    tt(p[:, :], bank(b), Gs[:, j, :], ALU.mult)
                    tt(tmp[2][:, :].rearrange("p (r c) -> p r c", r=2), uu, g[:, ::-1, :], ALU.mult)\
                        .then_inc(bank_free[b], 1)
                    wait(dve, taken[("Us", it, j)])
                    tt(p[:, 0:HC], p[:, 0:HC], p[:, HC:T], ALU.subtract)
                    tt(p[:, HC:T], tmp[2][:, 0:HC], tmp[2][:, HC:T], ALU.add).then_inc(s["yt"], 1)
                wait(dve, ends[("Un", it)])
                link(after().tensor_scalar(nyg[:, :], bank(4, HC)[0:1], 1.0 / 1024, None, ALU.mult))
                tt(nyg[:, :], bank(4, HC, HC)[0:1], nyg[:, :], ALU.mult).then_inc(bank_free[4], 1)
                wait(dve, taken[("Ny", it)])
                if it:
                    wait(dve, ends[("c", it - 1, TT - 1 if it < 3 else 1)])
                link(after().tensor_copy(nyh[:, :], nyg[:, :]))
                low(nyl[:, :], nyg[:, :], nyh[:, :]).then_inc(s["nyq"], 1)
                product_low(3)
                dve.wait_ge(s["ytl"], 4 * (it + 1))
                if o == 0:
                    def signal_low(t):
                        dve.wait_ge(s["uth"], TT * half + t + 1)
                        low(u_lo[half][:, t, :], tmp[t % 2][:, 0:HC], u_hi[half][:, t, :]).then_inc(s["utl"], 1)

                    for t in range(TT):
                        b = 6 + t % 2
                        wait(dve, ends[("c", it, t)])
                        tt(tmp[t % 2][:, 0:HC], bank(b, HC), g1t[half][:, t, :], ALU.mult).then_inc(bank_free[b], 1)
                        wait(dve, taken[("c", it, t)])
                        dve.drain().then_inc(s["ut"], 1)
                        if t:
                            signal_low(t - 1)
                    signal_low(3)
                else:
                    for i in range(2):
                        wait(dve, ends[("c", it, i)])
                        tt(tmp[i][:, :], bank(6 + i), g2c[half][:, i, :], ALU.mult).then_inc(bank_free[6 + i], 1)
                        wait(dve, taken[("c", it, i)])
                        dve.drain().then_inc(s["oun"], 1)
                        dve.wait_ge(s["oth"], HEADS + 4 + 2 * half + i + 1)
                        low(e_lo[:, 2 * half + i, :], tmp[i][:, :], e_hi[:, 2 * half + i, :])\
                            .then_inc(s["otl"], 1)
            def merged_low(m):
                dve.wait_ge(s["mh"], m + 1)
                low(m_lo[:, m, :], merged[:, m, :], m_hi[:, m, :]).then_inc(s["ml"], 1)

            def merged_out(m):
                dve.drain().then_inc(s["mg"], 1)
                if m:
                    merged_low(m - 1)

            merge(2, merged_out)
            merged_low(KD - 1)

            link(after().memset(onesq[:, :], 1.0))
            for m in range(KD):
                split_to(begin["w_out"] + m + 2)
                wait(dve, ends[("wo", m)])
                wait(dve, taken[("x2T", m)])
                after().scalar_tensor_tensor(xT[:, m, :], bank(m % 4), modx[:, 16 + m:17 + m], xT[:, m, :],
                                         ALU.mult, ALU.add).then_inc(bank_free[m % 4], 1)
            wait(dve, ends["ss"])
            after().tensor_scalar(vrow[:, :], bank(4), 1.0 / D, EPS, ALU.mult, ALU.add).then_inc(bank_free[4], 1)
            wait(dve, taken["ss"])
            dve.drain().then_inc(s["vf"], 1)
            dve.wait_ge(s["sf"], 1)
            refine(vrow[:, :], srow[:, :], sqk[0][:, :], sqk[1][:, :], srow[:, :])

            def low_h2(k):
                dve.wait_ge(s["h2h"], k + 1)
                low(h_lo[:, k, :], tmp[k % 2][:, :], h_hi[:, k, :]).then_inc(s["h2l"], 1)

            for k in range(KD):
                link(tt(tmp[k % 2][:, :], xT[:, k, :], srow[:, :], ALU.mult))
                after().tensor_scalar(tmp[k % 2][:, :], tmp[k % 2][:, :], affn[:, k:k + 1], modx[:, 24 + k:25 + k],
                                  ALU.mult, ALU.add).then_inc(s["h2t"], 1)
                if k:
                    low_h2(k - 1)
            low_h2(KD - 1)

            for f in range(FT):
                split_to(begin["up"] + 2 * f + 3)
                wait(dve, ends[("gu", f, 1)])
                wait(dve, taken[("gu", f, 0)])
                b = (2 * f + 1) % 8
                tt(tmp[f % 3][:, :], bank(b), tmp[f % 3][:, :], ALU.mult).then_inc(bank_free[b], 1)
                dve.wait_ge(s["ath"], f + 1)
                low(act_lo[:, f, :], tmp[f % 3][:, :], act_hi[:, f, :]).then_inc(s["atl"], 1)

            def weighted_out(m):
                wait(dve, taken[("yo", m)])
                if m == 0:
                    dve.wait_ge(ld["fnorm"], 16)
                cs = slice(m * P, (m + 1) * P)
                tt(ytok[:, :, cs], ytok[:, :, cs], fnorm[:, cs].unsqueeze(1).to_broadcast([P, TT, P]), ALU.mult)

            for m in range(KD):
                split_to(begin["down"] + 4 * m + 6)
                wait(dve, ends[("down", m)])
                after().scalar_tensor_tensor(xT[:, m, :], bank(m % 4), modx[:, 40 + m:41 + m], xT[:, m, :],
                                         ALU.mult, ALU.add).then_inc(bank_free[m % 4], 1)
                if m >= 2:
                    weighted_out(m - 2)
            weighted_out(KD - 2)
            wait(dve, taken[("yo", KD - 1)])
            link(after().tensor_reduce(rs[:, 2, 0, 0:TT], fsum[:, :, :], AX.X, ALU.add))
            link(after().tensor_scalar(rs[:, 2, 1, 0:TT], rs[:, 2, 0, 0:TT], 1.0 / D, EPS, ALU.mult, ALU.add))
            dve.drain().then_inc(s["var"], 1)
            weighted_out(KD - 1)
            dve.wait_ge(s["sqrt"], 3)
            refine(rs[:, 2, 1, 0:TT], rs[:, 2, 2, 0:TT], rs[:, 2, 3, 0:TT], rs[:, 2, 4, 0:TT], rs[:, 2, 5, 0:TT])
            dve.drain().then_inc(s["fr"], 1)
            for t in (0, 1):
                after().tensor_scalar(ytok[:, t, :], ytok[:, t, :], rs[:, 2, 5, t:t + 1], None, ALU.mult)\
                    .then_inc(s["fin"], 1)

        @block.gpsimd
        def _(pool):
            def product(o, x, y, op=ALU.mult):
                pool.drain()
                return pool.tensor_tensor(o, x, y, op)

            def both(q, d, span):
                return slice(16 * d + 4 * q, 16 * d + 4 * q + 4), slice(4 * d, 4 * d + 4), [P, 4, span, GC]

            def output_matrices(q):
                clr, cli = clr2[q % 2], cli2[q % 2]
                for d in range(2):
                    gl, ds, sh = both(q, d, 9)
                    sl = slice(0, 9) if d == 0 else slice(None, None, -1)
                    pr = lpr[:, gl, sl].unsqueeze(3).to_broadcast(sh)
                    pi = lpi[:, gl, sl].unsqueeze(3).to_broadcast(sh)
                    cr = ctr[:, gl, :].unsqueeze(2).to_broadcast(sh)
                    ci = cti[:, gl, :].unsqueeze(2).to_broadcast(sh)
                    x0, x1 = (t[:, :, :, :] for t in t5g)
                    product(x0, pr, cr)
                    product(x1, pi, ci)
                    product(clr[:, ds], x0, x1, ALU.add)
                    product(x0, pr, ci)
                    product(x1, pi, cr)
                    product(cli[:, ds], x0, x1, ALU.subtract)
                pool.drain().then_inc(s["cl"], 1)

            def side_by_side(q):
                for d in range(2):
                    gl, ds, _ = both(q, d, 8)
                    for dst, src in ((bdr, bbr), (bdi, bbi)):
                        pool.drain()
                        pool.tensor_copy(dst[0:64, ds, 0:GC], src[0:64, gl, :])
                        pool.tensor_copy(dst[64:P, ds, GC:2 * GC], src[64:P, gl, :])

            def input_matrices(q):
                for d in range(2):
                    gl, ds, sh = both(q, d, 8)
                    sl = slice(7, None, -1) if d == 0 else slice(0, 8)
                    pr = lpr[:, gl, sl].unsqueeze(3).to_broadcast(sh)
                    pi = lpi[:, gl, sl].unsqueeze(3).to_broadcast(sh)
                    br = bbr[:, gl, :].unsqueeze(2).to_broadcast(sh)
                    bi = bbi[:, gl, :].unsqueeze(2).to_broadcast(sh)
                    x0, x1 = (t[:, :, 0:8, :] for t in t5g)
                    o_r, o_i = (x[:, ds, :].rearrange("p a (e n) -> p a e n", e=8) for x in (pmr, pmi))
                    product(x0, pr, br)
                    product(x1, pi, bi)
                    product(o_r, x0, x1, ALU.subtract)
                    product(x0, pr, bi)
                    product(x1, pi, br)
                    product(o_i, x0, x1, ALU.add)
                pool.drain().then_inc(s["pm"], 2)

            for h in range(HEADS):
                pool.wait_ge(s["rc"], h + 1)
                if h:
                    wait(pool, ends[("rc", h - 1)])
                product(tmp[0][:, :].rearrange("p (t c) -> p t c", t=TT), ident.unsqueeze(1).to_broadcast([P, TT, P]),
                        den[:, 1, h, :].unsqueeze(2).to_broadcast([P, TT, P])).then_inc(s["diag"], 1)
            pool.wait_ge(s["s5r"], 1)
            pool.memset(bdr[:, :, :], 0.0)
            pool.memset(bdi[:, :, :], 0.0)
            side_by_side(0)
            output_matrices(0)
            pool.wait_ge(s_phase, 6)
            for q in range(1, 4):
                wait(pool, ends[("K", q - 1)])
                side_by_side(q)
                for part in range(2):
                    for d in range(2):
                        wait(pool, ends[("WT", q - 1, part, d)])
                input_matrices(q)
                if q >= 2:
                    wait(pool, ends[("Y", q - 2, 1)])
                output_matrices(q)
            for it in range(4):
                for j in range(3):
                    pool.wait_ge(s["yth"], 4 * it + j + 1)
                    product(ybuf[it][1][:, j, :], tmp[j % 2][:, :], ybuf[it][0][:, j, :].bitcast(F32), ALU.subtract)\
                        .then_inc(s["ytl"], 1)

        @block.sync
        def _(sp):
            at = [0]

            def load(o, i, which, n=16):
                sp.dma_start(o, i).then_inc(ld[which], 16)

            def ring_to(c1):
                while at[0] <= min(c1, len(chunks) - 1):
                    c = at[0]
                    at[0] += 1
                    src, kt, n, kind, dest = chunks[c]
                    i = c % RING
                    if c >= RING:
                        p = c - RING
                        if chunks[p][3] == "plain":
                            wait(sp, ends[("chunk", p)])
                        else:
                            sp.wait_ge(s_lo, nth_split[p] + 1)
                    sp.dma_start(raw[i][:, 0:kt * n].rearrange("p (k n) -> p k n", k=kt), src).then_inc(raw_in[i], 16)

            ring_to(begin["uq"] - 1)
            for t in range(KT):
                wait(sp, taken[("us", t)])
                load(uch[16 * t:16 * t + 16, :, :], us[:, t, :], "uch")
            wait(sp, ends[("us", KT - 1)])
            sp.wait_ge(s["htl"], 2 * KD)
            load(rope[:, :, :, :], a["rope"].rearrange("(t p) x f -> p t x f", p=P), "rope")
            ring_to(begin["merge0"] + 2)
            sp.wait_ge(s["otl"], HEADS)
            load(row[:, 0, :], a["s5_lam_re"], "s5")
            load(row[:, 1, :], a["s5_lam_im"], "s5")
            load(dt2[:, :], a["s5_log_dt"], "s5")
            for part, name in enumerate(("s5_b_re", "s5_b_im")):
                load(bld[:, part], a[name], "s5")
            for part, name in enumerate(("s5_c_re", "s5_c_im")):
                load(cld[:, part], a[name], "s5")
            ring_to(begin["merge1"] + 3)
            sp.wait_ge(s["otl"], HEADS + 4)
            load(w12[0:33, 0, :], a["hy_f_w1"], "hyp")
            load(w12[:, 1, :], a["hy_f_w2"], "hyp")
            load(zpos[:, :], a["zpos"], "hyp")
            load(hrnd[0:1, :], a["alt_row"], "hyp")
            ring_to(begin["hyena"] + 3)
            for it, (half, o) in enumerate(CONVS):
                hs = slice(half * HC, (half + 1) * HC)
                if it:
                    wait(sp, ends[("f", it - 1, TT - 1)])
                    sp.wait_ge(s["hs"], TT * (it - 1) + 1)
                load(w3[:, :, :], a["hy_f_w3"].rearrange("h (o d c) -> h o d c", o=2, d=2)[:, o, :, hs], "w3")
                load(hyb[:, :], a["hy_bias"][o:o + 1, hs], "hyb")
                for t in range(TT):
                    n = TT * it + t
                    if n == 5:
                        wait(sp, ends[("hz", 11)])
                    elif n == 9:
                        wait(sp, ends[("c", 0, TT - 1)])
                    elif n:
                        sp.wait_ge(s["hs"], n if n < 5 else n - 1)
                    w, which, _ = window(n)
                    load(w[:, :, :], a["window"][t * P:(t + 1) * P].rearrange("p (o d c) -> p o d c", o=2, d=2)
                         [:, o, :, hs], which)
                    if n == 0:
                        ring_to(begin["merge2"] - 1)
                if it == 0:
                    ring_to(begin["merge2"] + 3)
            wait(sp, taken[("c", 3, 1)])
            load(x2t[:, :, :], a["x"].rearrange("(t p) d -> p t d", p=P), "x2")
            ring_to(begin["down"] + 3)
            wait(sp, ends[("gu", FT - 1, 1)])
            load(fnorm[:, :], a["final_norm"].rearrange("(r n) -> r n", r=1).to_broadcast([P, D]), "fnorm")
            ring_to(len(chunks) - 1)
            for t in (0, 2, 1, 3):
                sp.wait_ge(s["fin_a" if t >= 2 else "fin"], t % 2 + 1)
                load(out[t * P:(t + 1) * P, :], ytok[:, t, :], "out")
            sp.wait_ge(ld["out"], 16 * TT)


def _constants():
    import math

    import numpy as np
    c = np.zeros((P, C_N), np.float64)
    c[:, C_ID:C_ID + P] = np.eye(P)
    c[:, C_EYE16:C_EYE16 + GC] = np.tile(np.eye(GC), (P // GC, 1))
    c[:, C_GS:C_GS + 4] = 2.0 / 1024
    c[0, C_GS] = 1.0 / 1024
    c[:, C_ALT:C_ALT + P] = np.where(np.arange(P) % 2, -1.0, 1.0)[:, None]
    c[:, C_E9:C_E9 + 9] = np.arange(9)
    c[:, C_K:C_K + NCH] = np.arange(1, NCH + 1)
    n = np.arange(T)
    ang = 2 * np.pi * (np.outer(n, n) % 1024) / 1024
    t = np.linspace(0.0, 1.0, T)[:, None]
    w = 2 * np.pi * n[:, None] / T
    bands = np.linspace(1e-4, 15, 16)[None, :]
    zpos = np.concatenate([t, np.cos(bands * w), -np.sin(bands * w)], axis=-1).T
    deltas = np.abs(np.linspace(math.log(1e-2) / 0.3, math.log(1e-2) / 1.5, 4 * W5))
    window = np.exp(-t * deltas) + 0.05
    inv = 10000.0 ** (-np.arange(8) / 8)
    ang2 = np.concatenate([(n // 64)[:, None] * inv, (n % 64)[:, None] * inv], axis=-1)
    rope = np.stack([np.cos(ang2), np.sin(ang2)], axis=1)
    alt = np.where(n % 2, -1.0, 1.0)[None, :]
    got = {"cst": c, "dft_cos": np.cos(ang), "dft_sin": -np.sin(ang), "zpos": zpos, "window": window,
           "rope": rope, "alt_row": alt}
    return {k: np.ascontiguousarray(v.astype(np.float32)) for k, v in got.items()}


def make(nc, arrays, dt_of):
    a = {}
    for name, v in arrays.items():
        ap = nc.dram_tensor("in_" + name, v.shape, dt_of(v.dtype), kind="ExternalInput").ap()
        a[name] = ap
    for name in list(a):
        if name in ("x", "ctx", "c"):
            a[name] = a[name][0]
        elif len(a[name].shape) > 1 and name not in ("cst", "dft_cos", "dft_sin", "zpos", "window", "rope", "alt_row"):
            a[name] = a[name][0]
    for name in ("s5_lam_re", "s5_lam_im"):
        a[name] = a[name].rearrange("d (a g) p -> (d a) (g p)", g=2)
    a["s5_log_dt"] = a["s5_log_dt"].rearrange("d (a g) -> (d a) g", g=2)
    for name in ("s5_b_re", "s5_b_im"):
        a[name] = a[name].rearrange("d (a g) p n -> (g p) (d a) n", g=2)
    for name in ("s5_c_re", "s5_c_im"):
        a[name] = a[name].rearrange("d (b r) n p -> (r n) (d b) p", r=8)
    scratch = nc.dram_tensor("lag_kernels", (4, P, 15 * GC), F32, kind="Internal").ap()
    out = nc.dram_tensor("out_x", (1, T, D), F32, kind="ExternalOutput").ap()
    build(nc, a, scratch, out[0])


def kernel(**inputs):
    import numpy as np
    from concourse import bacc
    from concourse.bass_utils import run_bass_kernel_spmd

    nc = bacc.Bacc("TRN2", target_bir_lowering=False, num_devices=1)
    arrays = {k: np.ascontiguousarray(v) for k, v in inputs.items()}
    arrays.update(_constants())
    make(nc, arrays, mybir.dt.from_np)
    r = run_bass_kernel_spmd(nc, [{"in_" + k: v for k, v in arrays.items()}], core_ids=[0])
    return r.results[0]["out_x"]
```
